# Optimizing a Trainium2 kernel written in Bass

```python
import jax, jax.numpy as jnp
from jax import lax
import numpy as np

D_MODEL = 2048
BATCH = 1
SEQ = 256
DEPTH = 1

GDN_HEADS = 8
GDN_HEAD_DIM = 128
GDN_WIDTH = GDN_HEADS * GDN_HEAD_DIM
CONV_WIDTH = 4
GDN_CHUNK = 64
MOBA_HEADS = 8
MOBA_HEAD_DIM = 128
MOBA_WIDTH = MOBA_HEADS * MOBA_HEAD_DIM
MOBA_BLOCK = 256
MOBA_TOPK = 3
MOBA_QCHUNK = 128

NORM_EPS = 1e-6
NEG_INF = -1e30
SPLITS = (3 * GDN_WIDTH, GDN_WIDTH, GDN_HEADS, GDN_HEADS, 3 * MOBA_WIDTH, MOBA_WIDTH, D_MODEL, D_MODEL)
IN_WIDTH = 3 * GDN_WIDTH + GDN_WIDTH + 2 * GDN_HEADS + 3 * MOBA_WIDTH + MOBA_WIDTH + 2 * D_MODEL


def rms_norm(x, w):
    xf = x.astype(jnp.float32)
    y = xf * lax.rsqrt(jnp.mean(xf * xf, axis=-1, keepdims=True) + NORM_EPS)
    return (y * w.astype(jnp.float32)).astype(x.dtype)

def l2_normalize(x):
    return x * lax.rsqrt(jnp.sum(x * x, axis=-1, keepdims=True) + NORM_EPS)

def causal_depthwise_conv(x, w):
    K = w.shape[0]
    S = x.shape[1]
    xp = jnp.pad(x, ((0, 0), (K - 1, 0), (0, 0)))
    out = w[0] * xp[:, 0:S]
    for j in range(1, K):
        out = out + w[j] * xp[:, j:j + S]
    return out

def gated_delta_rule(q, k, v, beta, g):
    B, H, S, dk = q.shape
    dv = v.shape[-1]
    C = GDN_CHUNK
    N = S // C
    q = q * (dk ** -0.5)
    q = q.reshape(B, H, N, C, dk)
    k = k.reshape(B, H, N, C, dk)
    v = v.reshape(B, H, N, C, dv)
    beta = beta.reshape(B, H, N, C)
    g = jnp.cumsum(g.reshape(B, H, N, C), axis=-1)
    kb = k * beta[..., None]
    vb = v * beta[..., None]
    incl = jnp.tril(jnp.ones((C, C), dtype=bool))
    strict = jnp.tril(jnp.ones((C, C), dtype=bool), -1)
    decay = jnp.exp(jnp.where(incl, g[..., :, None] - g[..., None, :], NEG_INF))
    L = jnp.where(strict, jnp.einsum('bhnid,bhnjd->bhnij', kb, k) * decay, 0.0)
    eye = jnp.eye(C, dtype=jnp.float32)
    T = lax.linalg.triangular_solve(L + eye, jnp.broadcast_to(eye, L.shape), left_side=True, lower=True)
    u = jnp.einsum('bhnij,bhnje->bhnie', T, vb)
    w = jnp.einsum('bhnij,bhnjd->bhnid', T, kb * jnp.exp(g)[..., None])
    intra = jnp.where(incl, jnp.einsum('bhnid,bhnjd->bhnij', q, k) * decay, 0.0)
    qg = q * jnp.exp(g)[..., None]
    kdec = k * jnp.exp(g[..., -1:] - g)[..., None]
    g_last = jnp.exp(g[..., -1])
    xs = (jnp.moveaxis(qg, 2, 0), jnp.moveaxis(kdec, 2, 0), jnp.moveaxis(u, 2, 0),
          jnp.moveaxis(w, 2, 0), jnp.moveaxis(intra, 2, 0), jnp.moveaxis(g_last, 2, 0))

    def step(state, inp):
        qg_i, kd_i, u_i, w_i, a_i, gl_i = inp
        v_new = u_i - jnp.einsum('bhcd,bhde->bhce', w_i, state)
        o = jnp.einsum('bhcd,bhde->bhce', qg_i, state) + jnp.einsum('bhij,bhje->bhie', a_i, v_new)
        state = state * gl_i[..., None, None] + jnp.einsum('bhcd,bhce->bhde', kd_i, v_new)
        return state, o

    state0 = jnp.zeros((B, H, dk, dv), jnp.float32)
    _, o = lax.scan(step, state0, xs)
    return jnp.moveaxis(o, 0, 2).reshape(B, H, S, dv)

def moba_attention(q, k, v):
    B, S, H, d = q.shape
    NB = -(-S // MOBA_BLOCK)
    S_pad = NB * MOBA_BLOCK
    QC = MOBA_QCHUNK
    NQ = S // QC
    k_sel = min(MOBA_TOPK, NB)
    pad = ((0, 0), (0, S_pad - S), (0, 0), (0, 0))
    kp = jnp.pad(k, pad).reshape(B, NB, MOBA_BLOCK, H, d).transpose(0, 3, 1, 2, 4)
    vp = jnp.pad(v, pad).reshape(B, NB, MOBA_BLOCK, H, d).transpose(0, 3, 1, 2, 4)
    kmean = jnp.mean(kp.astype(jnp.float32), axis=3)
    qh = q.transpose(0, 2, 1, 3)
    gate = jnp.einsum('bhsd,bhnd->bhsn', qh.astype(jnp.float32), kmean)
    q_blk = jnp.arange(S) // MOBA_BLOCK
    fully_past = jnp.arange(NB)[None, :] < q_blk[:, None]
    gate = jnp.where(fully_past, gate, NEG_INF)
    _, idx = lax.top_k(gate, k_sel)

    q_steps = qh.reshape(B, H, NQ, QC, d).transpose(0, 2, 1, 3, 4).reshape(B * NQ, H, QC, d)
    idx_steps = idx.reshape(B, H, NQ, QC, k_sel).transpose(0, 2, 1, 3, 4).reshape(B * NQ, H, QC, k_sel)
    b_ids = jnp.repeat(jnp.arange(B, dtype=jnp.int32), NQ)
    c_ids = jnp.tile(jnp.arange(NQ, dtype=jnp.int32), B)
    scale = MOBA_HEAD_DIM ** -0.5
    hh = jnp.arange(H)[:, None, None]

    def step(args):
        qc, ic, b, c = args
        kb = kp[b]
        vb = vp[b]
        kg = kb[hh, ic]
        vg = vb[hh, ic]
        own = (c * QC) // MOBA_BLOCK
        ko = lax.dynamic_index_in_dim(kb, own, axis=1, keepdims=False)
        vo = lax.dynamic_index_in_dim(vb, own, axis=1, keepdims=False)
        s_past = jnp.einsum('hqd,hqjpd->hqjp', qc, kg, preferred_element_type=jnp.float32)
        s_past = s_past.reshape(H, QC, k_sel * MOBA_BLOCK)
        s_own = jnp.einsum('hqd,hpd->hqp', qc, ko, preferred_element_type=jnp.float32)
        t_abs = c * QC + jnp.arange(QC)
        slot_ok = jnp.arange(k_sel)[None, :] < (t_abs // MOBA_BLOCK)[:, None]
        slot_ok = jnp.broadcast_to(slot_ok[:, :, None], (QC, k_sel, MOBA_BLOCK)).reshape(QC, k_sel * MOBA_BLOCK)
        own_ok = (own * MOBA_BLOCK + jnp.arange(MOBA_BLOCK))[None, :] <= t_abs[:, None]
        mask = jnp.concatenate([slot_ok, own_ok], axis=-1)[None]
        s = jnp.concatenate([s_past, s_own], axis=-1) * scale
        p = jax.nn.softmax(jnp.where(mask, s, NEG_INF), axis=-1).astype(vg.dtype)
        p_past = p[..., :k_sel * MOBA_BLOCK].reshape(H, QC, k_sel, MOBA_BLOCK)
        p_own = p[..., k_sel * MOBA_BLOCK:]
        return (jnp.einsum('hqjp,hqjpd->hqd', p_past, vg)
                + jnp.einsum('hqp,hpd->hqd', p_own, vo))

    o = lax.map(step, (q_steps, idx_steps, b_ids, c_ids))
    return o.reshape(B, NQ, H, QC, d).transpose(0, 1, 3, 2, 4).reshape(B, S, H * d)

def hybrid_mixer(h, w_in, conv_w, a_log, dt_bias, gdn_norm_w, w_branch_a, w_branch_b, w_out):
    B, S, _ = h.shape
    proj = h @ w_in
    offsets = []
    acc = 0
    for n in SPLITS[:-1]:
        acc += n
        offsets.append(acc)
    gdn_qkv, gdn_z, gdn_b, gdn_a, moba_qkv, moba_z, gate_a, gate_b = jnp.split(proj, offsets, axis=-1)

    qkv = jax.nn.silu(causal_depthwise_conv(gdn_qkv, conv_w)).astype(jnp.float32)
    qa, ka, va = jnp.split(qkv, 3, axis=-1)
    to_heads = lambda t: t.reshape(B, S, GDN_HEADS, GDN_HEAD_DIM).transpose(0, 2, 1, 3)
    qa, ka, va = l2_normalize(to_heads(qa)), l2_normalize(to_heads(ka)), to_heads(va)
    beta = jax.nn.sigmoid(gdn_b.astype(jnp.float32)).transpose(0, 2, 1)
    g = (-jnp.exp(a_log.astype(jnp.float32))
         * jax.nn.softplus(gdn_a.astype(jnp.float32) + dt_bias.astype(jnp.float32))).transpose(0, 2, 1)
    oa = gated_delta_rule(qa, ka, va, beta, g).transpose(0, 2, 1, 3)
    oa = oa * lax.rsqrt(jnp.mean(oa * oa, axis=-1, keepdims=True) + NORM_EPS)
    za = gdn_z.astype(jnp.float32).reshape(B, S, GDN_HEADS, GDN_HEAD_DIM)
    oa = (oa * gdn_norm_w.astype(jnp.float32) * jax.nn.silu(za)).reshape(B, S, GDN_WIDTH).astype(h.dtype)
    u_a = oa @ w_branch_a

    qb, kb, vb = jnp.split(moba_qkv, 3, axis=-1)
    to_mh = lambda t: t.reshape(B, S, MOBA_HEADS, MOBA_HEAD_DIM)
    ob = moba_attention(to_mh(qb), to_mh(kb), to_mh(vb)).astype(h.dtype)
    ob = ob * jax.nn.silu(moba_z)
    u_b = ob @ w_branch_b

    merged = jax.nn.sigmoid(gate_a) * u_a + jax.nn.sigmoid(gate_b) * u_b
    return merged @ w_out

def first_inputs(seed: int = 0) -> dict:
    key = jax.random.key(seed)
    ks = jax.random.split(key, 12)
    f32 = jnp.float32
    x = jax.random.normal(ks[0], (BATCH, SEQ, D_MODEL), f32)
    pre_norm_w = 1.0 + 0.05 * jax.random.normal(ks[1], (DEPTH, D_MODEL), f32)
    w_in = jax.random.normal(ks[2], (DEPTH, D_MODEL, IN_WIDTH), f32) * (D_MODEL ** -0.5)
    conv_w = jax.random.normal(ks[3], (DEPTH, CONV_WIDTH, 3 * GDN_WIDTH), f32) * (CONV_WIDTH ** -0.5)
    a_log = jnp.log(jax.random.uniform(ks[4], (DEPTH, GDN_HEADS), f32, minval=1.0, maxval=16.0))
    dt = jnp.exp(jax.random.uniform(ks[5], (DEPTH, GDN_HEADS), f32, minval=np.log(1e-3), maxval=np.log(1e-1)))
    dt_bias = dt + jnp.log(-jnp.expm1(-dt))
    gdn_norm_w = 1.0 + 0.05 * jax.random.normal(ks[6], (DEPTH, GDN_HEAD_DIM), f32)
    w_branch_a = jax.random.normal(ks[7], (DEPTH, GDN_WIDTH, D_MODEL), f32) * (GDN_WIDTH ** -0.5)
    w_branch_b = jax.random.normal(ks[8], (DEPTH, MOBA_WIDTH, D_MODEL), f32) * (MOBA_WIDTH ** -0.5)
    w_out = jax.random.normal(ks[9], (DEPTH, D_MODEL, D_MODEL), f32) * (D_MODEL ** -0.5)
    post_norm_w = 1.0 + 0.05 * jax.random.normal(ks[10], (DEPTH, D_MODEL), f32)
    return {"x": x, "pre_norm_w": pre_norm_w, "w_in": w_in, "conv_w": conv_w, "a_log": a_log,
            "dt_bias": dt_bias, "gdn_norm_w": gdn_norm_w, "w_branch_a": w_branch_a,
            "w_branch_b": w_branch_b, "w_out": w_out, "post_norm_w": post_norm_w}

def first_block(x, pre_norm_w, w_in, conv_w, a_log, dt_bias, gdn_norm_w, w_branch_a, w_branch_b, w_out, post_norm_w):
    for l in range(DEPTH):
        h = rms_norm(x, pre_norm_w[l])
        y = hybrid_mixer(h, w_in[l], conv_w[l], a_log[l], dt_bias[l], gdn_norm_w[l],
                         w_branch_a[l], w_branch_b[l], w_out[l])
        x = x + rms_norm(y, post_norm_w[l])
    return x


D_MIX = D_MODEL
ROPE_THETA = 10000.0
RMS_EPS = 1e-6
NEG_INF_2 = -1e30
TINY = 1e-30
Q_BLOCK = 128

WIDTH_A = D_MIX // 2
HEAD_DIM_A = 128
N_HEADS_A = WIDTH_A // HEAD_DIM_A
N_KV_A = 2
GROUP_A = N_HEADS_A // N_KV_A
KV_A = N_KV_A * HEAD_DIM_A
CMP_BLOCK = 32
CMP_STRIDE = 16
CMP_HIDDEN = 256
SEL_BLOCK = 64
SEL_TOPK = 16
SEL_Q_CHUNK = 32
WIN_A = 512
FORCE_SCORE = 1e4

WIDTH_B = D_MIX - WIDTH_A
HEAD_DIM_B = 64
N_HEADS_B = WIDTH_B // HEAD_DIM_B
N_KV_B = 2
GROUP_B = N_HEADS_B // N_KV_B
KV_B = N_KV_B * HEAD_DIM_B
WIN_B = 128

IN_SIZES = (WIDTH_A, KV_A, KV_A, KV_A, KV_A, KV_A, KV_A, WIDTH_A, 3 * N_HEADS_A,
            WIDTH_B, KV_B, KV_B, WIDTH_B)
D_IN = 2 * WIDTH_A + 6 * KV_A + 3 * N_HEADS_A + 2 * WIDTH_B + 2 * KV_B


def _rmsnorm(x, g):
    xf = x.astype(jnp.float32)
    y = xf * lax.rsqrt(jnp.mean(xf * xf, axis=-1, keepdims=True) + RMS_EPS)
    return (y * g.astype(jnp.float32)).astype(x.dtype)

def _heads(t, n, d):
    return t.reshape(t.shape[0], t.shape[1], n, d)

def _rope(x):
    S, d = x.shape[1], x.shape[-1]
    inv = ROPE_THETA ** (-jnp.arange(0, d, 2, dtype=jnp.float32) / d)
    ang = jnp.arange(S, dtype=jnp.float32)[:, None] * inv[None, :]
    cos = jnp.cos(ang)[None, :, None, :]
    sin = jnp.sin(ang)[None, :, None, :]
    xf = x.astype(jnp.float32)
    x1, x2 = xf[..., : d // 2], xf[..., d // 2:]
    return jnp.concatenate([x1 * cos - x2 * sin, x2 * cos + x1 * sin], axis=-1).astype(x.dtype)

def _masked_softmax(s, mask, sink=None):
    s = jnp.where(mask, s.astype(jnp.float32), NEG_INF_2)
    m = jnp.max(s, axis=-1, keepdims=True)
    if sink is not None:
        m = jnp.maximum(m, sink)
    e = jnp.where(mask, jnp.exp(s - m), 0.0)
    denom = jnp.sum(e, axis=-1, keepdims=True)
    if sink is not None:
        denom = denom + jnp.exp(sink - m)
    return e / jnp.maximum(denom, TINY)

def _compress(kv, pos_emb, w1, w2):
    B, S, Hkv, D = kv.shape
    n_c = (S - CMP_BLOCK) // CMP_STRIDE + 1
    idx = jnp.arange(n_c)[:, None] * CMP_STRIDE + jnp.arange(CMP_BLOCK)[None, :]
    blocks = kv[:, idx] + pos_emb[None, None, :, None, :].astype(kv.dtype)
    flat = blocks.transpose(0, 1, 3, 2, 4).reshape(B, n_c, Hkv, CMP_BLOCK * D)
    return jax.nn.silu(flat @ w1) @ w2

def _compressed_attention(q, kc, vc):
    S, D = q.shape[1], q.shape[-1]
    n_c = kc.shape[1]
    s = jnp.einsum('bskgd,bckd->bkgsc', q, kc) * (D ** -0.5)
    ends = jnp.arange(n_c) * CMP_STRIDE + CMP_BLOCK - 1
    mask = ends[None, :] <= jnp.arange(S)[:, None]
    p = _masked_softmax(s, mask)
    o = jnp.einsum('bkgsc,bckd->bskgd', p.astype(vc.dtype), vc)
    return o, p

def _select_blocks(p_cmp, S):
    n_c = p_cmp.shape[-1]
    n_sel = S // SEL_BLOCK
    c_start = np.arange(n_c) * CMP_STRIDE
    j_start = np.arange(n_sel) * SEL_BLOCK
    overlap = (c_start[:, None] < j_start[None, :] + SEL_BLOCK) & (c_start[:, None] + CMP_BLOCK > j_start[None, :])
    p_sel = jnp.einsum('bkgsc,cj->bksj', p_cmp, jnp.asarray(overlap, jnp.float32))
    t = jnp.arange(S)[:, None]
    j = jnp.arange(n_sel)[None, :]
    cur = t // SEL_BLOCK
    forced = (j == 0) | (j == cur) | (j == cur - 1)
    valid = j * SEL_BLOCK <= t
    score = jnp.where(forced, FORCE_SCORE, jnp.where(valid, p_sel, -1.0))
    _, idx = lax.top_k(score, min(SEL_TOPK, n_sel))
    return idx

def _selected_attention(q, k, v, idx):
    B, S, Hkv, G, D = q.shape
    K = idx.shape[-1]
    n_sel = S // SEL_BLOCK
    n_ch = S // SEL_Q_CHUNK
    kb = k.reshape(B, n_sel, SEL_BLOCK, Hkv, D).transpose(0, 3, 1, 2, 4)
    vb = v.reshape(B, n_sel, SEL_BLOCK, Hkv, D).transpose(0, 3, 1, 2, 4)
    gather = jax.vmap(jax.vmap(lambda blocks, i: blocks[i]))
    scale = D ** -0.5

    def chunk_fn(args):
        qc, ic, tc = args
        kg = gather(kb, ic)
        vg = gather(vb, ic)
        s = jnp.einsum('bckgd,bkcnld->bkgcnl', qc, kg) * scale
        tok = ic[..., None] * SEL_BLOCK + jnp.arange(SEL_BLOCK)
        mask = (tok <= tc[None, None, :, None, None])[:, :, None]
        C = qc.shape[1]
        p = _masked_softmax(s.reshape(B, Hkv, G, C, K * SEL_BLOCK), mask.reshape(B, Hkv, 1, C, K * SEL_BLOCK))
        p = p.reshape(B, Hkv, G, C, K, SEL_BLOCK)
        return jnp.einsum('bkgcnl,bkcnld->bckgd', p.astype(vg.dtype), vg)

    qs = jnp.moveaxis(q.reshape(B, n_ch, SEL_Q_CHUNK, Hkv, G, D), 1, 0)
    ids = jnp.moveaxis(idx.reshape(B, Hkv, n_ch, SEL_Q_CHUNK, K), 2, 0)
    ts = jnp.arange(S).reshape(n_ch, SEL_Q_CHUNK)
    o = lax.map(chunk_fn, (qs, ids, ts))
    return jnp.moveaxis(o, 0, 1).reshape(B, S, Hkv, G, D)

def _banded_attention(q, k, v, window, sink=None):
    B, S, Hkv, G, D = q.shape
    nq = S // Q_BLOCK
    kv_len = window + Q_BLOCK
    pad = ((0, 0), (window, 0), (0, 0), (0, 0))
    idx = jnp.arange(nq)[:, None] * Q_BLOCK + jnp.arange(kv_len)[None, :]
    kb = jnp.pad(k, pad)[:, idx]
    vb = jnp.pad(v, pad)[:, idx]
    qb = q.reshape(B, nq, Q_BLOCK, Hkv, G, D)
    s = jnp.einsum('bnqkgd,bnjkd->bnkgqj', qb, kb) * (D ** -0.5)
    key_pos = idx - window
    q_pos = jnp.arange(S).reshape(nq, Q_BLOCK)
    diff = q_pos[:, :, None] - key_pos[:, None, :]
    mask = ((diff >= 0) & (diff < window) & (key_pos[:, None, :] >= 0))[None, :, None, None]
    sink_b = None if sink is None else sink.astype(jnp.float32)[None, None, :, :, None, None]
    p = _masked_softmax(s, mask, sink_b)
    o = jnp.einsum('bnkgqj,bnjkd->bnqkgd', p.astype(vb.dtype), vb)
    return o.reshape(B, S, Hkv, G, D)

def second_inputs(seed: int = 0) -> dict:
    key = jax.random.key(seed)
    ks = jax.random.split(key, 12)

    def nrm(k, shape, scale):
        return jax.random.normal(k, shape, jnp.float32) * scale

    flat_in = CMP_BLOCK * HEAD_DIM_A
    return {
        'x': nrm(ks[0], (BATCH, SEQ, D_MODEL), 1.0),
        'w_in': nrm(ks[1], (DEPTH, D_MODEL, D_IN), D_MODEL ** -0.5),
        'cmp_k_w1': nrm(ks[2], (DEPTH, flat_in, CMP_HIDDEN), flat_in ** -0.5),
        'cmp_k_w2': nrm(ks[3], (DEPTH, CMP_HIDDEN, HEAD_DIM_A), CMP_HIDDEN ** -0.5),
        'cmp_v_w1': nrm(ks[4], (DEPTH, flat_in, CMP_HIDDEN), flat_in ** -0.5),
        'cmp_v_w2': nrm(ks[5], (DEPTH, CMP_HIDDEN, HEAD_DIM_A), CMP_HIDDEN ** -0.5),
        'cmp_k_pos': nrm(ks[6], (DEPTH, CMP_BLOCK, HEAD_DIM_A), 0.1),
        'cmp_v_pos': nrm(ks[7], (DEPTH, CMP_BLOCK, HEAD_DIM_A), 0.1),
        'sinks': nrm(ks[8], (DEPTH, N_HEADS_B), 1.0),
        'w_out': nrm(ks[9], (DEPTH, D_MIX, D_MODEL), D_MIX ** -0.5),
        'norm_g': 1.0 + nrm(ks[10], (DEPTH, D_MODEL), 0.01),
        'final_g': 1.0 + nrm(ks[11], (D_MODEL,), 0.01),
    }

def second_block(x, w_in, cmp_k_w1, cmp_k_w2, cmp_v_w1, cmp_v_w2, cmp_k_pos, cmp_v_pos, sinks, w_out, norm_g, final_g):
    B, S, _ = x.shape
    offsets = np.cumsum(IN_SIZES)[:-1].tolist()
    for l in range(DEPTH):
        h = _rmsnorm(x, norm_g[l])
        proj = h @ w_in[l]
        (qa, kca, vca, ksa, vsa, kwa, vwa, za, ga,
         qb, kb, vb, zb) = jnp.split(proj, offsets, axis=-1)

        qa = _rope(_heads(qa, N_HEADS_A, HEAD_DIM_A)).reshape(B, S, N_KV_A, GROUP_A, HEAD_DIM_A)
        kc = _compress(_rope(_heads(kca, N_KV_A, HEAD_DIM_A)), cmp_k_pos[l], cmp_k_w1[l], cmp_k_w2[l])
        vc = _compress(_heads(vca, N_KV_A, HEAD_DIM_A), cmp_v_pos[l], cmp_v_w1[l], cmp_v_w2[l])
        o_cmp, p_cmp = _compressed_attention(qa, kc, vc)
        sel_idx = _select_blocks(p_cmp, S)
        o_sel = _selected_attention(qa, _rope(_heads(ksa, N_KV_A, HEAD_DIM_A)), _heads(vsa, N_KV_A, HEAD_DIM_A), sel_idx)
        o_win = _banded_attention(qa, _rope(_heads(kwa, N_KV_A, HEAD_DIM_A)), _heads(vwa, N_KV_A, HEAD_DIM_A), WIN_A)
        gates = jax.nn.sigmoid(ga.astype(jnp.float32)).reshape(B, S, N_KV_A, GROUP_A, 3).astype(x.dtype)
        o_a = gates[..., 0:1] * o_cmp + gates[..., 1:2] * o_sel + gates[..., 2:3] * o_win
        y_a = o_a.reshape(B, S, WIDTH_A) * jax.nn.silu(za)

        qb = _rope(_heads(qb, N_HEADS_B, HEAD_DIM_B)).reshape(B, S, N_KV_B, GROUP_B, HEAD_DIM_B)
        o_b = _banded_attention(qb, _rope(_heads(kb, N_KV_B, HEAD_DIM_B)), _heads(vb, N_KV_B, HEAD_DIM_B),
                                WIN_B, sink=sinks[l].reshape(N_KV_B, GROUP_B))
        y_b = o_b.reshape(B, S, WIDTH_B) * jax.nn.silu(zb)

        x = x + jnp.concatenate([y_a, y_b], axis=-1) @ w_out[l]
    return _rmsnorm(x, final_g)


def setup_inputs(seed=0):
    out = dict(first_inputs(seed))
    for name, value in second_inputs(seed + 1).items():
        if name != "x":
            out[name + "_2"] = value
    return out


def reference(
    x, pre_norm_w, w_in, conv_w, a_log, dt_bias, gdn_norm_w, w_branch_a, w_branch_b, w_out,
    post_norm_w, w_in_2, cmp_k_w1_2, cmp_k_w2_2, cmp_v_w1_2, cmp_v_w2_2, cmp_k_pos_2,
    cmp_v_pos_2, sinks_2, w_out_2, norm_g_2, final_g_2,
):
    x = first_block(
        x, pre_norm_w, w_in, conv_w, a_log, dt_bias, gdn_norm_w, w_branch_a, w_branch_b, w_out,
        post_norm_w,
    )
    return second_block(
        x, w_in_2, cmp_k_w1_2, cmp_k_w2_2, cmp_v_w1_2, cmp_v_w2_2, cmp_k_pos_2, cmp_v_pos_2,
        sinks_2, w_out_2, norm_g_2, final_g_2,
    )


_drawn_inputs = setup_inputs


def setup_inputs(seed=0):
    import zlib

    import numpy as np

    out = dict(_drawn_inputs(seed))
    spreads = {}
    factors = {'cmp_k_w1_2': 3.62,
     'cmp_k_w2_2': 3.755,
     'cmp_k_pos_2': 8.0,
     'cmp_v_pos_2': 7.268,
     'sinks_2': 33.8,
     'norm_g_2': 8.0,
     'final_g_2': 32.793}
    for name, (base, spread) in spreads.items():
        noise = np.random.default_rng([zlib.crc32(name.encode()), seed]).standard_normal(out[name].shape)
        drawn = base * np.exp(spread * noise) if base else spread * noise
        out[name] = __import__('jax').numpy.asarray(drawn.astype(out[name].dtype))
    for name, factor in factors.items():
        out[name] = (out[name] * factor).astype(out[name].dtype)
    return out
```

```python
from contextlib import ExitStack

import numpy as np

import concourse.bass as bass
from concourse import mybir

F32 = mybir.dt.float32
F32R = mybir.dt.float32r
BF16 = mybir.dt.bfloat16
ALU = mybir.AluOpType
ACT = mybir.ActivationFunctionType
AXX = mybir.AxisListType.X

P = 128
SEQ = 256
NT = SEQ // P
D = 2048
KT = D // P
HEADS = 8
QUAD = 4
COLS = 512
PIECE_KT = 2
GDN_W = 1024
CONV = 4
EPS = 1e-6
SCALE = 128.0 ** -0.5
SCALE_B = 64.0 ** -0.5
NEG = -1e30
TINY = 1e-30
N_CMP = 15
CMP_L = 32
LEVELS = 7
RAW_SLOTS = 5
SPLIT_SLOTS = 4
AHEAD = 2
AUX = 4


class Signal:

    def __init__(self, sem, name, known, step=1):
        self.sem, self.name, self.known, self.step, self.seen, self.n = sem, name, known, step, {}, 0

    def event(self, *key):
        self.n += self.step
        assert key not in self.seen, (self.name, key)
        self.seen[key] = self.n
        return self.sem, self.step

    def after(self, *key):
        if self.known is None:
            return self.sem, 1
        return self.sem, self.known[key]


class Group:

    def __init__(self, name, weight, col, lhs, kt=KT, cols=COLS, kind="proj"):
        self.name, self.weight, self.col, self.lhs, self.kt, self.cols, self.kind = name, weight, col, lhs, kt, cols, kind


def groups():
    z, mo = 3 * GDN_W, 4 * GDN_W + 2 * HEADS
    mz, ga = mo + 3 * 1024, mo + 4 * 1024
    gb = ga + D
    out = []
    for h in range(2):
        for n, part in enumerate("qkv"):
            out.append(Group(("conv", part, h), "w_in", n * GDN_W + h * COLS, "h1"))
    for h in range(2):
        out.append(Group(("z", h), "w_in", z + h * COLS, "h1"))
    for h in range(2):
        for n, part in enumerate("qkv"):
            out.append(Group(("moba", part, h), "w_in", mo + n * 1024 + h * COLS, "h1"))
    for h in range(2):
        out.append(Group(("mz", h), "w_in", mz + h * COLS, "h1"))

    def gates(c):
        out.append(Group(("ga", c), "w_in", ga + c * COLS, "h1"))
        out.append(Group(("gb", c), "w_in", gb + c * COLS, "h1"))

    def branches(c):
        out.append(Group(("ua", c), "w_branch_a", c * COLS, "oa", kt=8))
        out.append(Group(("ub", c), "w_branch_b", c * COLS, "ob", kt=8))

    gates(0)
    gates(1)
    branches(0)
    branches(1)
    gates(2)
    branches(2)
    gates(3)
    branches(3)
    for c in range(4):
        out.append(Group(("wo", c), "w_out", c * COLS, "merged"))
    out.append(Group(("kcv",), "w_in_2", 1024, "h2"))
    out.append(Group(("qa", 0), "w_in_2", 0, "h2"))
    out.append(Group(("ksv",), "w_in_2", 1536, "h2"))
    out.append(Group(("kwv",), "w_in_2", 2048, "h2"))
    out.append(Group(("qa", 1), "w_in_2", 512, "h2"))
    out.append(Group(("cmp", "k"), "cmp_k_w1_2", 0, "blk", kt=CMP_L, cols=256, kind="cmp"))
    out.append(Group(("cmp", "v"), "cmp_v_w1_2", 0, "blk", kt=CMP_L, cols=256, kind="cmp"))
    out.append(Group(("kvb",), "w_in_2", 4632, "h2", cols=256))
    for h in range(2):
        out.append(Group(("qb", h), "w_in_2", 3608 + h * COLS, "h2"))
    for h in range(2):
        out.append(Group(("za", h), "w_in_2", 2560 + h * COLS, "h2"))
    for h in range(2):
        out.append(Group(("zb", h), "w_in_2", 4888 + h * COLS, "h2"))
    for c in range(4):
        out.append(Group(("w2", c), "w_out_2", c * COLS, "y"))
    return out


GROUPS = groups()
PIECES = []
END = {}
for _g, _group in enumerate(GROUPS):
    _n = PIECE_KT * COLS // _group.cols
    for _k in range(0, _group.kt, _n):
        PIECES.append((_g, _k, _n, _k == 0, _k + _n == _group.kt))
    END[_group.name] = len(PIECES) - 1
TICKS = len(PIECES)
LAST = 40
SPLIT = [n for n, p in enumerate(PIECES) if GROUPS[p[0]].kind == "proj"]
SPLIT_NO = {n: i for i, n in enumerate(SPLIT)}


def plan():
    steps = [[] for _ in range(TICKS + LAST)]

    def at(tick, *step):
        steps[tick].append(step)

    at(0, "ba")
    at(1, "gates")
    at(2, "gcum")
    for h in range(2):
        for part in "qkv":
            c = END[("conv", part, h)]
            at(c + 1, "raw_out", part, h)
            at(c + 2, "raw_flip", part, h)
            at(c + 3, "conv", part, h, 0)
            at(c + 4, "conv", part, h, 1)
            at(c + 5, "conv_silu", part, h)
            at(c + 6, "conv_back", part, h)
            at(c + 7, "token_out", part, h)
            if part != "v":
                at(c + 9, "qk_flip", part, h)
                at(c + 10, "qk_out", part, h)
    base = END[("conv", "v", 1)] + 9
    for h in range(2):
        for t in range(NT):
            s = base + 3 * t
            at(s, "gu", h, t)
            at(s + 1, "gram", h, t)
            at(s + 2, "decay", h, t)
            at(s + 3, "tri", h, t)
            at(s + 4, "tri_flip", h, t)
            at(s + 5, "invert_first", h, t)
            for n in range(2, LEVELS + 1):
                at(s + 8 + 2 * (n - 2), "invert_y", h, t, n)
                at(s + 9 + 2 * (n - 2), "invert_t", h, t, n)
        s = base + 23
        for n in range(5):
            at(s + 2 * n, "delta", h, n)
        at(s + 10, "delta_norm", h)
        for t in range(NT):
            at(s + 12, "flip", "oa", h, t)
        base = s + 11
    for h in range(2):
        at(END[("z", h)] + 1, "z_out", h)
    for h in range(2):
        c = END[("moba", "q", h)]
        for part in "qk":
            c = END[("moba", part, h)]
            at(c + 1, "m_raw", part, h)
            at(c + 2, "m_flip", part, h, 0)
            at(c + 4, "m_flip", part, h, 1)
        at(END[("moba", "v", h)] + 1, "m_v", h)
        at(END[("mz", h)] + 1, "mz_out", h)
    s = max(base + 3, END[("mz", 1)] + 2)
    for h in range(2):
        for t in range(NT):
            for n in range(5):
                at(s + n, "att", "m", h, t, n)
            at(s + 5, "flip", "ob", h, t)
            s += 4
    for c in range(4):
        at(END[("ga", c)] + 1, "gate_out", "a", c)
        at(END[("gb", c)] + 1, "gate_out", "b", c)
        at(END[("ua", c)] + 1, "branch", "a", c)
        at(END[("ub", c)] + 1, "branch", "b", c)
        for t in range(NT):
            at(END[("ub", c)] + 3, "flip", "merged", c, t)
        at(END[("wo", c)] + 1, "y_out", c)
    c = END[("wo", 3)]
    steps[c] += steps[c + 1]
    steps[c + 1] = []
    at(c, "residual")
    for n in range(4):
        for t in range(NT):
            at(c, "flip", "h2", n, t)
    at(c + 7, "ag")
    at(c + 8, "head_gates")
    for name in (("kcv",), ("ksv",), ("kwv",), ("qa", 0), ("qa", 1), ("kvb",), ("qb", 0), ("qb", 1)):
        c = END[name]
        at(c + 1, "rope", *name)
        at(c + 3, "rope_flip", *name)
    for n, part in enumerate("kv"):
        at(END[("kcv",)] + 5 + n, "blocks", part)
        at(END[("cmp", part)] + 1, "cmp_silu", part)
        at(END[("cmp", part)] + 2, "cmp_out", part)
    s = END[("ksv",)] + 5
    for h in range(2):
        for kind in "sw":
            for t in range(NT):
                for n in range(5):
                    at(s + n, "att", kind, h, t, n)
                s += 4
    s = max(s, END[("cmp", "v")] + 4)
    for t in range(NT):
        for n in range(5):
            at(s + n, "catt", t, n)
        s += 4
    s = max(s, END[("qb", 0)] + 5)
    for h in range(4):
        for t in range(NT):
            for n in range(5):
                at(s + n, "att", "b", h, t, n)
            s += 4
    for n, (name, h) in enumerate((("za", 0), ("za", 1), ("zb", 0), ("zb", 1))):
        c = END[(name, h)]
        at(c + 1, "z2_out", n)
        at(c + 2, "y_gate", n)
        for t in range(NT):
            at(c + 3, "flip", "y", n, t)
    for c in range(4):
        at(END[("w2", c)] + 1, "y2_out", c)
    at(END[("w2", 3)] + 2, "finish")
    return steps


PLAN = plan()


def constants():
    i, j = np.arange(P)[:, None], np.arange(P)[None, :]
    f = np.float32
    out = {"ident": (i == j).astype(f), "upto": (i <= j).astype(f)}
    level = []
    for n in range(1, LEVELS + 1):
        m = 2 ** (n - 1)
        level.append(((i // (2 * m) == j // (2 * m)) & (j // m % 2 == 1) & (i // m % 2 == 0)).astype(f))
    below = (i > j).astype(f)
    out["levels"] = np.ascontiguousarray(np.stack([below, level[0].T] + level, 1))
    causal = np.where(j <= i, 0.0, NEG).astype(f)
    out["masks"] = np.ascontiguousarray(np.concatenate(
        [np.zeros((P, P), f), causal, np.where(j > i, 0.0, NEG).astype(f), causal], 1))
    s = np.arange(SEQ)
    ok = (np.arange(N_CMP) * 16 + 31)[None, :] <= s[:, None]
    cm = np.stack([np.where(ok, 0.0, NEG), ok.astype(f)], 1).astype(f)
    out["cmask"] = np.ascontiguousarray(cm.reshape(NT, P, 2, N_CMP).transpose(1, 2, 0, 3))
    rope = []
    for d in (128, 64):
        inv = f(10000.0) ** (-np.arange(0, d, 2, dtype=f) / f(d))
        ang = (s.astype(f)[:, None] * inv[None, :].astype(f)).astype(f).astype(np.float64)
        cos, sin = np.cos(ang), np.sin(ang)
        both = np.stack([np.concatenate([cos, cos], 1), np.concatenate([-sin, sin], 1)], 0).astype(f)
        rope.append(both.reshape(2, NT, P, d).transpose(2, 0, 1, 3))
    out["rope_a"], out["rope_b"] = (np.ascontiguousarray(r) for r in rope)
    return out


def build(nc, known, ins, out):
    ctx = ExitStack()
    with ctx:
        signals = {}

        def signal(name, step=1):
            k = None if known is None else known["signals"][name]
            s = signals[name] = Signal(ctx.enter_context(nc.semaphore(name)), name, k, step)
            return s

        start = (nc.sbuf_base + 31) // 32 * 32
        end = nc.sbuf_usable_end
        ctx.enter_context(nc.sbuf_tensor("arena", [P, (end - start) // 4 - 16], F32))
        cursor = [start]

        def place(name, shape, dtype, offset=None):
            size = int(np.prod(shape[1:])) * (2 if dtype == BF16 else 4)
            if offset is None:
                offset = cursor[0]
                cursor[0] += (size + 31) // 32 * 32
                assert cursor[0] <= end, (name, cursor[0], end)
            return nc.alloc_sbuf_tensor_at(name, list(shape), dtype, offset=offset)

        raw_w = [place(f"raw_w{i}", [P, PIECE_KT * COLS], F32) for i in range(RAW_SLOTS)]
        hi_w = [place(f"hi_w{i}", [P, PIECE_KT * COLS], F32R) for i in range(SPLIT_SLOTS)]
        lo_w = [place(f"lo_w{i}", [P, PIECE_KT * COLS], F32R) for i in range(SPLIT_SLOTS)]
        h_hi = place("h_hi", [P, KT, SEQ], F32R)
        h_lo = place("h_lo", [P, KT, SEQ], F32R)
        ident = place("ident", [P, P], F32)
        upto = place("upto", [P, P], F32)
        ones = place("ones", [P, P], F32)
        levels = place("levels", [P, LEVELS + 2, P], F32)
        masks = place("masks", [P, 2, SEQ], F32)
        cmask = place("cmask", [P, 2, NT, N_CMP], F32)
        rope_a = place("rope_a", [P, 2, NT, 128], F32)
        rope_b = place("rope_b", [P, 2, NT, 64], F32)
        conv_w = place("conv_w", [P, CONV, 24], F32)
        gnorm_w = place("gnorm_w", [P, P], F32)
        small = place("small", [P, 640], F32)
        half = place("half", [P, 16], F32)
        w2s = {k: place(f"w2_{k}", [P, 2, P], F32) for k in "kv"}
        pos = {k: place(f"pos_{k}", [P, CMP_L], F32) for k in "kv"}
        top = [0]

        def bit(n):
            top[0] += n
            assert top[0] <= 640
            return small[:, top[0] - n:top[0]]

        dt_row, alog_row, sink_row = bit(HEADS), bit(HEADS), bit(16)
        r1, ry, r2, r3 = bit(NT), bit(NT), bit(NT), bit(NT)
        sum1, sumy, sum2, sum3 = bit(NT * 4), bit(NT * 4), bit(NT * 4), bit(NT * 4)
        tot = bit(NT)
        ba = bit(NT * 16)
        beta, nbeta, g, gcum, ngcum, eg, beg = (bit(NT * HEADS) for _ in range(7))
        tail, sp0, sp1, nexp = bit(HEADS), bit(NT * HEADS), bit(NT * HEADS), bit(HEADS)
        ssq, rnorm = bit(NT * QUAD), bit(NT * QUAD)
        head_gate = bit(NT * 24)
        mx, nmx, den, rden, esink = (bit(2 * QUAD) for _ in range(5))
        cmx, cden, crden = bit(HEADS), bit(HEADS), bit(HEADS)

        def tiles(ap, n):
            return ap.rearrange("p (t n) -> p t n", n=n)

        R0 = cursor[0]

        def arena(name, shape, dtype, kb):
            size = int(np.prod(shape[1:])) * 4
            assert R0 + kb * 1024 + size <= end, (name, kb, size, end - R0)
            return place(name, shape, dtype, R0 + int(kb * 1024))

        q_t = arena("q_t", [P, HEADS, SEQ], F32, 0)
        k_t = arena("k_t", [P, HEADS, SEQ], F32, 8)
        oa_hi = arena("oa_hi", [P, HEADS, SEQ], F32R, 0)
        oa_lo = arena("oa_lo", [P, HEADS, SEQ], F32R, 8)
        k_tok = arena("k_tok", [P, NT, HEADS, P], F32, 16)
        v_tok = arena("v_tok", [P, NT, HEADS, P], F32, 24)
        inv_t = arena("inv_t", [P, HEADS, NT, P], F32, 32)
        attn_t = arena("attn_t", [P, HEADS, NT, P], F32, 40)
        chain = [{n: arena(f"{n}{t}", [P, QUAD, P], F32, 48 + 8 * t + 2 * i)
                  for i, n in enumerate(("low_t", "low_m", "inv", "wide"))} for t in range(NT)]
        delta_u, delta_s, delta_r, delta_q = (arena(f"delta_{n}", [P, QUAD, P], F32, 48 + 2 * i)
                                              for i, n in enumerate("usrq"))
        delta_sq = arena("delta_sq", [P, NT, QUAD, P], F32, 48)
        raw = arena("raw", [P, NT, COLS], F32, 48)
        cv = arena("cv", [P, QUAD, SEQ], F32, 52)
        sil = arena("sil", [P, QUAD, SEQ], F32, 56)
        q_tok = arena("q_tok", [P, NT, QUAD, P], F32, 60)
        sq = arena("sq", [P, NT, QUAD, P], F32, 92)
        x_in = arena("x_in", [P, NT, D], F32, 48)
        row1 = arena("row1", [P, D], F32, 64)
        mzs = arena("mzs", [P, NT, HEADS, P], F32, 56)
        m_t = {"q": arena("mq_t", [P, HEADS, SEQ], F32, 64), "k": arena("mk_t", [P, HEADS, SEQ], F32, 72)}
        ob_hi = arena("ob_hi", [P, HEADS, SEQ], F32R, 64)
        ob_lo = arena("ob_lo", [P, HEADS, SEQ], F32R, 72)
        m_v = arena("m_v", [P, NT, HEADS, P], F32, 80)
        zs = arena("zs", [P, NT, HEADS, P], F32, 88)
        m_raw = arena("m_raw", [P, NT, COLS], F32, 96)
        ba_raw = arena("ba_raw", [P, KT, 24], F32, 96)
        ba_hi = arena("ba_hi", [P, KT, 24], F32R, 97.5)
        ba_lo = arena("ba_lo", [P, KT, 24], F32R, 99)
        junk = arena("junk", [P, COLS], F32, 104)
        att_s = arena("att_s", [P, QUAD * SEQ], F32, 96)
        att_p = arena("att_p", [P, NT, QUAD * P], F32, 100)
        att_o = arena("att_o", [P, QUAD * P], F32, 104)
        sg = {"a": [arena(f"sga{i}", [P, NT, COLS], F32, 48 + 4 * i) for i in range(2)],
              "b": [arena(f"sgb{i}", [P, NT, COLS], F32, 88 + 4 * i) for i in range(2)]}
        merged = arena("merged", [P, NT, COLS], F32, 96)
        m_hi = arena("m_hi", [P, KT, SEQ], F32R, 16)
        m_lo = arena("m_lo", [P, KT, SEQ], F32R, 32)
        y1 = arena("y1", [P, NT, D], F32, 48)
        x2 = arena("x2", [P, NT, D], F32, 64)
        post_row = arena("post_row", [P, D], F32, 80)
        row2 = arena("row2", [P, D], F32, 88)
        qa_t = arena("qa_t", [P, HEADS, SEQ], F32, 0)
        kt2 = {n: arena(f"{n}_t", [P, 2, SEQ], F32, 8 + 2 * i) for i, n in enumerate(("kc", "vc", "ks", "kw"))}
        v2 = {n: arena(f"{n}_tok", [P, NT, 2, P], F32, 48 + 2 * i) for i, n in enumerate(("vs", "vw"))}
        kz = arena("kz", [P, 2, 2, SEQ], F32, 52)
        vb = arena("vb", [P, NT, 2, 64], F32, 56)
        hs = {p: arena(f"hs_{p}", [P, 2, 2 * N_CMP], F32, 57 + 0.25 * i) for i, p in enumerate("kv")}
        ck_t = arena("ck_t", [P, 2 * N_CMP], F32, 57.5)
        cs = arena("cs", [P, HEADS, N_CMP], F32, 58)
        cv_tok = arena("cv_tok", [N_CMP, 2, P], F32, 59)
        oa_tok = arena("oa_tok", [P, NT, HEADS * P], F32, 60)
        ob_tok = arena("ob_tok", [P, NT, 16 * 64], F32, 68)
        blk = {p: arena(f"blk_{p}", [P, CMP_L, 2, N_CMP], F32, 76 + 4 * i) for i, p in enumerate("kv")}
        qb_t = arena("qb_t", [P, 8, SEQ], F32, 76)
        rot = [arena(f"rot{i}", [P, NT, COLS], F32, 84 + 4 * i) for i in range(3)]
        z2 = [arena(f"z2_{i}", [P, NT, COLS], F32, 84 + 4 * i) for i in range(2)]
        cp_t = arena("cp_t", [N_CMP, HEADS * P], F32, 100)
        x3 = arena("x3", [P, NT, D], F32, 0)
        last_row = arena("last_row", [P, D], F32, 48)
        y3 = arena("y3", [P, NT, D], F32, 76)
        rows_in = arena("rows_in", [P, 2, P], F32, 102)

        acc = ctx.enter_context(nc.psum_tensor("acc", [P, 2, NT, COLS], F32))
        aux = ctx.enter_context(nc.psum_tensor("aux", [P, AUX, COLS], F32))
        scratch = nc.dram_tensor("x2_scratch", [SEQ, D], F32, kind="Internal").ap()

        raw_ready = [signal(f"raw_ready{i}", 16) for i in range(RAW_SLOTS)]
        x_ready = [signal(f"x_ready{i}", 16) for i in range(NT)]
        row_ready = signal("row_ready", 16)
        const_ready = signal("const_ready", 16)
        ba_ready = signal("ba_ready", 16)
        block2_rows = signal("block2_rows", 16)
        x_again = signal("x_again", 16)
        spilled = signal("spilled", 16)
        x3_ready = signal("x3_ready", 16)
        last_ready = signal("last_ready", 16)
        stored = signal("stored", 16)
        hi_ready = signal("hi_ready")
        lo_ready = signal("lo_ready")
        used = signal("used")
        pe_did = signal("pe_did")
        act_did = signal("act_did")
        dve_did = signal("dve_did")
        pool_did = signal("pool_did")
        flip_source = signal("flip_source")
        flip_filled = signal("flip_filled")
        flip_hi = signal("flip_hi")
        flip_lo = signal("flip_lo")
        act_chain, dve_chain, pool_chain = (ctx.enter_context(nc.semaphore(f"{e}_chain"))
                                            for e in ("act", "dve", "pool"))

        LHS = {"h1": (h_hi, h_lo), "h2": (h_hi, h_lo), "oa": (oa_hi, oa_lo), "ob": (ob_hi, ob_lo),
               "merged": (m_hi, m_lo), "y": (m_hi, m_lo)}

        def flip_bank(name, n, t):
            return {"oa": 3, "ob": 3, "y": 2 + t}.get(name, (2 * n + t) % AUX)

        def acc_of(tick):
            return acc[:, PIECES[tick][0] % 2]

        def quad(h):
            return slice(h * QUAD, (h + 1) * QUAD)

        def over_heads(ap, n=QUAD):
            return ap.unsqueeze(1).broadcast_to([P, n, ap.shape[-1]])

        def over_cols(ap, m=P):
            return ap.unsqueeze(2).broadcast_to([P, ap.shape[-1], m])

        conv_order = [(p, h) for h in range(2) for p in "qkv"]
        qk_order = [(p, h) for h in range(2) for p in "qk"]

        def before_conv(part, h):
            return conv_order[conv_order.index((part, h)) - 1]

        def before_qk(part, h):
            return qk_order[qk_order.index((part, h)) - 1]

        att_before, rope_before, last_att, last_rope = {}, {}, None, None
        for steps_ in PLAN:
            for name, *args in steps_:
                if name == "att" and args[3] == 0:
                    att_before[tuple(args[:3])] = last_att
                    last_att = ("att", *args[:3], 4)
                if name == "rope":
                    rope_before[tuple(args)] = last_rope
                    last_rope = tuple(args)

        block = ctx.enter_context(nc.Block())

        def piece_source(no):
            g, k0, n, _, _ = PIECES[no]
            group = GROUPS[g]
            w = ins[group.weight][0]
            return w[k0 * P:(k0 + n) * P, group.col:group.col + group.cols].rearrange("(k p) c -> p k c", p=P)

        def piece_view(buf, no):
            g, _, n, _, _ = PIECES[no]
            return buf[:, :].rearrange("p (k c) -> p k c", k=n)

        @block.sync
        def _(sp):
            x = ins["x"][0].rearrange("(t p) d -> p t d", p=P)
            for t in range(NT):
                sp.dma_start(x_in[:, t], x[:, t]).then_inc(*x_ready[t].event(0))
                if t == 0:
                    sp.dma_start(row1[:], ins["pre_norm_w"][0].partition_broadcast(P)).then_inc(*row_ready.event(1))
                    sp.dma_start(ident[:], ins["ident"]).then_inc(*row_ready.event(0))

            def load(no):
                if no >= RAW_SLOTS:
                    old = no - RAW_SLOTS
                    sp.wait_ge(*(lo_ready if old in SPLIT_NO else used).after(old))
                sp.dma_start(piece_view(raw_w[no % RAW_SLOTS], no), piece_source(no)).then_inc(
                    *raw_ready[no % RAW_SLOTS].event(no))

            for no in range(3):
                load(no)
            loads = [
                (rows_in[0:96, 0], ins["conv_w"][0].rearrange("j (i c) -> (j i) c", c=P)),
                (rows_in[0:CMP_L, 1], ins["cmp_k_pos_2"][0]),
                (rows_in[CMP_L:2 * CMP_L, 1], ins["cmp_v_pos_2"][0]),
                (ba_raw[:, :, 0:16], ins["w_in"][0][:, 4 * GDN_W:4 * GDN_W + 16].rearrange("(k p) c -> p k c", p=P)),
                (dt_row, ins["dt_bias"][0].partition_broadcast(P)),
                (alog_row, ins["a_log"][0].partition_broadcast(P)),
                (upto[:], ins["upto"]),
            ]
            for n, (to, source) in enumerate(loads):
                sp.dma_start(to, source).then_inc(*const_ready.event(n))
            for no in range(3, RAW_SLOTS):
                load(no)
            loads = [
                (levels[:], ins["levels"]),
                (masks[:], ins["masks"].rearrange("p (a b) -> p a b", a=2)),
                (cmask[:], ins["cmask"]),
                (rope_a[:], ins["rope_a"]),
                (rope_b[:], ins["rope_b"]),
                (gnorm_w[:], ins["gdn_norm_w"][0].partition_broadcast(P)),
                (sink_row, ins["sinks_2"][0].partition_broadcast(P)),
                (w2s["k"][:], ins["cmp_k_w2_2"][0].rearrange("(k p) c -> p k c", p=P)),
                (w2s["v"][:], ins["cmp_v_w2_2"][0].rearrange("(k p) c -> p k c", p=P)),
            ]
            for n, (to, source) in enumerate(loads):
                sp.dma_start(to, source).then_inc(*block2_rows.event(n))
            for no in range(RAW_SLOTS, TICKS):
                load(no)
            store = out[0].rearrange("(t p) d -> p t d", p=P)
            for t in range(NT):
                sp.wait_ge(*(act_did, dve_did)[t].after("finish"))
                sp.dma_start(store[:, t], y3[:, t]).then_inc(*stored.event(t))
            sp.wait_ge(*stored.after(NT - 1))

        @block.gpsimd
        def _(pool):
            n_chain = [0]

            def link(ins_):
                n_chain[0] += 1
                ins_.then_inc(pool_chain, 1)
                pool.wait_ge(pool_chain, n_chain[0])

            link(pool.memset(half[:], -0.5))
            pool.memset(ones[:], 1.0).then_inc(*pool_did.event("ones"))

            def root(dst, src, scale, key, times=None):
                n = dst.shape[-1]
                link(pool.tensor_scalar(dst, src, scale, EPS, ALU.mult, ALU.add))
                last = pool.tensor_tensor(dst, dst, half[:, 0:n], ALU.pow)
                if times is not None:
                    link(last)
                    last = pool.tensor_scalar(dst, dst, times, None, ALU.mult)
                last.then_inc(*pool_did.event(*key))

            pool.wait_ge(*dve_did.after("sum1"))
            root(r1, tot, 1.0 / D, ("r1",))

            def token_out(part, h):
                if part != "v":
                    pool.wait_ge(*dve_did.after("ssq", part, h))
                    root(rnorm, ssq, 1.0, ("rnorm", part, h), SCALE if part == "q" else None)

            def delta_norm(h):
                pool.wait_ge(*dve_did.after("delta_ssq", h))
                root(rnorm, ssq, 1.0 / P, ("delta_rnorm", h))

            def branch(ab, c):
                if (ab, c) == ("b", 3):
                    pool.wait_ge(*used.after(END[("ub", 3)]))
                    pool.wait_ge(*dve_did.after("branch", "b", 3))
                    pool.dma_start(x2[:], ins["x"][0].rearrange("(t p) d -> p t d", p=P)).then_inc(*x_again.event(0))
                    pool.dma_start(post_row[:], ins["post_norm_w"][0].partition_broadcast(P)).then_inc(*x_again.event(1))
                    pool.dma_start(row2[:], ins["norm_g_2"][0].partition_broadcast(P)).then_inc(*x_again.event(2))
                    for n in range(4):
                        for t in range(NT):
                            pool.wait_ge(*flip_filled.after("merged", n, t))
                    pool.dma_start(ba_raw[:], ins["w_in_2"][0][:, 3584:3608].rearrange("(k p) c -> p k c", p=P)).then_inc(
                        *ba_ready.event(0))

            def residual():
                pool.wait_ge(*dve_did.after("sumy"))
                root(ry, tot, 1.0 / D, ("ry",))
                pool.wait_ge(*dve_did.after("x2", 1))
                pool.dma_start(scratch.rearrange("(t p) d -> p t d", p=P), x2[:]).then_inc(*spilled.event(0))
                pool.wait_ge(*dve_did.after("sum2"))
                root(r2, tot, 1.0 / D, ("r2",))
                pool.wait_ge(*spilled.after(0))
                pool.wait_ge(*flip_filled.after("h2", 3, 1))
                pool.memset(kz[:], 0.0).then_inc(*pool_did.event("kz"))

            def att(kind, h, t, n):
                if (kind, h, t, n) == ("w", 1, 1, 4):
                    pool.wait_ge(*dve_did.after("catt", 1))
                    pool.dma_start(x3[:], scratch.rearrange("(t p) d -> p t d", p=P)).then_inc(*x3_ready.event(0))
                if (kind, h, t, n) == ("b", 3, 1, 4):
                    pool.wait_ge(*pe_did.after("att", "b", 3, 1, 4))
                    pool.dma_start(last_row[:], ins["final_g_2"].partition_broadcast(P)).then_inc(*last_ready.event(0))

            def finish():
                pool.wait_ge(*dve_did.after("sum3"))
                root(r3, tot, 1.0 / D, ("r3",))

            steps = {"token_out": token_out, "delta_norm": delta_norm, "branch": branch,
                     "residual": residual, "att": att, "finish": finish}
            for tick in range(TICKS + LAST):
                for name, *args in PLAN[tick]:
                    if name in steps:
                        steps[name](*args)

        @block.scalar
        def _(act):
            n_chain = [0]

            def link(ins_):
                n_chain[0] += 1
                ins_.then_inc(act_chain, 1)
                act.wait_ge(act_chain, n_chain[0])

            def split(no):
                if no not in SPLIT_NO:
                    return
                slot = SPLIT_NO[no] % SPLIT_SLOTS
                act.wait_ge(*raw_ready[no % RAW_SLOTS].after(no))
                if SPLIT_NO[no] >= SPLIT_SLOTS:
                    act.wait_ge(*used.after(SPLIT[SPLIT_NO[no] - SPLIT_SLOTS]))
                n = PIECES[no][2] * GROUPS[PIECES[no][0]].cols
                act.activation(hi_w[slot][:, 0:n], raw_w[no % RAW_SLOTS][:, 0:n], ACT.Copy).then_inc(
                    *hi_ready.event(no))

            def scaled(dst, source, r, func, last):
                for t in range(NT):
                    i = act.activation(dst[:, t], source[:, t], func, scale=r[:, t:t + 1])
                i.then_inc(*last)

            def squares(sources, key):
                for m, (source, to) in enumerate(sources):
                    last = act.activation(junk[:], source, ACT.Square, accum_out=to)
                    if m < len(sources) - 1:
                        link(last)
                last.then_inc(*act_did.event(*key))
                act.wait_ge(*act_did.after(*key))

            def flip(name, n, t):
                b = flip_bank(name, n, t)
                act.wait_ge(*flip_filled.after(name, n, t))
                hi = LHS[name][0]
                act.activation(hi[:, quad(n), t * P:(t + 1) * P],
                               aux[:, b].rearrange("p (k c) -> p k c", k=QUAD), ACT.Copy).then_inc(
                    *flip_hi.event(name, n, t))

            def gates():
                act.wait_ge(*dve_did.after("ba"))
                b3, a3 = tiles(ba, 16)[:, :, 0:HEADS], tiles(sp0, HEADS)
                act.activation(tiles(beta, HEADS), b3, ACT.Exp, scale=-1.0).then_inc(*act_did.event("exp_b"))
                link(act.activation(tiles(sp1, HEADS), a3, ACT.Abs))
                link(act.activation(sp1, sp1, ACT.Exp, scale=-1.0))
                act.wait_ge(*const_ready.after(6))
                act.activation(nexp, alog_row, ACT.Exp)
                act.activation(sp1, sp1, ACT.Ln, bias=1.0).then_inc(*act_did.event("softplus"))

            def gcum_():
                act.wait_ge(*dve_did.after("gcum"))
                act.activation(eg, gcum, ACT.Exp)
                act.activation(tail, tail, ACT.Exp).then_inc(*act_did.event("eg"))

            def raw_out(part, h):
                a = acc_of(END[("conv", part, h)])
                act.wait_ge(*used.after(END[("conv", part, h)]))
                if (part, h) != ("q", 0):
                    act.wait_ge(*pe_did.after("raw_flip", *before_conv(part, h)))
                else:
                    act.wait_ge(*pool_did.after("r1"))
                    for n in range(4):
                        for t in range(NT):
                            act.wait_ge(*flip_filled.after("h1", n, t))
                scaled(raw, a, r1, ACT.Copy, act_did.event("raw_out", part, h))

            def conv(part, h, n):
                if n:
                    return
                act.wait_ge(*pe_did.after("raw_flip", part, h))
                if (part, h) != ("q", 0):
                    act.wait_ge(*act_did.after("silu", *before_conv(part, h)))
                s = aux[:, 0:2].rearrange("p b (i c) -> p (b i) c", c=SEQ)
                first = "qkv".index(part) * HEADS + h * QUAD
                for i in range(QUAD):
                    tap = act.activation(cv[:, i], s[:, i], ACT.Copy,
                                         scale=conv_w[:, CONV - 1, first + i:first + i + 1])
                tap.then_inc(*act_did.event("tap", part, h))

            def conv_silu(part, h):
                act.wait_ge(*dve_did.after("conv", part, h))
                if (part, h) != ("q", 0):
                    act.wait_ge(*pe_did.after("conv_back", *before_conv(part, h)))
                act.activation(sil[:], cv[:], ACT.Silu).then_inc(*act_did.event("silu", part, h))

            def token_out(part, h):
                if part == "v":
                    return
                act.wait_ge(*pe_did.after("conv_back", part, h))
                if (part, h) != ("q", 0):
                    act.wait_ge(*dve_did.after("ssq", *before_qk(part, h)))
                act.activation(sq[:], aux[:, 2:4].rearrange("p b (i c) -> p b i c", c=P), ACT.Square).then_inc(
                    *act_did.event("sq", part, h))

            def qk_out(part, h):
                act.wait_ge(*pe_did.after("qk_flip", part, h))
                to = q_t if part == "q" else k_t
                s = aux[:, 2:4].rearrange("p b (i c) -> p (b i) c", c=SEQ)
                act.activation(to[:, quad(h)], s, ACT.Copy).then_inc(
                    *act_did.event("qk_out", part, h))

            def decay(h, t):
                c = chain[t]
                act.wait_ge(*pe_did.after("gram", h, t))
                for i in range(QUAD):
                    o = t * HEADS + h * QUAD + i
                    last = act.activation(c["inv"][:, i], aux[:, 0, i * P:(i + 1) * P], ACT.Abs,
                                          bias=ngcum[:, o:o + 1])
                link(last)
                act.activation(c["inv"][:], c["inv"][:], ACT.Exp, scale=-1.0).then_inc(*act_did.event("decay", h, t))

            def tri_flip(h, t):
                act.wait_ge(*pe_did.after("tri_flip", h, t))
                act.activation(chain[t]["low_t"][:], aux[:, 3].rearrange("p (i c) -> p i c", c=P), ACT.Copy).then_inc(
                    *act_did.event("tri_flip", h, t))

            def invert_t(h, t, n):
                if n == LEVELS:
                    return
                act.wait_ge(*pe_did.after("invert_t", h, t, n))
                act.activation(chain[t]["inv"][:], aux[:, 1].rearrange("p (i c) -> p i c", c=P), ACT.Copy).then_inc(
                    *act_did.event("invert_t", h, t, n))

            def delta(h, n):
                bank_to = {0: (0, delta_u), 1: (1, delta_s), 3: (1, delta_u)}
                if n in bank_to:
                    b, to = bank_to[n]
                    act.wait_ge(*pe_did.after("delta", h, n))
                    act.activation(to[:], aux[:, b].rearrange("p (i c) -> p i c", c=P), ACT.Copy).then_inc(
                        *act_did.event("delta", h, n))

            def delta_norm(h):
                act.wait_ge(*dve_did.after("delta", h, 4))
                act.activation(delta_sq[:], k_tok[:, :, quad(h)], ACT.Square).then_inc(*act_did.event("delta_sq", h))

            def z_out(h):
                a = acc_of(END[("z", h)])
                act.wait_ge(*used.after(END[("z", h)]))
                if h == 0:
                    act.wait_ge(*dve_did.after("ssq", "k", 1))
                for t in range(NT):
                    i = act.activation(zs[:, t, quad(h)], a[:, t].rearrange("p (i c) -> p i c", c=P), ACT.Silu,
                                       scale=r1[:, t:t + 1])
                i.then_inc(*act_did.event("z", h))

            def m_raw_(part, h):
                a = acc_of(END[("moba", part, h)])
                act.wait_ge(*used.after(END[("moba", part, h)]))
                if (part, h) != ("q", 0):
                    act.wait_ge(*pe_did.after("m_flip", *before_qk(part, h), 1))
                scaled(m_raw, a, r1, ACT.Copy, act_did.event("m_raw", part, h))

            def m_flip(part, h, t):
                act.wait_ge(*pe_did.after("m_flip", part, h, t))
                act.activation(m_t[part][:, quad(h), t * P:(t + 1) * P],
                               aux[:, 3].rearrange("p (i c) -> p i c", c=P), ACT.Copy).then_inc(
                    *act_did.event("m_flip", part, h, t))

            def m_v_(h):
                a = acc_of(END[("moba", "v", h)])
                act.wait_ge(*used.after(END[("moba", "v", h)]))
                for t in range(NT):
                    i = act.activation(m_v[:, t, quad(h)], a[:, t].rearrange("p (i c) -> p i c", c=P), ACT.Copy,
                                       scale=r1[:, t:t + 1])
                i.then_inc(*act_did.event("m_v", h))

            def mz_out(h):
                a = acc_of(END[("mz", h)])
                act.wait_ge(*used.after(END[("mz", h)]))
                for t in range(NT):
                    i = act.activation(mzs[:, t, quad(h)], a[:, t].rearrange("p (i c) -> p i c", c=P), ACT.Silu,
                                       scale=r1[:, t:t + 1])
                i.then_inc(*act_did.event("mz", h))

            def att(kind, h, t, n):
                k = (t + 1) * P
                if n == 2:
                    act.wait_ge(*dve_did.after("max", kind, h, t))
                    sc = SCALE_B if kind == "b" else SCALE
                    if kind == "b":
                        act.activation(esink[:, 0:QUAD], esink[:, 0:QUAD], ACT.Exp)
                    for i in range(QUAD):
                        e = act.activation(att_s[:, i * k:(i + 1) * k], att_s[:, i * k:(i + 1) * k], ACT.Exp,
                                           bias=nmx[:, i:i + 1], scale=sc, accum_out=den[:, i:i + 1])
                    e.then_inc(*act_did.event("exp", kind, h, t))
                if n == 3:
                    act.wait_ge(*pe_did.after("att", kind, h, t, 3))
                    if att_before[(kind, h, t)]:
                        act.wait_ge(*pe_did.after(*att_before[(kind, h, t)]))
                    act.activation(att_p[:, 0:t + 1], aux[:, 2:3 + t], ACT.Copy).then_inc(
                        *act_did.event("att_p", kind, h, t))

            def gate_out(ab, c):
                a = acc_of(END[("g" + ab, c)])
                act.wait_ge(*used.after(END[("g" + ab, c)]))
                if c >= 2:
                    act.wait_ge(*dve_did.after("branch", "b", c - 2))
                scaled(sg[ab][c % 2], a, r1, ACT.Sigmoid, act_did.event("gate_out", ab, c))

            def y_out(c):
                a = acc_of(END[("wo", c)])
                act.wait_ge(*used.after(END[("wo", c)]))
                squares([(a[:, t], sumy[:, t * 4 + c:t * 4 + c + 1]) for t in range(NT)], ("y_out", c))

            def residual():
                for t in range(NT):
                    act.wait_ge(*dve_did.after("x2", t))
                    squares([(x2[:, t, c * COLS:(c + 1) * COLS], sum2[:, t * 4 + c:t * 4 + c + 1])
                             for c in range(4)], ("sq2", t))
                act.wait_ge(*ba_ready.after(0))
                act.activation(ba_hi[:], ba_raw[:], ACT.Copy).then_inc(*act_did.event("ag_hi"))

            def head_gates():
                act.wait_ge(*pe_did.after("ag"))
                act.wait_ge(*pool_did.after("r2"))
                for t in range(NT):
                    i = act.activation(head_gate[:, t * 24:(t + 1) * 24], aux[:, 0, t * 24:(t + 1) * 24], ACT.Sigmoid,
                                       scale=r2[:, t:t + 1])
                i.then_inc(*act_did.event("head_gates"))

            def rope(*name):
                a = acc_of(END[name])
                half_ = COLS // 2
                to = {"kcv": rot[2][:, :, half_:COLS], "ksv": v2["vs"], "kwv": v2["vw"], "kvb": vb}.get(name[0])
                if to is None:
                    return
                act.wait_ge(*dve_did.after("rope_read", *name))
                act.wait_ge(*pool_did.after("kz"))
                w = P if name[0] == "kvb" else half_
                for t in range(NT):
                    s = a[:, t, w:2 * w]
                    if name[0] != "kcv":
                        s = s.rearrange("p (k c) -> p k c", k=2)
                    i = act.activation(to[:, t], s, ACT.Copy, scale=r2[:, t:t + 1])
                i.then_inc(*act_did.event("values", *name))

            def rope_flip(*name):
                act.wait_ge(*pe_did.after("rope_flip", *name))
                s = aux[:, 2:4].rearrange("p b (i c) -> p (b i) c", c=SEQ)
                if name[0] in ("qa", "qb"):
                    to = qa_t if name[0] == "qa" else qb_t
                    i = act.activation(to[:, quad(name[1])], s, ACT.Copy)
                elif name[0] == "kcv":
                    act.activation(kt2["kc"][:], s[:, 0:2], ACT.Copy)
                    i = act.activation(kt2["vc"][:], s[:, 2:4], ACT.Copy)
                elif name[0] == "kvb":
                    act.activation(kz[0:64, :, 0], s[0:64, 0:2], ACT.Copy)
                    i = act.activation(kz[64:P, :, 1], s[64:P, 0:2], ACT.Copy)
                else:
                    i = act.activation(kt2[name[0][0:2]][:], s[:, 0:2], ACT.Copy)
                i.then_inc(*act_did.event("rope_flip", *name))

            def cmp_silu(part):
                a = acc_of(END[("cmp", part)])
                act.wait_ge(*used.after(END[("cmp", part)]))
                act.activation(hs[part][:], a[:, :, 0:2 * N_CMP], ACT.Silu).then_inc(*act_did.event("hs", part))

            def cmp_out(part):
                act.wait_ge(*pe_did.after("cmp_out", part))
                if part == "k":
                    i = act.activation(ck_t[:], aux[:, 0, 0:2 * N_CMP], ACT.Copy)
                else:
                    i = act.activation(cv_tok[:], aux[0:N_CMP, 0, 0:2 * P].rearrange("p (k c) -> p k c", k=2), ACT.Copy)
                i.then_inc(*act_did.event("cmp_out", part))

            def catt(t, n):
                if n == 2:
                    act.wait_ge(*dve_did.after("cmax", t))
                    act.activation(cs[:], cs[:], ACT.Exp).then_inc(*act_did.event("cexp", t))
                if n == 3:
                    act.wait_ge(*pe_did.after("catt", t, 3))
                    if t == 0:
                        act.wait_ge(*pe_did.after("att", "w", 1, 1, 4))
                    else:
                        act.wait_ge(*pe_did.after("catt", 0, 4))
                    act.activation(cp_t[:].rearrange("p (b c) -> p b c", b=2), aux[0:N_CMP, 2:4], ACT.Copy).then_inc(
                        *act_did.event("cp", t))

            def z2_out(n):
                name = (("za", 0), ("za", 1), ("zb", 0), ("zb", 1))[n]
                a = acc_of(END[name])
                act.wait_ge(*used.after(END[name]))
                if n == 0:
                    act.wait_ge(*pe_did.after("rope_flip", "qb", 1))
                if n >= 2:
                    act.wait_ge(*dve_did.after("y_gate", n - 2))
                scaled(z2[n % 2], a, r2, ACT.Silu, act_did.event("z2", n))

            def y2_out(c):
                act.wait_ge(*dve_did.after("x3", c))
                squares([(x3[:, t, c * COLS:(c + 1) * COLS], sum3[:, t * 4 + c:t * 4 + c + 1]) for t in range(NT)],
                        ("sq3", c))

            def finish():
                act.wait_ge(*pool_did.after("r3"))
                act.wait_ge(*dve_did.after("y3", 3))
                act.activation(y3[:, 0], y3[:, 0], ACT.Copy, scale=r3[:, 0:1]).then_inc(*act_did.event("finish"))

            for t in range(NT):
                act.wait_ge(*x_ready[t].after(0))
                squares([(x_in[:, t, c * COLS:(c + 1) * COLS], sum1[:, t * 4 + c:t * 4 + c + 1]) for c in range(4)],
                        ("sq1", t))
            for n in range(4):
                for t in range(NT):
                    flip("h1", n, t)
            split(0)
            split(1)
            act.wait_ge(*const_ready.after(6))
            act.activation(ba_hi[:, :, 0:16], ba_raw[:, :, 0:16], ACT.Copy).then_inc(*act_did.event("ba_hi"))
            steps = {"gates": gates, "gcum": gcum_, "raw_out": raw_out, "conv": conv, "conv_silu": conv_silu,
                     "token_out": token_out, "qk_out": qk_out, "decay": decay, "tri_flip": tri_flip,
                     "invert_t": invert_t, "delta": delta, "delta_norm": delta_norm, "z_out": z_out,
                     "m_raw": m_raw_, "m_flip": m_flip, "m_v": m_v_, "mz_out": mz_out, "att": att, "flip": flip,
                     "gate_out": gate_out, "y_out": y_out, "residual": residual, "head_gates": head_gates,
                     "rope": rope, "rope_flip": rope_flip, "cmp_silu": cmp_silu, "cmp_out": cmp_out, "catt": catt,
                     "z2_out": z2_out, "y2_out": y2_out, "finish": finish}
            for tick in range(TICKS + LAST):
                if tick + AHEAD < TICKS:
                    split(tick + AHEAD)
                for name, *args in PLAN[tick]:
                    if name in steps:
                        steps[name](*args)

        @block.vector
        def _(dve):
            n_chain = [0]

            def link(ins_):
                n_chain[0] += 1
                ins_.then_inc(dve_chain, 1)
                dve.wait_ge(dve_chain, n_chain[0])

            def split(no):
                if no not in SPLIT_NO:
                    return
                slot = SPLIT_NO[no] % SPLIT_SLOTS
                dve.wait_ge(*hi_ready.after(no))
                n = PIECES[no][2] * GROUPS[PIECES[no][0]].cols
                dve.tensor_tensor(lo_w[slot][:, 0:n], raw_w[no % RAW_SLOTS][:, 0:n],
                                  hi_w[slot][:, 0:n].bitcast(F32), ALU.subtract).then_inc(*lo_ready.event(no))

            def flip(name, n, t):
                b = flip_bank(name, n, t)
                dve.wait_ge(*flip_hi.after(name, n, t))
                hi, lo = LHS[name]
                at = (slice(None), quad(n), slice(t * P, (t + 1) * P))
                dve.tensor_tensor(lo[at], aux[:, b].rearrange("p (k c) -> p k c", k=QUAD), hi[at].bitcast(F32),
                                  ALU.subtract).then_inc(*flip_lo.event(name, n, t))

            def ba_():
                dve.wait_ge(*pe_did.after("ba"))
                dve.wait_ge(*pool_did.after("r1"))
                for t in range(NT):
                    last = dve.tensor_scalar(ba[:, t * 16:(t + 1) * 16], aux[:, 0, t * 16:(t + 1) * 16], r1[:, t:t + 1],
                                             None, ALU.mult)
                link(last)
                dve.wait_ge(*const_ready.after(6))
                dve.tensor_tensor(tiles(sp0, HEADS), tiles(ba, 16)[:, :, HEADS:2 * HEADS], over_heads(dt_row, NT),
                                  ALU.add).then_inc(*dve_did.event("ba"))

            def gates():
                dve.wait_ge(*act_did.after("exp_b"))
                link(dve.tensor_scalar(beta, beta, 1.0, None, ALU.add))
                link(dve.reciprocal(beta, beta))
                dve.tensor_scalar(nbeta, beta, -1.0, None, ALU.mult)
                dve.wait_ge(*act_did.after("softplus"))
                link(dve.tensor_scalar(sp0, sp0, 0.0, None, ALU.max))
                link(dve.tensor_tensor(sp0, sp0, sp1, ALU.add))
                link(dve.tensor_scalar(sp0, sp0, -1.0, None, ALU.mult))
                dve.tensor_tensor(tiles(g, HEADS), tiles(sp0, HEADS), over_heads(nexp, NT), ALU.mult).then_inc(
                    *dve_did.event("g"))

            def gcum_():
                dve.wait_ge(*pe_did.after("gcum"))
                link(dve.tensor_copy(gcum, aux[:, 1, 0:NT * HEADS]))
                dve.tensor_scalar(ngcum, gcum, -1.0, None, ALU.mult)
                dve.tensor_tensor(tail, aux[:, 1, NT * HEADS:NT * HEADS + HEADS], gcum[:, 0:HEADS],
                                  ALU.subtract).then_inc(*dve_did.event("gcum"))
                dve.wait_ge(*act_did.after("eg"))
                dve.tensor_tensor(beg, beta, eg, ALU.mult).then_inc(*dve_did.event("beg"))

            def conv(part, h, n):
                dve.wait_ge(*act_did.after("tap", part, h))
                s = aux[:, 0:2].rearrange("p b (i c) -> p (b i) c", c=SEQ)
                first = "qkv".index(part) * HEADS + h * QUAD
                for back in range(1, CONV):
                    for i in range(2 * n, 2 * n + 2):
                        last = dve.scalar_tensor_tensor(
                            cv[:, i, back:SEQ], s[:, i, 0:SEQ - back],
                            conv_w[:, CONV - 1 - back, first + i:first + i + 1], cv[:, i, back:SEQ], ALU.mult, ALU.add)
                    if back < CONV - 1:
                        link(last)
                if n:
                    last.then_inc(*dve_did.event("conv", part, h))
                else:
                    link(last)

            def token_out(part, h):
                if part == "v":
                    dve.wait_ge(*pe_did.after("conv_back", part, h))
                    for t in range(NT):
                        last = dve.tensor_tensor(v_tok[:, t, quad(h)], aux[:, 2 + t].rearrange("p (i c) -> p i c", c=P),
                                                 over_cols(beta[:, t * HEADS + h * QUAD:t * HEADS + (h + 1) * QUAD]),
                                                 ALU.mult)
                    last.then_inc(*dve_did.event("token_out", part, h))
                    return
                dve.wait_ge(*act_did.after("sq", part, h))
                if (part, h) != ("q", 0):
                    dve.wait_ge(*pool_did.after("rnorm", *before_qk(part, h)))
                dve.tensor_reduce(tiles(ssq, QUAD), sq[:], AXX, ALU.add).then_inc(*dve_did.event("ssq", part, h))
                dve.wait_ge(*pool_did.after("rnorm", part, h))
                if part == "q" and h:
                    dve.wait_ge(*pe_did.after("qk_flip", "q", 0))
                for t in range(NT):
                    to = q_tok[:, t] if part == "q" else k_tok[:, t, quad(h)]
                    last = dve.tensor_tensor(to, aux[:, 2 + t].rearrange("p (i c) -> p i c", c=P),
                                             over_cols(rnorm[:, t * QUAD:(t + 1) * QUAD]), ALU.mult)
                last.then_inc(*dve_did.event("token_out", part, h))

            def gu(h, t):
                o = t * HEADS + h * QUAD
                if (h, t) == (0, 0):
                    dve.wait_ge(*pe_did.after("conv_back", "v", 1))
                    dve.wait_ge(*pe_did.after("qk_flip", "q", 1))
                    dve.wait_ge(*act_did.after("silu", "v", 1))
                dve.tensor_tensor(chain[t]["wide"][:], over_heads(upto[:]), over_cols(g[:, o:o + QUAD]),
                                  ALU.mult).then_inc(*dve_did.event("gu", h, t))

            def tri(h, t):
                c = chain[t]
                dve.wait_ge(*act_did.after("decay", h, t))
                dve.tensor_tensor(c["low_m"][:], c["inv"][:], over_heads(levels[:, 0]), ALU.mult)
                link(dve.tensor_tensor(c["low_t"][:], c["inv"][:], over_heads(upto[:]), ALU.mult))
                dve.tensor_tensor(attn_t[:, quad(h), t], aux[:, 2].rearrange("p (i c) -> p i c", c=P), c["low_t"][:],
                                  ALU.mult)
                for i in range(QUAD):
                    o = t * HEADS + h * QUAD + i
                    last = dve.scalar_tensor_tensor(c["wide"][:, i], aux[:, 1, i * P:(i + 1) * P], nbeta[:, o:o + 1],
                                                    c["low_m"][:, i], ALU.mult, ALU.mult)
                last.then_inc(*dve_did.event("tri", h, t))

            def masked(h, t, n):
                c = chain[t]
                return dve.tensor_tensor(c["low_m"][:], c["low_t"][:], over_heads(levels[:, n + 1]), ALU.mult)

            def invert_first(h, t):
                c = chain[t]
                inv_q = inv_t[:, quad(h), t]
                dve.wait_ge(*act_did.after("tri_flip", h, t))
                dve.tensor_tensor(c["inv"][:], c["wide"][:], over_heads(levels[:, 1]), ALU.mult)
                link(dve.tensor_tensor(inv_q, c["low_t"][:], over_heads(levels[:, 2]), ALU.mult))
                dve.tensor_tensor(c["inv"][:], c["inv"][:], over_heads(ident[:]), ALU.add)
                dve.tensor_tensor(inv_q, inv_q, over_heads(ident[:]), ALU.add)
                masked(h, t, 2).then_inc(*dve_did.event("masked", h, t, 2))

            def invert_y(h, t, n):
                dve.wait_ge(*pe_did.after("invert_y", h, t, n))
                dve.tensor_tensor(chain[t]["wide"][:], aux[:, 0].rearrange("p (i c) -> p i c", c=P),
                                  over_heads(ident[:]), ALU.add).then_inc(*dve_did.event("invert_y", h, t, n))
                if n < LEVELS:
                    masked(h, t, n + 1).then_inc(*dve_did.event("masked", h, t, n + 1))

            def invert_t(h, t, n):
                dve.wait_ge(*pe_did.after("invert_t", h, t, n))
                dve.tensor_copy(inv_t[:, quad(h), t], aux[:, 2].rearrange("p (i c) -> p i c", c=P)).then_inc(
                    *dve_did.event("invert_t", h, t, n))

            def delta(h, n):
                q4 = quad(h)
                o = HEADS + h * QUAD
                if n == 0:
                    dve.wait_ge(*act_did.after("eg"))
                    dve.tensor_tensor(k_tok[:, 0, q4], k_tok[:, 0, q4], over_cols(tail[:, q4]), ALU.mult).then_inc(
                        *dve_did.event("delta", h, 0))
                if n == 1:
                    dve.wait_ge(*pe_did.after("delta", h, 1))
                    dve.tensor_copy(k_tok[:, 0, q4], aux[:, 2].rearrange("p (i c) -> p i c", c=P)).then_inc(
                        *dve_did.event("delta", h, 1))
                if n == 2:
                    dve.wait_ge(*pe_did.after("delta", h, 2))
                    link(dve.tensor_tensor(delta_r[:], aux[:, 3].rearrange("p (i c) -> p i c", c=P),
                                           over_cols(beg[:, o:o + QUAD]), ALU.mult))
                    dve.tensor_tensor(delta_q[:], aux[:, 0].rearrange("p (i c) -> p i c", c=P),
                                      over_cols(eg[:, o:o + QUAD]), ALU.mult)
                    dve.tensor_tensor(delta_r[:], v_tok[:, 1, q4], delta_r[:], ALU.subtract).then_inc(
                        *dve_did.event("delta", h, 2))
                if n == 4:
                    dve.wait_ge(*pe_did.after("delta", h, 4))
                    dve.tensor_tensor(k_tok[:, 1, q4], aux[:, 2].rearrange("p (i c) -> p i c", c=P), delta_q[:],
                                      ALU.add).then_inc(*dve_did.event("delta", h, 4))

            def delta_norm(h):
                dve.wait_ge(*act_did.after("delta_sq", h))
                dve.tensor_reduce(tiles(ssq, QUAD), delta_sq[:], AXX, ALU.add).then_inc(*dve_did.event("delta_ssq", h))
                dve.wait_ge(*pool_did.after("delta_rnorm", h))
                for t in range(NT):
                    o = k_tok[:, t, quad(h)]
                    last = dve.tensor_tensor(o, o, over_cols(rnorm[:, t * QUAD:(t + 1) * QUAD]), ALU.mult)
                link(last)
                dve.wait_ge(*act_did.after("z", h))
                for t in range(NT):
                    o = k_tok[:, t, quad(h)]
                    last = dve.tensor_tensor(o, o, zs[:, t, quad(h)], ALU.mult)
                last.then_inc(*flip_source.event("oa", h))

            def z_out(h):
                dve.wait_ge(*act_did.after("z", h))
                for t in range(NT):
                    z = zs[:, t, quad(h)]
                    last = dve.tensor_tensor(z, z, over_heads(gnorm_w[:]), ALU.mult)
                link(last)

            def att(kind, h, t, n):
                k = (t + 1) * P
                s = att_s[:, 0:QUAD * k].rearrange("p (i c) -> p i c", c=k)
                if n == 1:
                    dve.wait_ge(*pe_did.after("att", kind, h, t, 0))
                    if att_before[(kind, h, t)]:
                        dve.wait_ge(*pe_did.after(*att_before[(kind, h, t)][:-1], 3))
                    ps = aux[:, 0:2].rearrange("p b c -> p (b c)")[:, 0:QUAD * k].rearrange("p (i c) -> p i c", c=k)
                    mask = masks[:, 1 if kind == "b" else 0, SEQ - k:SEQ]
                    link(dve.tensor_tensor(s, ps, over_heads(mask), ALU.add))
                    link(dve.tensor_reduce(mx[:, 0:QUAD], s, AXX, ALU.max))
                    if kind == "b":
                        sinks = sink_row[:, quad(h)]
                        link(dve.scalar_tensor_tensor(mx[:, 0:QUAD], mx[:, 0:QUAD], SCALE_B, sinks, ALU.mult, ALU.max))
                        dve.tensor_tensor(esink[:, 0:QUAD], sinks, mx[:, 0:QUAD], ALU.subtract)
                    dve.tensor_scalar(nmx[:, 0:QUAD], mx[:, 0:QUAD], -1.0 if kind == "b" else -SCALE, None,
                                      ALU.mult).then_inc(*dve_did.event("max", kind, h, t))
                if n == 4:
                    dve.wait_ge(*act_did.after("exp", kind, h, t))
                    d, r = den[:, 0:QUAD], rden[:, 0:QUAD]
                    if kind == "b":
                        link(dve.tensor_tensor(d, d, esink[:, 0:QUAD], ALU.add))
                    link(dve.reciprocal(r, d))
                    if kind in "sw":
                        dve.wait_ge(*act_did.after("head_gates"))
                        o = t * 24 + h * QUAD * 3
                        gate = head_gate[:, o:o + QUAD * 3].rearrange("p (i b) -> p i b", b=3)[:, :, 1 if kind == "s" else 2]
                        link(dve.tensor_tensor(r, r, gate, ALU.mult))
                    dve.wait_ge(*pe_did.after("att", kind, h, t, 4))
                    w = 64 if kind == "b" else P
                    o = aux[:, 2, 0:QUAD * w].rearrange("p (i c) -> p i c", c=w)
                    if kind == "m":
                        to = att_o[:].rearrange("p (i c) -> p i c", c=P)
                        if att_before[(kind, h, t)]:
                            dve.wait_ge(*flip_filled.after("ob", *att_before[(kind, h, t)][2:4]))
                        link(dve.tensor_tensor(to, o, over_cols(r), ALU.mult))
                        dve.wait_ge(*act_did.after("mz", h))
                        dve.tensor_tensor(to, to, mzs[:, t, quad(h)], ALU.mult).then_inc(*flip_source.event("ob", h, t))
                        return
                    to = oa_tok if kind in "sw" else ob_tok
                    to = to[:, t, h * QUAD * w:(h + 1) * QUAD * w].rearrange("p (i c) -> p i c", c=w)
                    if kind == "w":
                        for i in range(QUAD):
                            last = dve.scalar_tensor_tensor(to[:, i], o[:, i], r[:, i:i + 1], to[:, i], ALU.mult, ALU.add)
                    else:
                        last = dve.tensor_tensor(to, o, over_cols(r, w), ALU.mult)
                    last.then_inc(*dve_did.event("att", kind, h, t))

            def branch(ab, c):
                a = acc_of(END[("u" + ab, c)])
                dve.wait_ge(*act_did.after("gate_out", ab, c))
                dve.wait_ge(*used.after(END[("u" + ab, c)]))
                to = sg[ab][c % 2]
                last = dve.tensor_tensor(to[:], to[:], a, ALU.mult)
                if ab == "a":
                    last.then_inc(*dve_did.event("branch", ab, c))
                    return
                last.then_inc(*dve_did.event("branch_mult", c))
                dve.wait_ge(*dve_did.after("branch_mult", c))
                if c:
                    dve.wait_ge(*flip_filled.after("merged", c - 1, 1))
                dve.tensor_tensor(merged[:], sg["a"][c % 2][:], to[:], ALU.add).then_inc(*flip_source.event("merged", c))
                dve.wait_ge(*flip_source.after("merged", c))
                dve.tensor_copy(tot[:, 0:1], tot[:, 0:1]).then_inc(*dve_did.event("branch", ab, c))

            def y_out(c):
                a = acc_of(END[("wo", c)])
                dve.wait_ge(*x_again.after(2))
                dve.wait_ge(*act_did.after("y_out", c))
                cols = slice(c * COLS, (c + 1) * COLS)
                dve.tensor_tensor(y1[:, :, cols], a, over_heads(post_row[:, cols], NT), ALU.mult).then_inc(
                    *dve_did.event("y_out", c))

            def residual():
                dve.wait_ge(*act_did.after("y_out", 3))
                dve.tensor_reduce(tot, tiles(sumy, 4), AXX, ALU.add).then_inc(*dve_did.event("sumy"))
                dve.wait_ge(*pool_did.after("ry"))
                dve.wait_ge(*dve_did.after("y_out", 3))
                for t in range(NT):
                    dve.scalar_tensor_tensor(x2[:, t], y1[:, t], ry[:, t:t + 1], x2[:, t], ALU.mult, ALU.add).then_inc(
                        *dve_did.event("x2", t))
                    dve.wait_ge(*dve_did.after("x2", t))
                    for n in range(4):
                        cols = slice(n * COLS, (n + 1) * COLS)
                        dve.tensor_tensor(y1[:, t, cols], x2[:, t, cols], row2[:, cols], ALU.mult).then_inc(
                            *flip_source.event("h2", n, t))
                dve.wait_ge(*act_did.after("sq2", 1))
                dve.tensor_reduce(tot, tiles(sum2, 4), AXX, ALU.add).then_inc(*dve_did.event("sum2"))
                dve.wait_ge(*act_did.after("ag_hi"))
                dve.tensor_tensor(ba_lo[:], ba_raw[:], ba_hi[:].bitcast(F32), ALU.subtract).then_inc(*dve_did.event("ag_lo"))

            def head_gates():
                dve.wait_ge(*pool_did.after("r2"))
                for t in range(NT):
                    for table in (rope_a, rope_b):
                        last = dve.tensor_scalar(table[:, :, t], table[:, :, t], r2[:, t:t + 1], None, ALU.mult)
                link(last)

            def rope(*name):
                a = acc_of(END[name])
                dve.wait_ge(*used.after(END[name]))
                table, d, heads = {"qa": (rope_a, 128, 4), "qb": (rope_b, 64, 8), "kvb": (rope_b, 64, 2)}.get(
                    name[0], (rope_a, 128, 2))
                w, d2 = heads * d, d // 2
                for t in range(NT):
                    x = a[:, t, 0:w].rearrange("p (i c) -> p i c", c=d)
                    ra, rb = (rot[i][:, t, 0:w].rearrange("p (i c) -> p i c", c=d) for i in range(2))
                    dve.tensor_tensor(ra, x, over_heads(table[:, 0, t], heads), ALU.mult)
                    dve.tensor_tensor(rb[:, :, 0:d2], x[:, :, d2:d], over_heads(table[:, 1, t, 0:d2], heads), ALU.mult)
                    last = dve.tensor_tensor(rb[:, :, d2:d], x[:, :, 0:d2], over_heads(table[:, 1, t, d2:d], heads),
                                             ALU.mult)
                last.then_inc(*dve_did.event("rope_read", *name))
                dve.wait_ge(*dve_did.after("rope_read", *name))
                if rope_before[name]:
                    dve.wait_ge(*pe_did.after("rope_flip", *rope_before[name]))
                for t in range(NT):
                    if name[0] == "kvb":
                        ra, rb = (rot[i][:, t, 0:w].rearrange("p (i c) -> p i c", c=d) for i in range(2))
                        rc = rot[2][:, t, 0:2 * w].rearrange("p (i r c) -> p i r c", r=2, c=d)
                        for r in range(2):
                            last = dve.tensor_tensor(rc[:, :, r], ra, rb, ALU.add)
                    else:
                        last = dve.tensor_tensor(rot[2][:, t, 0:w], rot[0][:, t, 0:w], rot[1][:, t, 0:w], ALU.add)
                last.then_inc(*dve_did.event("rope", *name))

            def blocks(part):
                dve.wait_ge(*act_did.after("rope_flip", "kcv"))
                s = kt2["kc" if part == "k" else "vc"][:].rearrange("p i (c l) -> p l i c", l=16)
                for n in range(2):
                    for i in range(2):
                        last = dve.tensor_tensor(blk[part][:, n * 16:(n + 1) * 16, i], s[:, :, i, n:n + N_CMP],
                                                 over_cols(pos[part][:, n * 16:(n + 1) * 16], N_CMP), ALU.add)
                last.then_inc(*dve_did.event("blocks", part))

            def catt(t, n):
                if n == 1:
                    dve.wait_ge(*pe_did.after("catt", t, 0))
                    s = aux[:, 0, 0:HEADS * N_CMP].rearrange("p (i c) -> p i c", c=N_CMP)
                    if t:
                        dve.wait_ge(*pe_did.after("catt", 0, 3))
                    link(dve.scalar_tensor_tensor(cs[:], s, SCALE, over_heads(cmask[:, 0, t], HEADS), ALU.mult, ALU.add))
                    link(dve.tensor_reduce(cmx, cs[:], AXX, ALU.max))
                    dve.tensor_tensor(cs[:], cs[:], over_cols(cmx, N_CMP), ALU.subtract).then_inc(
                        *dve_did.event("cmax", t))
                if n == 2:
                    dve.wait_ge(*act_did.after("cexp", t))
                    dve.tensor_tensor(cs[:], cs[:], over_heads(cmask[:, 1, t], HEADS), ALU.mult).then_inc(
                        *dve_did.event("cprob", t))
                    dve.wait_ge(*dve_did.after("cprob", t))
                    link(dve.tensor_reduce(cden, cs[:], AXX, ALU.add))
                    link(dve.tensor_scalar(cden, cden, TINY, None, ALU.max))
                    link(dve.reciprocal(crden, cden))
                    gate = head_gate[:, t * 24:(t + 1) * 24].rearrange("p (i b) -> p i b", b=3)[:, :, 0]
                    link(dve.tensor_tensor(crden, crden, gate, ALU.mult))
                if n == 4:
                    dve.wait_ge(*pe_did.after("catt", t, 4))
                    o = aux[:, 0:2].rearrange("p b (i c) -> p (b i) c", c=P)
                    for i in range(HEADS):
                        to = oa_tok[:, t, i * P:(i + 1) * P]
                        last = dve.scalar_tensor_tensor(to, o[:, i], crden[:, i:i + 1], to, ALU.mult, ALU.add)
                    last.then_inc(*dve_did.event("catt", t))

            def y_gate(n):
                dve.wait_ge(*act_did.after("z2", n))
                tok = (oa_tok, ob_tok)[n // 2][:, :, n % 2 * COLS:(n % 2 + 1) * COLS]
                dve.tensor_tensor(tok, tok, z2[n % 2][:], ALU.mult).then_inc(*flip_source.event("y", n))
                dve.wait_ge(*flip_source.after("y", n))
                dve.tensor_copy(tot[:, 0:1], tot[:, 0:1]).then_inc(*dve_did.event("y_gate", n))

            def y2_out(c):
                a = acc_of(END[("w2", c)])
                dve.wait_ge(*x3_ready.after(0))
                dve.wait_ge(*last_ready.after(0))
                dve.wait_ge(*used.after(END[("w2", c)]))
                cols = slice(c * COLS, (c + 1) * COLS)
                dve.tensor_tensor(x3[:, :, cols], x3[:, :, cols], a, ALU.add).then_inc(*dve_did.event("x3", c))
                dve.wait_ge(*dve_did.after("x3", c))
                dve.tensor_tensor(y3[:, :, cols], x3[:, :, cols], over_heads(last_row[:, cols], NT),
                                  ALU.mult).then_inc(*dve_did.event("y3", c))

            def finish():
                dve.wait_ge(*act_did.after("sq3", 3))
                dve.tensor_reduce(tot, tiles(sum3, 4), AXX, ALU.add).then_inc(*dve_did.event("sum3"))
                dve.wait_ge(*pool_did.after("r3"))
                dve.tensor_scalar(y3[:, 1], y3[:, 1], r3[:, 1:2], None, ALU.mult).then_inc(*dve_did.event("finish"))

            for t in range(NT):
                dve.wait_ge(*x_ready[t].after(0))
                if t == 0:
                    dve.wait_ge(*row_ready.after(0))
                if t == NT - 1:
                    for m in range(NT):
                        dve.wait_ge(*act_did.after("sq1", m))
                    dve.tensor_reduce(tot, tiles(sum1, 4), AXX, ALU.add).then_inc(*dve_did.event("sum1"))
                dve.wait_ge(*act_did.after("sq1", t))
                for n in range(4):
                    cols = slice(n * COLS, (n + 1) * COLS)
                    dve.tensor_tensor(x_in[:, t, cols], x_in[:, t, cols], row1[:, cols], ALU.mult).then_inc(
                        *flip_source.event("h1", n, t))
            dve.wait_ge(*const_ready.after(6))
            dve.wait_ge(*pe_did.after("conv_w"))
            dve.tensor_copy(conv_w[:].rearrange("p j i -> p (j i)"), aux[:, 0, 0:CONV * 24])
            dve.wait_ge(*pe_did.after("pos"))
            dve.tensor_copy(pos["k"][:], aux[:, 1, 0:CMP_L])
            dve.tensor_copy(pos["v"][:], aux[:, 1, CMP_L:2 * CMP_L]).then_inc(*dve_did.event("pos"))
            for n in range(4):
                for t in range(NT):
                    flip("h1", n, t)
            split(0)
            split(1)
            dve.wait_ge(*act_did.after("ba_hi"))
            dve.tensor_tensor(ba_lo[:, :, 0:16], ba_raw[:, :, 0:16], ba_hi[:, :, 0:16].bitcast(F32),
                              ALU.subtract).then_inc(*dve_did.event("ba_lo"))
            dve.wait_ge(*block2_rows.after(8))
            steps = {"ba": ba_, "gates": gates, "gcum": gcum_, "conv": conv, "token_out": token_out, "gu": gu,
                     "tri": tri, "invert_first": invert_first, "invert_y": invert_y, "invert_t": invert_t,
                     "delta": delta, "delta_norm": delta_norm, "z_out": z_out, "att": att, "flip": flip,
                     "branch": branch, "y_out": y_out, "residual": residual, "head_gates": head_gates, "rope": rope,
                     "blocks": blocks, "catt": catt, "y_gate": y_gate, "y2_out": y2_out, "finish": finish}
            for tick in range(TICKS + LAST):
                if tick + AHEAD < TICKS:
                    split(tick + AHEAD)
                for name, *args in PLAN[tick]:
                    if name in steps:
                        steps[name](*args)

        @block.tensor
        def _(pe):
            held = {b: () for b in range(AUX)}

            def take(b, *readers):
                for s, *key in held[b]:
                    pe.wait_ge(*s.after(*key))
                held[b] = readers

            def turn(to, source):
                return pe.transpose(to, source, ident[0:source.shape[0], 0:source.shape[0]])

            acc_readers = {}
            for c in range(4):
                acc_readers[("ga", c)] = (act_did, "gate_out", "a", c)
                acc_readers[("gb", c)] = (act_did, "gate_out", "b", c)
                acc_readers[("ua", c)] = (dve_did, "branch", "a", c)
                acc_readers[("ub", c)] = (dve_did, "branch_mult", c)
                acc_readers[("wo", c)] = ((act_did, "y_out", c), (dve_did, "y_out", c))
                acc_readers[("w2", c)] = (dve_did, "x3", c)
            for h in range(2):
                for part in "qkv":
                    acc_readers[("conv", part, h)] = (act_did, "raw_out", part, h)
                    acc_readers[("moba", part, h)] = (act_did, "m_raw", part, h) if part != "v" else (act_did, "m_v", h)
                acc_readers[("z", h)] = (act_did, "z", h)
                acc_readers[("mz", h)] = (act_did, "mz", h)
                acc_readers[("za", h)] = (act_did, "z2", h)
                acc_readers[("zb", h)] = (act_did, "z2", 2 + h)
                for name in ("qa", "qb"):
                    acc_readers[(name, h)] = (dve_did, "rope", name, h)
            for name in ("kcv", "ksv", "kwv", "kvb"):
                acc_readers[(name,)] = ((dve_did, "rope", name), (act_did, "values", name))
            for part in "kv":
                acc_readers[("cmp", part)] = (act_did, "hs", part)

            def wait_readers(name):
                r = acc_readers[name]
                for s, *key in (r if isinstance(r[0], tuple) else (r,)):
                    pe.wait_ge(*s.after(*key))

            filled = set()

            def products(no):
                g_, k0, n, first, last = PIECES[no]
                group = GROUPS[g_]
                if first and g_ >= 2:
                    wait_readers(GROUPS[g_ - 2].name)
                to = acc[:, g_ % 2]
                if group.kind == "cmp":
                    w = piece_view(raw_w[no % RAW_SLOTS], no)
                    part = group.name[1]
                    pe.wait_ge(*raw_ready[no % RAW_SLOTS].after(no))
                    pe.wait_ge(*dve_did.after("blocks", part))
                    for k in range(n):
                        for m in range(2):
                            i = pe.matmul(to[:, m, 0:2 * N_CMP], w[:, k, m * P:(m + 1) * P],
                                          blk[part][:, k0 + k].rearrange("p i c -> p (i c)"),
                                          start=first and k == 0, stop=last and k == n - 1)
                    i.then_inc(*used.event(no))
                    return
                slot = SPLIT_NO[no] % SPLIT_SLOTS
                hi = piece_view(hi_w[slot], no)
                lo = piece_view(lo_w[slot], no)
                x_hi, x_lo = LHS[group.lhs]
                for k in range(k0, k0 + n):
                    if (group.lhs, k // 4) not in filled:
                        filled.add((group.lhs, k // 4))
                        for t in range(NT):
                            pe.wait_ge(*flip_lo.after(group.lhs, k // 4, t))
                pe.wait_ge(*lo_ready.after(no))
                for t in range(NT):
                    for k in range(n):
                        at = (slice(None), k0 + k, slice(t * P, (t + 1) * P))
                        for m, (x, w) in enumerate(((x_hi, hi), (x_hi, lo), (x_lo, hi))):
                            i = pe.matmul(to[:, t, 0:group.cols], x[at], w[:, k], start=first and k == 0 and m == 0,
                                          stop=last and k == n - 1 and m == 2)
                i.then_inc(*used.event(no))

            def flip(name, n, t):
                b = flip_bank(name, n, t)
                take(b, (flip_hi, name, n, t), (flip_lo, name, n, t))
                source = {"h1": (n, t), "h2": (n, t), "ob": (n, t)}.get(name, (n,))
                pe.wait_ge(*flip_source.after(name, *source))
                if name in ("h1", "h2"):
                    s = (x_in if name == "h1" else y1)[:, t, n * COLS:(n + 1) * COLS]
                elif name == "oa":
                    s = k_tok[:, t, quad(n)].rearrange("p i c -> p (i c)")
                elif name == "ob":
                    s = att_o[:]
                elif name == "merged":
                    s = merged[:, t]
                else:
                    s = (oa_tok, ob_tok)[n // 2][:, t, n % 2 * COLS:(n % 2 + 1) * COLS]
                for i in range(QUAD):
                    last = turn(aux[:, b, i * P:(i + 1) * P], s[:, i * P:(i + 1) * P])
                last.then_inc(*flip_filled.event(name, n, t))

            def few_columns(n, key, *waits):
                take(0, *waits)
                for t in range(NT):
                    for k in range(KT):
                        at = (slice(None), k, slice(t * P, (t + 1) * P))
                        for m, (x, w) in enumerate(((h_hi, ba_hi), (h_hi, ba_lo), (h_lo, ba_hi))):
                            i = pe.matmul(aux[:, 0, t * n:(t + 1) * n], x[at], w[:, k, 0:n],
                                          start=k == 0 and m == 0, stop=k == KT - 1 and m == 2)
                i.then_inc(*pe_did.event(key))

            def ba_():
                pe.wait_ge(*dve_did.after("ba_lo"))
                few_columns(16, "ba", (dve_did, "ba"))

            def ag():
                pe.wait_ge(*dve_did.after("ag_lo"))
                few_columns(24, "ag", (act_did, "head_gates"))

            def gcum_():
                take(1, (dve_did, "gcum"))
                pe.wait_ge(*dve_did.after("g"))
                pe.wait_ge(*pool_did.after("ones"))
                pe.matmul(aux[:, 1, 0:NT * HEADS], upto[:], g, start=True, stop=True)
                pe.matmul(aux[:, 1, NT * HEADS:NT * HEADS + HEADS], ones[:], g[:, 0:HEADS], start=True,
                          stop=True).then_inc(*pe_did.event("gcum"))

            def raw_flip(part, h):
                take(0, (dve_did, "conv", part, h))
                take(1, (dve_did, "conv", part, h))
                pe.wait_ge(*act_did.after("raw_out", part, h))
                for i in range(QUAD):
                    for t in range(NT):
                        o = i % 2 * SEQ + t * P
                        last = turn(aux[:, i // 2, o:o + P], raw[:, t, i * P:(i + 1) * P])
                last.then_inc(*pe_did.event("raw_flip", part, h))

            def conv_back(part, h):
                for b in (2, 3):
                    take(b, (dve_did, "token_out", part, h))
                pe.wait_ge(*act_did.after("silu", part, h))
                for t in range(NT):
                    for i in range(QUAD):
                        last = turn(aux[:, 2 + t, i * P:(i + 1) * P], sil[:, i, t * P:(t + 1) * P])
                last.then_inc(*pe_did.event("conv_back", part, h))

            def qk_flip(part, h):
                for b in (2, 3):
                    take(b, (act_did, "qk_out", part, h))
                pe.wait_ge(*dve_did.after("token_out", part, h))
                for i in range(QUAD):
                    for t in range(NT):
                        s = q_tok[:, t, i] if part == "q" else k_tok[:, t, h * QUAD + i]
                        o = i % 2 * SEQ + t * P
                        last = turn(aux[:, 2 + i // 2, o:o + P], s)
                last.then_inc(*pe_did.event("qk_flip", part, h))

            def gram(h, t):
                take(0, (act_did, "decay", h, t))
                take(1, (dve_did, "tri", h, t))
                take(2, (dve_did, "tri", h, t))
                pe.wait_ge(*dve_did.after("gu", h, t))
                pe.wait_ge(*act_did.after("qk_out", "k", h))
                pe.matmul(aux[:, 0], ones[:], chain[t]["wide"][:].rearrange("p i c -> p (i c)"), start=True, stop=True)
                for b, x in ((1, k_t), (2, q_t)):
                    for i in range(QUAD):
                        at = (slice(None), h * QUAD + i, slice(t * P, (t + 1) * P))
                        last = pe.matmul(aux[:, b, i * P:(i + 1) * P], k_t[at], x[at], start=True, stop=True)
                last.then_inc(*pe_did.event("gram", h, t))

            def tri_flip(h, t):
                take(3, (act_did, "tri_flip", h, t))
                pe.wait_ge(*dve_did.after("tri", h, t))
                for i in range(QUAD):
                    last = turn(aux[:, 3, i * P:(i + 1) * P], chain[t]["wide"][:, i])
                last.then_inc(*pe_did.event("tri_flip", h, t))

            def invert_y(h, t, n):
                take(0, (dve_did, "invert_y", h, t, n))
                pe.wait_ge(*dve_did.after("masked", h, t, n))
                if n > 2:
                    pe.wait_ge(*act_did.after("invert_t", h, t, n - 1))
                for i in range(QUAD):
                    last = pe.matmul(aux[:, 0, i * P:(i + 1) * P], chain[t]["low_m"][:, i], chain[t]["inv"][:, i],
                                     start=True, stop=True)
                last.then_inc(*pe_did.event("invert_y", h, t, n))

            def invert_t(h, t, n):
                if n < LEVELS:
                    take(1, (act_did, "invert_t", h, t, n))
                take(2, (dve_did, "invert_t", h, t, n))
                pe.wait_ge(*dve_did.after("invert_y", h, t, n))
                if n > 2:
                    pe.wait_ge(*dve_did.after("invert_t", h, t, n - 1))
                for i in range(QUAD):
                    wide, inv = chain[t]["wide"][:, i], inv_t[:, h * QUAD + i, t]
                    if n < LEVELS:
                        pe.matmul(aux[:, 1, i * P:(i + 1) * P], inv, wide, start=True, stop=True)
                    last = pe.matmul(aux[:, 2, i * P:(i + 1) * P], wide, inv, start=True, stop=True)
                last.then_inc(*pe_did.event("invert_t", h, t, n))

            def delta(h, n):
                readers = {0: [(0, act_did, 0)], 1: [(1, act_did, 1), (2, dve_did, 1)],
                           2: [(3, dve_did, 2), (0, dve_did, 2)], 3: [(1, act_did, 3)], 4: [(2, dve_did, 4)]}
                for b, s, m in readers[n]:
                    take(b, (s, "delta", h, m))
                if n == 0:
                    for t in range(NT):
                        pe.wait_ge(*dve_did.after("invert_t", h, t, LEVELS))
                if n == 1:
                    pe.wait_ge(*dve_did.after("delta", h, 0))
                if n in (1, 2, 4):
                    pe.wait_ge(*act_did.after("delta", h, n - 1))
                if n == 3:
                    pe.wait_ge(*dve_did.after("delta", h, 2))
                for i in range(QUAD):
                    hd, o = h * QUAD + i, slice(i * P, (i + 1) * P)
                    if n == 0:
                        last = pe.matmul(aux[:, 0, o], inv_t[:, hd, 0], v_tok[:, 0, hd], start=True, stop=True)
                    if n == 1:
                        pe.matmul(aux[:, 1, o], k_tok[:, 0, hd], delta_u[:, i], start=True, stop=True)
                        last = pe.matmul(aux[:, 2, o], attn_t[:, hd, 0], delta_u[:, i], start=True, stop=True)
                    if n == 2:
                        pe.matmul(aux[:, 3, o], k_t[:, hd, P:SEQ], delta_s[:, i], start=True, stop=True)
                        last = pe.matmul(aux[:, 0, o], q_t[:, hd, P:SEQ], delta_s[:, i], start=True, stop=True)
                    if n == 3:
                        last = pe.matmul(aux[:, 1, o], inv_t[:, hd, 1], delta_r[:, i], start=True, stop=True)
                    if n == 4:
                        last = pe.matmul(aux[:, 2, o], attn_t[:, hd, 1], delta_u[:, i], start=True, stop=True)
                last.then_inc(*pe_did.event("delta", h, n))

            def m_flip(part, h, t):
                take(3, (act_did, "m_flip", part, h, t))
                pe.wait_ge(*act_did.after("m_raw", part, h))
                for i in range(QUAD):
                    last = turn(aux[:, 3, i * P:(i + 1) * P], m_raw[:, t, i * P:(i + 1) * P])
                last.then_inc(*pe_did.event("m_flip", part, h, t))

            def att(kind, h, t, n):
                k = (t + 1) * P
                tok = slice(t * P, (t + 1) * P)
                if n == 0:
                    for b in range(2):
                        take(b, (dve_did, "max", kind, h, t))
                    s = aux[:, 0:2].rearrange("p b c -> p (b c)")
                    if kind == "m":
                        pe.wait_ge(*act_did.after("m_flip", "k", h, 1))
                    elif kind == "b":
                        pe.wait_ge(*act_did.after("rope_flip", "kvb"))
                        pe.wait_ge(*act_did.after("rope_flip", "qb", h // 2))
                    else:
                        pe.wait_ge(*act_did.after("rope_flip", "qa", h))
                        pe.wait_ge(*act_did.after("rope_flip", "k" + kind + "v"))
                    if kind == "b":
                        for i in range(2):
                            last = pe.matmul(s[:, 2 * i * k:2 * (i + 1) * k].rearrange("p (i c) -> p i c", c=k),
                                             qb_t[:, 2 * h + i, tok], kz[:, h // 2, :, 0:k], start=True, stop=True)
                    else:
                        for i in range(QUAD):
                            hd = h * QUAD + i
                            q = (m_t["q"] if kind == "m" else qa_t)[:, hd, tok]
                            keys = m_t["k"][:, hd, 0:k] if kind == "m" else kt2["k" + kind][:, h, 0:k]
                            last = pe.matmul(s[:, i * k:(i + 1) * k], q, keys, start=True, stop=True)
                elif n == 3:
                    for b in range(t + 1):
                        take(2 + b, (act_did, "att_p", kind, h, t))
                    pe.wait_ge(*act_did.after("exp", kind, h, t))
                    for b in range(t + 1):
                        for i in range(QUAD):
                            o = i * k + b * P
                            last = turn(aux[:, 2 + b, i * P:(i + 1) * P], att_s[:, o:o + P])
                elif n == 4:
                    take(2, (flip_source, "ob", h, t) if kind == "m" else (dve_did, "att", kind, h, t))
                    if kind == "m":
                        pe.wait_ge(*act_did.after("m_v", h))
                    else:
                        pe.wait_ge(*act_did.after("values", {"s": "ksv", "w": "kwv", "b": "kvb"}[kind]))
                    w = 64 if kind == "b" else P
                    for i in range(QUAD):
                        for b in range(t + 1):
                            if kind == "m":
                                v = m_v[:, b, h * QUAD + i]
                            elif kind == "b":
                                v = vb[:, b, h // 2]
                            else:
                                v = v2["v" + kind][:, b, h]
                            last = pe.matmul(aux[:, 2, i * w:(i + 1) * w], att_p[:, b, i * P:(i + 1) * P], v,
                                             start=b == 0, stop=b == t)
                else:
                    return
                last.then_inc(*pe_did.event("att", kind, h, t, n))

            def rope_flip(*name):
                for b in (2, 3):
                    take(b, (act_did, "rope_flip", *name))
                pe.wait_ge(*dve_did.after("rope", *name))
                if name[0] == "kcv":
                    pe.wait_ge(*act_did.after("values", "kcv"))
                for i in range(2 if name[0] in ("ksv", "kwv", "kvb") else QUAD):
                    for t in range(NT):
                        o = i % 2 * SEQ + t * P
                        last = turn(aux[:, 2 + i // 2, o:o + P], rot[2][:, t, i * P:(i + 1) * P])
                last.then_inc(*pe_did.event("rope_flip", *name))

            def cmp_out(part):
                take(0, (act_did, "cmp_out", part))
                pe.wait_ge(*act_did.after("hs", part))
                for i in range(1 if part == "k" else 2):
                    for m in range(2):
                        if part == "k":
                            last = pe.matmul(aux[:, 0, 0:2 * N_CMP], w2s["k"][:, m], hs["k"][:, m], start=m == 0,
                                             stop=m == 1)
                        else:
                            last = pe.matmul(aux[0:N_CMP, 0, i * P:(i + 1) * P],
                                             hs["v"][:, m, i * N_CMP:(i + 1) * N_CMP], w2s["v"][:, m], start=m == 0,
                                             stop=m == 1)
                last.then_inc(*pe_did.event("cmp_out", part))

            def catt(t, n):
                if n == 0:
                    take(0, (dve_did, "cmax", t))
                    pe.wait_ge(*act_did.after("cmp_out", "v"))
                    for i in range(HEADS):
                        last = pe.matmul(aux[:, 0, i * N_CMP:(i + 1) * N_CMP], qa_t[:, i, t * P:(t + 1) * P],
                                         ck_t[:, i // QUAD * N_CMP:(i // QUAD + 1) * N_CMP], start=True, stop=True)
                elif n == 3:
                    for b in (2, 3):
                        take(b, (act_did, "cp", t))
                    pe.wait_ge(*dve_did.after("cprob", t))
                    for i in range(HEADS):
                        last = turn(aux[0:N_CMP, 2 + i // QUAD, i % QUAD * P:(i % QUAD + 1) * P], cs[:, i])
                elif n == 4:
                    for b in (0, 1):
                        take(b, (dve_did, "catt", t))
                    pe.wait_ge(*act_did.after("cp", t))
                    for i in range(HEADS):
                        last = pe.matmul(aux[:, i // QUAD, i % QUAD * P:(i % QUAD + 1) * P],
                                         cp_t[:, i * P:(i + 1) * P], cv_tok[:, i // QUAD], start=True, stop=True)
                else:
                    return
                last.then_inc(*pe_did.event("catt", t, n))

            pe.wait_ge(*row_ready.after(0))
            pe.wait_ge(*const_ready.after(6))
            take(0, (dve_did, "pos"))
            turn(aux[:, 0, 0:96], rows_in[0:96, 0]).then_inc(*pe_did.event("conv_w"))
            take(1, (dve_did, "pos"))
            turn(aux[:, 1, 0:64], rows_in[0:64, 1]).then_inc(*pe_did.event("pos"))
            for n in range(4):
                for t in range(NT):
                    flip("h1", n, t)
            steps = {"ba": ba_, "gcum": gcum_, "raw_flip": raw_flip, "conv_back": conv_back, "qk_flip": qk_flip,
                     "gram": gram, "tri_flip": tri_flip, "invert_y": invert_y, "invert_t": invert_t, "delta": delta,
                     "m_flip": m_flip, "att": att, "flip": flip, "ag": ag, "rope_flip": rope_flip,
                     "cmp_out": cmp_out, "catt": catt}
            for tick in range(TICKS + LAST):
                if tick < TICKS:
                    products(tick)
                for name, *args in PLAN[tick]:
                    if name in steps:
                        steps[name](*args)

        return {"signals": {n: s.seen for n, s in signals.items()}}


INPUTS = ["x", "pre_norm_w", "w_in", "conv_w", "a_log", "dt_bias", "gdn_norm_w", "w_branch_a", "w_branch_b", "w_out",
          "post_norm_w", "w_in_2", "cmp_k_w1_2", "cmp_k_w2_2", "cmp_v_w1_2", "cmp_v_w2_2", "cmp_k_pos_2",
          "cmp_v_pos_2", "sinks_2", "w_out_2", "norm_g_2", "final_g_2"]


def kernel(**inputs):
    import concourse.bacc as _bacc
    from concourse.bass_utils import run_bass_kernel_spmd as _run

    arrays = {n: np.ascontiguousarray(inputs[n]) for n in INPUTS}
    arrays.update(constants())
    known = None
    for _ in range(2):
        nc = _bacc.Bacc("TRN2", target_bir_lowering=False, num_devices=1)
        ins = {n: nc.dram_tensor(f"in_{n}", a.shape, mybir.dt.from_np(a.dtype), kind="ExternalInput").ap()
               for n, a in arrays.items()}
        out = nc.dram_tensor("out_y", (1, SEQ, D), F32, kind="ExternalOutput").ap()
        known = build(nc, known, ins, out)
    r = _run(nc, [{f"in_{n}": a for n, a in arrays.items()}], core_ids=[0])
    return r.results[0]["out_y"]
```

```python
from contextlib import ExitStack

import numpy as np

import concourse.bass as bass
from concourse import mybir

F32 = mybir.dt.float32
F32R = mybir.dt.float32r
ALU = mybir.AluOpType
ACT = mybir.ActivationFunctionType
AXX = mybir.AxisListType.X

P = 128
SEQ = 256
NT = SEQ // P
D = 2048
KT = D // P
HEADS = 8
QUAD = 4
COLS = 512
PIECE_KT = 2
GDN_W = 1024
CONV = 4
EPS = 1e-6
SCALE = 128.0 ** -0.5
SCALE_B = 64.0 ** -0.5
NEG = -1e30
TINY = 1e-30
N_CMP = 15
CMP_L = 32
LEVELS = 7
BLOCK_LEVELS = 5
RAW_SLOTS = 5
SPLIT_SLOTS = 4
AHEAD = 2
AUX = 4


class Signal:

    def __init__(self, sem, name, known, step=1):
        self.sem, self.name, self.known, self.step, self.seen, self.n = sem, name, known, step, {}, 0

    def event(self, *key):
        self.n += self.step
        assert key not in self.seen, (self.name, key)
        self.seen[key] = self.n
        return self.sem, self.step

    def after(self, *key):
        if self.known is None:
            return self.sem, 1
        return self.sem, self.known[key]


class Group:

    def __init__(self, name, weight, col, lhs, kt=KT, cols=COLS, kind="proj"):
        self.name, self.weight, self.col, self.lhs, self.kt, self.cols, self.kind = name, weight, col, lhs, kt, cols, kind


def groups():
    z, mo = 3 * GDN_W, 4 * GDN_W + 2 * HEADS
    mz, ga = mo + 3 * 1024, mo + 4 * 1024
    gb = ga + D
    out = []
    for h in range(2):
        for n, part in enumerate("qkv"):
            out.append(Group(("conv", part, h), "w_in", n * GDN_W + h * COLS, "h1", kind="channels"))
    for h in range(2):
        out.append(Group(("z", h), "w_in", z + h * COLS, "h1"))
    for h in range(2):
        for n, part in enumerate("qkv"):
            out.append(Group(("moba", part, h), "w_in", mo + n * 1024 + h * COLS, "h1",
                             kind="proj" if part == "v" else "channels"))
    for h in range(2):
        out.append(Group(("mz", h), "w_in", mz + h * COLS, "h1"))

    def gates(c):
        out.append(Group(("ga", c), "w_in", ga + c * COLS, "h1"))
        out.append(Group(("gb", c), "w_in", gb + c * COLS, "h1"))

    def branches(c):
        out.append(Group(("ua", c), "w_branch_a", c * COLS, "oa", kt=8))
        out.append(Group(("ub", c), "w_branch_b", c * COLS, "ob", kt=8))

    gates(0)
    gates(1)
    branches(0)
    branches(1)
    gates(2)
    branches(2)
    gates(3)
    branches(3)
    for c in range(4):
        out.append(Group(("wo", c), "w_out", c * COLS, "merged"))
    out.append(Group(("kcv",), "w_in_2", 1024, "h2"))
    out.append(Group(("qa", 0), "w_in_2", 0, "h2"))
    out.append(Group(("ksv",), "w_in_2", 1536, "h2"))
    out.append(Group(("kwv",), "w_in_2", 2048, "h2"))
    out.append(Group(("kvb",), "w_in_2", 4632, "h2", cols=256))
    out.append(Group(("qb", 0), "w_in_2", 3608, "h2"))
    out.append(Group(("qa", 1), "w_in_2", 512, "h2"))
    out.append(Group(("cmp", "k"), "cmp_k_w1_2", 0, "blk", kt=CMP_L, cols=256, kind="cmp"))
    out.append(Group(("qb", 1), "w_in_2", 3608 + COLS, "h2"))
    out.append(Group(("cmp", "v"), "cmp_v_w1_2", 0, "blk", kt=CMP_L, cols=256, kind="cmp"))
    for h in range(2):
        out.append(Group(("za", h), "w_in_2", 2560 + h * COLS, "h2"))
    for h in range(2):
        out.append(Group(("zb", h), "w_in_2", 4888 + h * COLS, "h2"))
    for c in range(4):
        out.append(Group(("w2", c), "w_out_2", c * COLS, "y"))
    return out


GROUPS = groups()
PIECES = []
END = {}
for _g, _group in enumerate(GROUPS):
    _n = PIECE_KT * COLS // _group.cols
    _own = [(_g, _k, _n, _k == 0, _k + _n == _group.kt) for _k in range(0, _group.kt, _n)]
    if _group.kind == "cmp":
        _m = len(PIECES) - len(_own)
        for _i, _piece in enumerate(_own):
            PIECES.insert(min(_m + 3 + 2 * _i, len(PIECES)), _piece)
    else:
        PIECES += _own
for _no, _piece in enumerate(PIECES):
    if _piece[4]:
        END[GROUPS[_piece[0]].name] = _no
TICKS = len(PIECES)
LAST = 40


def plan():
    steps = [[] for _ in range(TICKS + LAST)]

    def at(tick, *step):
        steps[tick].append(step)

    for n in (2, 3):
        at(n - 2, "scale_x", n)
        for t in range(NT):
            at(n - 2, "flip", "h1", n, t)
    for n in range(4):
        at(n + 1, "sq1", n)
    at(5, "norm1")
    at(6, "small_rows")
    at(6, "r1_row")
    at(12, "ba_split")
    at(20, "few_rows", "ba")
    at(21, "ba")
    at(22, "softplus")
    at(23, "gates")
    at(24, "gcum")
    at(25, "exp_gcum")
    at(26, "beta_gcum")
    for h in range(2):
        for part in "qkv":
            c = END[("conv", part, h)]
            at(c + 1, "raw_out", part, h)
            at(c + 2, "conv", part, h, 0)
            at(c + 3, "conv", part, h, 1)
            at(c + 4, "conv_silu", part, h)
            at(c + 5, "conv_back", part, h)
            at(c + 6, "token_out", part, h)
            if part != "v":
                at(c + 8, "qk_flip", part, h)
                at(c + 9, "qk_out", part, h)
    base = END[("conv", "v", 1)] + 8
    for h in range(2):
        for t in range(NT):
            s = base + 4 * t
            at(s, "gu", h, t)
            at(s + 1, "gram", h, t)
            at(s + 2, "decay", h, t)
            at(s + 3, "tri", h, t)
            at(s + 4, "tri_flip", h, t)
            at(s + 5, "invert_first", h, t)
            for n in range(2, LEVELS + 1):
                at(s + 8 + 3 * (n - 2), "invert_y", h, t, n)
                at(s + 9 + 3 * (n - 2), "invert_t", h, t, n)
                if n < LEVELS:
                    at(s + 10 + 3 * (n - 2), "invert_flip", h, t, n)
        s = base + 29
        for n in range(5):
            at(s + n, "delta", h, n)
        at(s + 5, "delta_norm", h)
        for t in range(NT):
            at(s + 7, "flip", "oa", h, t)
        base += 33
    base = s + 8
    for h in range(2):
        at(END[("z", h)] + 1, "z_out", h)
    for h in range(2):
        for part in "qk":
            at(END[("moba", part, h)] + 1, "m_out", part, h)
        at(END[("moba", "v", h)] + 1, "m_v", h)
        at(END[("mz", h)] + 1, "mz_out", h)
    s = max(base, END[("mz", 1)] + 2)
    for h in range(2):
        for t in range(NT):
            for n in range(5):
                at(s + n, "att", "m", h, t, n)
            at(s + 5, "flip", "ob", h, t)
            s += 4
    for c in range(4):
        at(END[("ga", c)] + 1, "gate_out", "a", c)
        at(END[("gb", c)] + 1, "gate_out", "b", c)
        at(END[("ua", c)] + 1, "branch", "a", c)
        at(END[("ub", c)] + 1, "branch", "b", c)
        for t in range(NT):
            at(END[("ub", c)] + 3, "flip", "merged", c, t)
        at(END[("wo", c)] + 1, "y_out", c)
    c = END[("wo", 3)]
    steps[c] += steps[c + 1]
    steps[c + 1] = []
    at(c, "residual", 0)
    at(c, "residual", 1)
    for n in range(4):
        for t in range(NT):
            at(c + n, "flip", "h2", n, t)
        if n in (1, 2):
            at(c + n, "residual", n + 1)
        at(c + 2 + n, "sq2", n)
    at(c + 5, "ag_split")
    at(c + 6, "norm2")
    at(c + 6, "few_rows", "ag")
    at(c + 7, "ag")
    at(c + 8, "head_gates")
    for name in (("kcv",), ("ksv",), ("kwv",), ("qa", 0), ("qa", 1), ("kvb",), ("qb", 0), ("qb", 1)):
        c = END[name]
        at(c + 1, "rope", *name)
        at(c + (5 if name in (("kvb",), ("qa", 1), ("qb", 1)) else 3), "rope_flip", *name)
    for n, part in enumerate("kv"):
        at(END[("kcv",)] + 5 + n, "blocks", part)
        at(END[("kcv",)] + 6 + n, "blocks_split", part)
        at(END[("cmp", part)] + 1, "cmp_rows", part)
        at(END[("cmp", part)] + 2, "cmp_fold", part)
        at(END[("cmp", part)] + (6 if part == "k" else 4), "cmp_out", part)
    def attend(start, kind, h):
        for t in range(NT):
            for n in range(5):
                at(start + 4 * t + n, "att", kind, h, t, n)
        return start + 4 * NT

    s = attend(max(END[("ksv",)], END[("qa", 0)]) + 4, "s", 0)
    s = attend(max(s, END[("kwv",)] + 4), "w", 0)
    s = max(s, END[("kvb",)] + 4, END[("qb", 0)] + 4)
    s = attend(attend(s, "b", 0), "b", 1)
    s = max(s, END[("qa", 1)] + 4)
    s = attend(attend(s, "s", 1), "w", 1)
    s = max(s + 1, END[("cmp", "v")] + 5)
    for t in range(NT):
        for n in range(5):
            at(s + n, "catt", t, n)
        s += 5
    s = max(s, END[("qb", 1)] + 4)
    first = s
    s = attend(attend(s, "b", 2), "b", 3)
    for n, (name, h) in enumerate((("za", 0), ("za", 1), ("zb", 0), ("zb", 1))):
        c = END[(name, h)]
        at(c + 1, "z2_out", n)
        gate = max(c + 2, first + 1) if n < 2 else max(c + 2, first + 1 if n == 2 else s + 1)
        at(gate, "y_gate", n)
        turn = gate + 2
        while first <= turn < s and (turn - first) % 4 not in (1, 2):
            turn += 1
        for t in range(NT):
            at(turn, "flip", "y", n, t)
    for c in range(4):
        at(END[("w2", c)] + 1, "y2_out", c)
    at(END[("w2", 3)] + 2, "finish")
    return steps


PLAN = plan()


def constants():
    i, j = np.arange(P)[:, None], np.arange(P)[None, :]
    f = np.float32
    out = {"ident": (i == j).astype(f), "upto": (i <= j).astype(f)}
    level = []
    for n in range(1, LEVELS + 1):
        m = 2 ** (n - 1)
        level.append(((i // (2 * m) == j // (2 * m)) & (j // m % 2 == 1) & (i // m % 2 == 0)).astype(f))
    below = (i > j).astype(f)
    out["levels"] = np.ascontiguousarray(np.stack([below, level[0].T] + level, 1))
    causal = np.where(j <= i, 0.0, NEG).astype(f)
    out["masks"] = np.ascontiguousarray(np.concatenate(
        [np.zeros((P, P), f), causal, np.where(j > i, 0.0, NEG).astype(f), causal], 1))
    s = np.arange(SEQ)
    ok = (np.arange(N_CMP) * 16 + 31)[None, :] <= s[:, None]
    cm = np.stack([np.where(ok, 0.0, NEG), ok.astype(f)], 1).astype(f)
    out["cmask"] = np.ascontiguousarray(cm.reshape(NT, P, 2, N_CMP).transpose(1, 2, 0, 3))
    rope = []
    for d in (128, 64):
        inv = f(10000.0) ** (-np.arange(0, d, 2, dtype=f) / f(d))
        ang = (s.astype(f)[:, None] * inv[None, :].astype(f)).astype(f).astype(np.float64)
        cos, sin = np.cos(ang), np.sin(ang)
        both = np.stack([np.concatenate([cos, cos], 1), np.concatenate([-sin, sin], 1)], 0).astype(f)
        rope.append(both.reshape(2, NT, P, d).transpose(2, 0, 1, 3))
    out["rope_a"], out["rope_b"] = (np.ascontiguousarray(r) for r in rope)
    return out


def build(nc, known, ins, out):
    ctx = ExitStack()
    with ctx:
        signals = {}

        def signal(name, step=1):
            k = None if known is None else known["signals"][name]
            s = signals[name] = Signal(ctx.enter_context(nc.semaphore(name)), name, k, step)
            return s

        start = (nc.sbuf_base + 31) // 32 * 32
        end = nc.sbuf_usable_end
        ctx.enter_context(nc.sbuf_tensor("arena", [P, (end - start) // 4 - 16], F32))
        cursor = [start]

        def place(name, shape, dtype, offset=None):
            size = int(np.prod(shape[1:])) * 4
            if offset is None:
                offset = cursor[0]
                cursor[0] += (size + 31) // 32 * 32
                assert cursor[0] <= end, (name, cursor[0], end)
            return nc.alloc_sbuf_tensor_at(name, list(shape), dtype, offset=offset)

        raw_w = [place(f"raw_w{i}", [P, PIECE_KT * COLS], F32) for i in range(RAW_SLOTS)]
        hi_w = [place(f"hi_w{i}", [P, PIECE_KT * COLS], F32R) for i in range(SPLIT_SLOTS)]
        lo_w = [place(f"lo_w{i}", [P, PIECE_KT * COLS], F32R) for i in range(SPLIT_SLOTS)]
        h_hi = place("h_hi", [P, KT, SEQ], F32R)
        h_lo = place("h_lo", [P, KT, SEQ], F32R)
        ident = place("ident", [P, P], F32)
        upto = place("upto", [P, P], F32)
        ones = place("ones", [P, P], F32)
        levels = place("levels", [P, LEVELS + 2, P], F32)
        masks = place("masks", [P, 2, SEQ], F32)
        cmask = place("cmask", [P, 2, NT, N_CMP], F32)
        rope_a = place("rope_a", [P, 2, NT, 128], F32)
        rope_b = place("rope_b", [P, 2, NT, 64], F32)
        conv_w = place("conv_w", [P, CONV, 24], F32)
        gnorm_w = place("gnorm_w", [P, P], F32)
        small = place("small", [P, 400], F32)
        half = place("half", [P, 16], F32)
        r1_row = place("r1_row", [P, SEQ], F32)
        w2s = {k: place(f"w2_{k}", [P, 2, P], F32) for k in "kv"}
        pos = {k: place(f"pos_{k}", [P, CMP_L], F32) for k in "kv"}
        top = [0]

        def bit(n):
            top[0] += n
            assert top[0] <= 400
            return small[:, top[0] - n:top[0]]

        dt_row, alog_row, sink_row = bit(HEADS), bit(HEADS), bit(16)
        r1, ry, r2, r3 = bit(NT), bit(NT), bit(NT), bit(NT)
        sum1, sumy, sum2, sum3 = bit(NT * 4), bit(NT * 4), bit(NT * 4), bit(NT * 4)
        tot = bit(NT)
        ba = bit(NT * 16)
        beta, nbeta, g, gcum, ngcum, eg, beg = (bit(NT * HEADS) for _ in range(7))
        tail, sp0, sp1, nexp = bit(HEADS), bit(NT * HEADS), bit(NT * HEADS), bit(HEADS)
        ssq, rnorm = bit(NT * QUAD), bit(NT * QUAD)
        head_gate = bit(NT * 24)
        mx, nmx, den, rden, esink = (bit(2 * QUAD) for _ in range(5))
        cmx, cden, crden = bit(HEADS), bit(HEADS), bit(HEADS)

        def tiles(ap, n):
            return ap.rearrange("p (t n) -> p t n", n=n)

        R0 = cursor[0]

        def arena(name, shape, dtype, kb):
            size = int(np.prod(shape[1:])) * 4
            assert R0 + kb * 1024 + size <= end, (name, kb, size, end - R0)
            return place(name, shape, dtype, R0 + int(kb * 1024))

        q_t = arena("q_t", [P, HEADS, SEQ], F32, 0)
        k_t = arena("k_t", [P, HEADS, SEQ], F32, 8)
        oa_hi = arena("oa_hi", [P, HEADS, SEQ], F32R, 0)
        oa_lo = arena("oa_lo", [P, HEADS, SEQ], F32R, 8)
        k_tok = arena("k_tok", [P, NT, HEADS, P], F32, 16)
        v_tok = arena("v_tok", [P, NT, HEADS, P], F32, 24)
        inv_t = arena("inv_t", [P, HEADS, NT, P], F32, 32)
        attn_t = arena("attn_t", [P, HEADS, NT, P], F32, 40)
        chain = [{n: arena(f"{n}{t}", [P, QUAD, P], F32, 48 + 8 * t + 2 * i)
                  for i, n in enumerate(("low_t", "low_m", "inv", "wide"))} for t in range(NT)]
        delta_u, delta_s, delta_r = (arena(f"delta_{n}", [P, QUAD, P], F32, 100 + 2 * i) for i, n in enumerate("usr"))
        delta_sq = arena("delta_sq", [P, NT, QUAD, P], F32, 100)
        raw = arena("raw", [P, QUAD, SEQ], F32, 48)
        cv = arena("cv", [P, QUAD, SEQ], F32, 52)
        sil = arena("sil", [P, QUAD, SEQ], F32, 56)
        q_tok = arena("q_tok", [P, NT, QUAD, P], F32, 60)
        sq = arena("sq", [P, NT, QUAD, P], F32, 92)
        x_in = arena("x_in", [P, NT, D], F32, 48)
        row1 = arena("row1", [1, D], F32, 64)
        xw = arena("xw", [P, NT, D], F32, 72)
        mzs = arena("mzs", [P, NT, HEADS, P], F32, 56)
        m_t = {"q": arena("mq_t", [P, HEADS, SEQ], F32, 64), "k": arena("mk_t", [P, HEADS, SEQ], F32, 72)}
        ob_hi = arena("ob_hi", [P, HEADS, SEQ], F32R, 64)
        ob_lo = arena("ob_lo", [P, HEADS, SEQ], F32R, 72)
        m_v = arena("m_v", [P, NT, HEADS, P], F32, 80)
        zs = arena("zs", [P, NT, HEADS, P], F32, 88)
        ba_raw = arena("ba_raw", [P, KT, 24], F32, 96)
        ba_parts = arena("ba_parts", [P, KT, 2, 16], F32R, 97.5)
        ag_parts = arena("ag_parts", [P, KT, 2, 24], F32R, 97.5)
        r1_diag = arena("r1_diag", [P, NT, P], F32, 101)
        few_t = arena("few_t", [48, SEQ], F32, 101)
        junk = arena("junk", [P, COLS], F32, 104)
        att_s = arena("att_s", [P, QUAD * SEQ], F32, 96)
        att_p = arena("att_p", [P, NT, QUAD * P], F32, 100)
        att_o = arena("att_o", [P, QUAD * P], F32, 104)
        sg = {"a": [arena(f"sga{i}", [P, NT, COLS], F32, 48 + 4 * i) for i in range(2)],
              "b": [arena(f"sgb{i}", [P, NT, COLS], F32, 88 + 4 * i) for i in range(2)]}
        merged = arena("merged", [P, NT, COLS], F32, 96)
        m_hi = arena("m_hi", [P, KT, SEQ], F32R, 16)
        m_lo = arena("m_lo", [P, KT, SEQ], F32R, 32)
        y1 = arena("y1", [P, NT, D], F32, 48)
        x2 = arena("x2", [P, NT, D], F32, 64)
        post_row = arena("post_row", [P, D], F32, 80)
        row2 = arena("row2", [P, D], F32, 88)
        qa_t = arena("qa_t", [P, HEADS, SEQ], F32, 0)
        kt2 = {n: arena(f"{n}_t", [P, 2, SEQ], F32, 8 + 2 * i) for i, n in enumerate(("kc", "vc", "ks", "kw"))}
        v2 = {n: arena(f"{n}_tok", [P, NT, 2, P], F32, 48 + 2 * i) for i, n in enumerate(("vs", "vw"))}
        kz = arena("kz", [P, 2, 2, SEQ], F32, 52)
        vb = arena("vb", [P, NT, 2, 64], F32, 56)
        hs = {p: arena(f"hs_{p}", [P, 2, 2 * N_CMP], F32, 57 + 0.25 * i) for i, p in enumerate("kv")}
        ck_t = arena("ck_t", [P, 2 * N_CMP], F32, 57.5)
        cs = arena("cs", [P, HEADS, N_CMP], F32, 58)
        cv_tok = arena("cv_tok", [N_CMP, 2, P], F32, 59)
        oa_tok = arena("oa_tok", [P, NT, HEADS * P], F32, 60)
        ob_tok = arena("ob_tok", [P, NT, 16 * 64], F32, 68)
        blk_parts = {p: arena(f"blk_parts_{p}", [P, CMP_L, 2, 2 * N_CMP], F32R, 16 + 8 * i) for i, p in enumerate("kv")}
        cmp_rows = arena("cmp_rows", [4 * N_CMP, 256], F32, 32)
        blk = {p: arena(f"blk_{p}", [P, CMP_L, 2, N_CMP], F32, 76 + 4 * i) for i, p in enumerate("kv")}
        qb_t = [arena(f"qb_t{i}", [P, QUAD, SEQ], F32, (8, 76)[i]) for i in range(2)]
        rot = [arena(f"rot{i}", [P, NT, COLS], F32, 84 + 4 * i) for i in range(3)]
        z2 = [arena(f"z2_{i}", [P, NT, COLS], F32, 84 + 4 * i) for i in range(2)]
        cp_t = arena("cp_t", [N_CMP, HEADS * P], F32, 100)
        x3 = arena("x3", [P, NT, D], F32, 0)
        last_row = arena("last_row", [P, D], F32, 48)
        y3 = arena("y3", [P, NT, D], F32, 76)
        rows_in = arena("rows_in", [P, 2, P], F32, 102)

        acc = ctx.enter_context(nc.psum_tensor("acc", [P, 2, NT, COLS], F32))
        aux = ctx.enter_context(nc.psum_tensor("aux", [P, AUX, COLS], F32))
        scratch = nc.dram_tensor("x2_scratch", [SEQ, D], F32, kind="Internal").ap()

        raw_ready = [signal(f"raw_ready{i}", 16) for i in range(RAW_SLOTS)]
        x_ready = [signal(f"x_ready{i}", 16) for i in range(2 * NT)]
        row_ready = signal("row_ready", 16)
        const_ready = signal("const_ready", 16)
        ba_ready = signal("ba_ready", 16)
        block2_rows = signal("block2_rows", 16)
        x_again = signal("x_again", 16)
        spilled = signal("spilled", 16)
        x3_ready = signal("x3_ready", 16)
        last_ready = signal("last_ready", 16)
        stored = signal("stored", 16)
        hi_ready = signal("hi_ready")
        lo_ready = signal("lo_ready")
        used = signal("used")
        pe_did = signal("pe_did")
        act_did = signal("act_did")
        dve_did = signal("dve_did")
        pool_did = signal("pool_did")
        flip_source = signal("flip_source")
        flip_filled = signal("flip_filled")
        flip_hi = signal("flip_hi")
        flip_lo = signal("flip_lo")
        act_chain, dve_chain, pool_chain = (ctx.enter_context(nc.semaphore(f"{e}_chain"))
                                            for e in ("act", "dve", "pool"))

        LHS = {"h1": (h_hi, h_lo), "h2": (h_hi, h_lo), "oa": (oa_hi, oa_lo), "ob": (ob_hi, ob_lo),
               "merged": (m_hi, m_lo), "y": (m_hi, m_lo)}

        def flip_bank(name, n, t):
            return {"oa": 3 * t, "ob": 3, "y": 2 + t}.get(name, (2 * n + t) % AUX)

        def acc_of(tick):
            return acc[:, PIECES[tick][0] % 2]

        def channels_of(tick):
            return acc_of(tick).rearrange("p b (i c) -> p (b i) c", c=SEQ)

        def quad(h):
            return slice(h * QUAD, (h + 1) * QUAD)

        def blocks_of(ap, n, odd):
            b = 2 ** (n - 1)
            if len(ap.shape) == 2:
                return ap.rearrange("p (m r b) -> p m r b", r=2, b=b)[:, :, odd]
            return ap.rearrange("p i (m r b) -> p i m r b", r=2, b=b)[:, :, :, odd]

        def half_bank(bank, n):
            return aux[:, bank, 0:QUAD * P // 2].rearrange("p (i m b) -> p i m b", i=QUAD, b=2 ** (n - 1))

        def over_heads(ap, n=QUAD):
            return ap.unsqueeze(1).broadcast_to([P, n, ap.shape[-1]])

        def over_cols(ap, m=P):
            return ap.unsqueeze(2).broadcast_to([P, ap.shape[-1], m])

        conv_order = [(p, h) for h in range(2) for p in "qkv"]
        qk_order = [(p, h) for h in range(2) for p in "qk"]

        def before_conv(part, h):
            return conv_order[conv_order.index((part, h)) - 1]

        def before_qk(part, h):
            return qk_order[qk_order.index((part, h)) - 1]

        att_before, rope_before, last_att, last_rope = {}, {}, None, None
        for steps_ in PLAN:
            for name, *args in steps_:
                if name == "att" and args[3] == 0:
                    att_before[tuple(args[:3])] = last_att
                    last_att = ("att", *args[:3], 4)
                if name == "rope":
                    rope_before[tuple(args)] = last_rope
                    last_rope = tuple(args)

        block = ctx.enter_context(nc.Block())

        def piece_source(no):
            g, k0, n, _, _ = PIECES[no]
            group = GROUPS[g]
            w = ins[group.weight][0]
            return w[k0 * P:(k0 + n) * P, group.col:group.col + group.cols].rearrange("(k p) c -> p k c", p=P)

        def piece_view(buf, no):
            g, _, n, _, _ = PIECES[no]
            return buf[:, :].rearrange("p (k c) -> p k c", k=n)

        @block.sync
        def _(sp):
            x = ins["x"][0].rearrange("(t p) d -> p t d", p=P)
            sp.dma_start(ident[:], ins["ident"]).then_inc(*row_ready.event(0))
            sp.dma_start(row1[:], ins["pre_norm_w"]).then_inc(*row_ready.event(1))
            for m in range(2):
                for t in range(NT):
                    cols = slice(m * D // 2, (m + 1) * D // 2)
                    sp.dma_start(x_in[:, t, cols], x[:, t, cols]).then_inc(*x_ready[2 * m + t].event(0))

            def load(no):
                if no >= RAW_SLOTS:
                    old = no - RAW_SLOTS
                    sp.wait_ge(*lo_ready.after(old))
                sp.dma_start(piece_view(raw_w[no % RAW_SLOTS], no), piece_source(no)).then_inc(
                    *raw_ready[no % RAW_SLOTS].event(no))

            for no in range(RAW_SLOTS):
                load(no)
            loads = [
                (rows_in[0:96, 0], ins["conv_w"][0].rearrange("j (i c) -> (j i) c", c=P)),
                (rows_in[0:CMP_L, 1], ins["cmp_k_pos_2"][0]),
                (rows_in[CMP_L:2 * CMP_L, 1], ins["cmp_v_pos_2"][0]),
                (ba_raw[:, :, 0:16], ins["w_in"][0][:, 4 * GDN_W:4 * GDN_W + 16].rearrange("(k p) c -> p k c", p=P)),
                (dt_row, ins["dt_bias"][0].partition_broadcast(P)),
                (alog_row, ins["a_log"][0].partition_broadcast(P)),
                (upto[:], ins["upto"]),
            ]
            for n, (to, source) in enumerate(loads):
                sp.dma_start(to, source).then_inc(*const_ready.event(n))
            loads = [
                (levels[:], ins["levels"]),
                (masks[:], ins["masks"].rearrange("p (a b) -> p a b", a=2)),
                (cmask[:], ins["cmask"]),
                (rope_a[:], ins["rope_a"]),
                (rope_b[:], ins["rope_b"]),
                (gnorm_w[:], ins["gdn_norm_w"][0].partition_broadcast(P)),
                (sink_row, ins["sinks_2"][0].partition_broadcast(P)),
                (w2s["k"][:], ins["cmp_k_w2_2"][0].rearrange("(k p) c -> p k c", p=P)),
                (w2s["v"][:], ins["cmp_v_w2_2"][0].rearrange("(k p) c -> p k c", p=P)),
            ]
            for n, (to, source) in enumerate(loads):
                sp.dma_start(to, source).then_inc(*block2_rows.event(n))
            for no in range(RAW_SLOTS, TICKS):
                load(no)
            store = out[0].rearrange("(t p) d -> p t d", p=P)
            for m in range(2):
                for t in range(NT):
                    cols = slice(m * D // 2, (m + 1) * D // 2)
                    sp.wait_ge(*(act_did, dve_did)[t].after("finish", m))
                    sp.dma_start(store[:, t, cols], y3[:, t, cols]).then_inc(*stored.event(m, t))
            sp.wait_ge(*stored.after(1, NT - 1))

        @block.gpsimd
        def _(pool):
            n_chain = [0]

            def link(ins_):
                n_chain[0] += 1
                ins_.then_inc(pool_chain, 1)
                pool.wait_ge(pool_chain, n_chain[0])

            link(pool.memset(half[:], -0.5))
            pool.memset(ones[:], 1.0).then_inc(*pool_did.event("ones"))

            def root(dst, src, scale, key, times=None):
                n = dst.shape[-1]
                link(pool.tensor_scalar(dst, src, scale, EPS, ALU.mult, ALU.add))
                last = pool.tensor_tensor(dst, dst, half[:, 0:n], ALU.pow)
                if times is not None:
                    link(last)
                    last = pool.tensor_scalar(dst, dst, times, None, ALU.mult)
                last.then_inc(*pool_did.event(*key))

            def norm1():
                pool.wait_ge(*dve_did.after("sum1"))
                root(r1, tot, 1.0 / D, ("r1",))

            def token_out(part, h):
                if part != "v":
                    pool.wait_ge(*dve_did.after("ssq", part, h))
                    root(rnorm, ssq, 1.0, ("rnorm", part, h), SCALE if part == "q" else None)

            def delta_norm(h):
                pool.wait_ge(*dve_did.after("delta_ssq", h))
                root(rnorm, ssq, 1.0 / P, ("delta_rnorm", h))

            def branch(ab, c):
                if (ab, c) == ("b", 3):
                    pool.wait_ge(*used.after(END[("ub", 3)]))
                    pool.wait_ge(*flip_source.after("merged", 3))
                    pool.dma_start(x2[:], ins["x"][0].rearrange("(t p) d -> p t d", p=P)).then_inc(*x_again.event(0))
                    pool.dma_start(post_row[:], ins["post_norm_w"][0].partition_broadcast(P)).then_inc(*x_again.event(1))
                    pool.dma_start(row2[:], ins["norm_g_2"][0].partition_broadcast(P)).then_inc(*x_again.event(2))
                    for n in range(4):
                        for t in range(NT):
                            pool.wait_ge(*flip_filled.after("merged", n, t))
                    pool.dma_start(ba_raw[:], ins["w_in_2"][0][:, 3584:3608].rearrange("(k p) c -> p k c", p=P)).then_inc(
                        *ba_ready.event(0))

            def residual(n):
                if n == 0:
                    pool.wait_ge(*dve_did.after("sumy"))
                    root(ry, tot, 1.0 / D, ("ry",))
                if n == 3:
                    pool.wait_ge(*dve_did.after("x2", 3))
                    pool.dma_start(scratch.rearrange("(t p) d -> p t d", p=P), x2[:]).then_inc(*spilled.event(0))

            def norm2():
                pool.wait_ge(*dve_did.after("sum2"))
                root(r2, tot, 1.0 / D, ("r2",))
                pool.wait_ge(*flip_filled.after("h2", 3, 1))
                pool.memset(kz[:], 0.0).then_inc(*pool_did.event("kz"))

            def att(kind, h, t, n):
                if (kind, h, t, n) == ("w", 1, 1, 4):
                    pool.wait_ge(*dve_did.after("catt", 1))
                    pool.dma_start(x3[:], scratch.rearrange("(t p) d -> p t d", p=P)).then_inc(*x3_ready.event(0))
                if (kind, h, t, n) == ("b", 3, 1, 4):
                    pool.wait_ge(*pe_did.after("att", "b", 3, 1, 4))
                    pool.dma_start(last_row[:], ins["final_g_2"].partition_broadcast(P)).then_inc(*last_ready.event(0))

            def finish():
                pool.wait_ge(*dve_did.after("sum3"))
                root(r3, tot, 1.0 / D, ("r3",))

            steps = {"token_out": token_out, "delta_norm": delta_norm, "branch": branch,
                     "norm1": norm1, "norm2": norm2, "residual": residual, "att": att, "finish": finish}
            for tick in range(TICKS + LAST):
                for name, *args in PLAN[tick]:
                    if name in steps:
                        steps[name](*args)

        @block.scalar
        def _(act):
            n_chain = [0]

            def link(ins_):
                n_chain[0] += 1
                ins_.then_inc(act_chain, 1)
                act.wait_ge(act_chain, n_chain[0])

            def split(no):
                slot = no % SPLIT_SLOTS
                act.wait_ge(*raw_ready[no % RAW_SLOTS].after(no))
                if no >= SPLIT_SLOTS:
                    act.wait_ge(*used.after(no - SPLIT_SLOTS))
                n = PIECES[no][2] * GROUPS[PIECES[no][0]].cols
                act.activation(hi_w[slot][:, 0:n], raw_w[no % RAW_SLOTS][:, 0:n], ACT.Copy).then_inc(
                    *hi_ready.event(no))

            def scaled(dst, source, r, func, last):
                for t in range(NT):
                    i = act.activation(dst[:, t], source[:, t], func, scale=r[:, t:t + 1])
                i.then_inc(*last)

            def squares(sources, key):
                for m, (source, to) in enumerate(sources):
                    last = act.activation(junk[:], source, ACT.Square, accum_out=to)
                    if m < len(sources) - 1:
                        link(last)
                last.then_inc(*act_did.event(*key))
                act.wait_ge(*act_did.after(*key))

            def flip(name, n, t):
                b = flip_bank(name, n, t)
                act.wait_ge(*flip_filled.after(name, n, t))
                hi = LHS[name][0]
                act.activation(hi[:, quad(n), t * P:(t + 1) * P],
                               aux[:, b].rearrange("p (k c) -> p k c", k=QUAD), ACT.Copy).then_inc(
                    *flip_hi.event(name, n, t))

            def sq1(n):
                t = n % 2
                squares([(x_in[:, t, c * COLS:(c + 1) * COLS], sum1[:, t * 4 + c:t * 4 + c + 1])
                         for c in range(n // 2 * 2, n // 2 * 2 + 2)], ("sq1", n))

            def ba_split():
                act.wait_ge(*const_ready.after(6))
                act.activation(ba_parts[:, :, 0], ba_raw[:, :, 0:16], ACT.Copy).then_inc(*act_did.event("ba_hi"))

            def few_rows(key):
                n = 2 * {"ba": 16, "ag": 24}[key]
                act.wait_ge(*pe_did.after("few_rows", key))
                act.activation(few_t[0:n], aux[0:n, 0, 0:SEQ], ACT.Copy).then_inc(*act_did.event("few_rows", key))

            def softplus():
                act.wait_ge(*dve_did.after("ba"))
                b3, a3 = tiles(ba, 16)[:, :, 0:HEADS], tiles(sp0, HEADS)
                act.activation(tiles(beta, HEADS), b3, ACT.Exp, scale=-1.0)
                act.activation(nexp, alog_row, ACT.Exp)
                link(act.activation(tiles(sp1, HEADS), a3, ACT.Abs))
                link(act.activation(sp1, sp1, ACT.Exp, scale=-1.0))
                act.activation(sp1, sp1, ACT.Ln, bias=1.0).then_inc(*act_did.event("softplus"))

            def exp_gcum():
                act.wait_ge(*dve_did.after("gcum"))
                act.activation(eg, gcum, ACT.Exp)
                act.activation(tail, tail, ACT.Exp).then_inc(*act_did.event("eg"))

            def conv(part, h, n):
                if n:
                    return
                act.wait_ge(*dve_did.after("raw_out", part, h))
                if (part, h) != ("q", 0):
                    act.wait_ge(*act_did.after("silu", *before_conv(part, h)))
                first = "qkv".index(part) * HEADS + h * QUAD
                for i in range(QUAD):
                    tap = act.activation(cv[:, i], raw[:, i], ACT.Copy,
                                         scale=conv_w[:, CONV - 1, first + i:first + i + 1])
                tap.then_inc(*act_did.event("tap", part, h))

            def conv_silu(part, h):
                act.wait_ge(*dve_did.after("conv", part, h))
                if (part, h) != ("q", 0):
                    act.wait_ge(*pe_did.after("conv_back", *before_conv(part, h)))
                act.activation(sil[:], cv[:], ACT.Silu).then_inc(*act_did.event("silu", part, h))

            def token_out(part, h):
                if part == "v":
                    return
                act.wait_ge(*pe_did.after("conv_back", part, h))
                if (part, h) != ("q", 0):
                    act.wait_ge(*dve_did.after("ssq", *before_qk(part, h)))
                act.activation(sq[:], aux[:, 2:4].rearrange("p b (i c) -> p b i c", c=P), ACT.Square).then_inc(
                    *act_did.event("sq", part, h))

            def qk_out(part, h):
                act.wait_ge(*pe_did.after("qk_flip", part, h))
                to = q_t if part == "q" else k_t
                s = aux[:, 2:4].rearrange("p b (i c) -> p (b i) c", c=SEQ)
                act.activation(to[:, quad(h)], s, ACT.Copy).then_inc(
                    *act_did.event("qk_out", part, h))

            def decay(h, t):
                c = chain[t]
                act.wait_ge(*pe_did.after("gram", h, t))
                for i in range(QUAD):
                    o = t * HEADS + h * QUAD + i
                    last = act.activation(c["inv"][:, i], aux[:, 0, i * P:(i + 1) * P], ACT.Abs,
                                          bias=ngcum[:, o:o + 1])
                link(last)
                act.activation(c["inv"][:], c["inv"][:], ACT.Exp, scale=-1.0).then_inc(*act_did.event("decay", h, t))

            def tri_flip(h, t):
                act.wait_ge(*pe_did.after("tri_flip", h, t))
                act.activation(chain[t]["low_t"][:], aux[:, 3].rearrange("p (i c) -> p i c", c=P), ACT.Copy).then_inc(
                    *act_did.event("tri_flip", h, t))

            def invert_flip(h, t, n):
                if n <= BLOCK_LEVELS:
                    return
                act.wait_ge(*pe_did.after("invert_flip", h, t, n))
                act.activation(blocks_of(chain[t]["inv"], n, 0), half_bank(1, n), ACT.Copy).then_inc(
                    *act_did.event("invert_flip", h, t, n))

            def delta(h, n):
                bank_to = {0: (0, delta_u), 1: (1, delta_s), 3: (1, delta_u)}
                if n in bank_to:
                    b, to = bank_to[n]
                    act.wait_ge(*pe_did.after("delta", h, n))
                    act.activation(to[:], aux[:, b].rearrange("p (i c) -> p i c", c=P), ACT.Copy).then_inc(
                        *act_did.event("delta", h, n))

            def delta_norm(h):
                act.wait_ge(*dve_did.after("delta", h, 4))
                act.activation(delta_sq[:], k_tok[:, :, quad(h)], ACT.Square).then_inc(*act_did.event("delta_sq", h))

            def z_out(h):
                a = acc_of(END[("z", h)])
                act.wait_ge(*used.after(END[("z", h)]))
                if h == 0:
                    act.wait_ge(*dve_did.after("ssq", "k", 1))
                for t in range(NT):
                    i = act.activation(zs[:, t, quad(h)], a[:, t].rearrange("p (i c) -> p i c", c=P), ACT.Silu,
                                       scale=r1[:, t:t + 1])
                i.then_inc(*act_did.event("z", h))

            def m_v_(h):
                a = acc_of(END[("moba", "v", h)])
                act.wait_ge(*used.after(END[("moba", "v", h)]))
                for t in range(NT):
                    i = act.activation(m_v[:, t, quad(h)], a[:, t].rearrange("p (i c) -> p i c", c=P), ACT.Copy,
                                       scale=r1[:, t:t + 1])
                i.then_inc(*act_did.event("m_v", h))

            def mz_out(h):
                a = acc_of(END[("mz", h)])
                act.wait_ge(*used.after(END[("mz", h)]))
                for t in range(NT):
                    i = act.activation(mzs[:, t, quad(h)], a[:, t].rearrange("p (i c) -> p i c", c=P), ACT.Silu,
                                       scale=r1[:, t:t + 1])
                i.then_inc(*act_did.event("mz", h))

            def att(kind, h, t, n):
                k = (t + 1) * P
                if n == 2:
                    act.wait_ge(*dve_did.after("max", kind, h, t))
                    sc = SCALE_B if kind == "b" else SCALE
                    if kind == "b":
                        act.activation(esink[:, 0:QUAD], esink[:, 0:QUAD], ACT.Exp)
                    for i in range(QUAD):
                        e = act.activation(att_s[:, i * k:(i + 1) * k], att_s[:, i * k:(i + 1) * k], ACT.Exp,
                                           bias=nmx[:, i:i + 1], scale=sc, accum_out=den[:, i:i + 1])
                    e.then_inc(*act_did.event("exp", kind, h, t))
                if n == 3:
                    act.wait_ge(*pe_did.after("att", kind, h, t, 3))
                    if att_before[(kind, h, t)]:
                        act.wait_ge(*pe_did.after(*att_before[(kind, h, t)]))
                    act.activation(att_p[:, 0:t + 1], aux[:, 2:3 + t], ACT.Copy).then_inc(
                        *act_did.event("att_p", kind, h, t))

            def gate_out(ab, c):
                a = acc_of(END[("g" + ab, c)])
                act.wait_ge(*used.after(END[("g" + ab, c)]))
                if c >= 2:
                    act.wait_ge(*flip_source.after("merged", c - 2))
                scaled(sg[ab][c % 2], a, r1, ACT.Sigmoid, act_did.event("gate_out", ab, c))

            def y_out(c):
                a = acc_of(END[("wo", c)])
                act.wait_ge(*used.after(END[("wo", c)]))
                for t in range(NT):
                    if t:
                        act.wait_ge(*dve_did.after("y_out", c, t))
                    squares([(a[:, t], sumy[:, t * 4 + c:t * 4 + c + 1])], ("y_out", c, t))

            def sq2(n):
                act.wait_ge(*dve_did.after("x2", n))
                cols = slice(n * COLS, (n + 1) * COLS)
                squares([(x2[:, t, cols], sum2[:, t * 4 + n:t * 4 + n + 1]) for t in range(NT)], ("sq2", n))

            def ag_split():
                act.wait_ge(*ba_ready.after(0))
                act.activation(ag_parts[:, :, 0], ba_raw[:], ACT.Copy).then_inc(*act_did.event("ag_hi"))

            def head_gates():
                act.wait_ge(*pe_did.after("ag"))
                act.wait_ge(*pool_did.after("r2"))
                for t in range(NT):
                    i = act.activation(head_gate[:, t * 24:(t + 1) * 24], aux[:, 0, t * 24:(t + 1) * 24], ACT.Sigmoid,
                                       scale=r2[:, t:t + 1])
                i.then_inc(*act_did.event("head_gates"))

            def rope(*name):
                a = acc_of(END[name])
                half_ = COLS // 2
                to = {"kcv": rot[2][:, :, half_:COLS], "ksv": v2["vs"], "kwv": v2["vw"], "kvb": vb}.get(name[0])
                if to is None:
                    return
                act.wait_ge(*dve_did.after("rope_read", *name))
                act.wait_ge(*pool_did.after("kz"))
                w = P if name[0] == "kvb" else half_
                for t in range(NT):
                    s = a[:, t, w:2 * w]
                    if name[0] != "kcv":
                        s = s.rearrange("p (k c) -> p k c", k=2)
                    i = act.activation(to[:, t], s, ACT.Copy, scale=r2[:, t:t + 1])
                i.then_inc(*act_did.event("values", *name))

            def rope_flip(*name):
                act.wait_ge(*pe_did.after("rope_flip", *name))
                s = aux[:, 2:4].rearrange("p b (i c) -> p (b i) c", c=SEQ)
                if name[0] in ("qa", "qb"):
                    if name[0] == "qa":
                        to = qa_t[:, quad(name[1])]
                    else:
                        to = qb_t[name[1]][:]
                        act.wait_ge(*dve_did.after("blocks", "v"))
                        if name[1] == 1:
                            act.wait_ge(*used.after(END[("cmp", "v")]))
                    i = act.activation(to, s, ACT.Copy)
                elif name[0] == "kcv":
                    act.activation(kt2["kc"][:], s[:, 0:2], ACT.Copy)
                    i = act.activation(kt2["vc"][:], s[:, 2:4], ACT.Copy)
                elif name[0] == "kvb":
                    act.activation(kz[0:64, :, 0], s[0:64, 0:2], ACT.Copy)
                    i = act.activation(kz[64:P, :, 1], s[64:P, 0:2], ACT.Copy)
                else:
                    i = act.activation(kt2[name[0][0:2]][:], s[:, 0:2], ACT.Copy)
                i.then_inc(*act_did.event("rope_flip", *name))

            def blocks_split(part):
                act.wait_ge(*dve_did.after("blocks", part))
                act.activation(blk_parts[part][:, :, 0], blk[part][:].rearrange("p l i c -> p l (i c)"),
                               ACT.Copy).then_inc(*act_did.event("blocks_hi", part))

            def cmp_rows_(part):
                a = acc_of(END[("cmp", part)])
                act.wait_ge(*used.after(END[("cmp", part)]))
                if part == "v":
                    act.wait_ge(*pe_did.after("cmp_fold", "k"))
                act.activation(cmp_rows[:], a[0:4 * N_CMP, 0, 0:256], ACT.Copy).then_inc(*act_did.event("cmp_rows", part))

            def cmp_fold(part):
                act.wait_ge(*pe_did.after("cmp_fold", part))
                act.activation(hs[part][:], aux[:, 0, 0:4 * N_CMP].rearrange("p (m c) -> p m c", m=2),
                               ACT.Silu).then_inc(*act_did.event("hs", part))

            def cmp_out(part):
                act.wait_ge(*pe_did.after("cmp_out", part))
                if part == "k":
                    i = act.activation(ck_t[:], aux[:, 0, 0:2 * N_CMP], ACT.Copy)
                else:
                    i = act.activation(cv_tok[:], aux[0:N_CMP, 0, 0:2 * P].rearrange("p (k c) -> p k c", k=2), ACT.Copy)
                i.then_inc(*act_did.event("cmp_out", part))

            def catt(t, n):
                if n == 2:
                    act.wait_ge(*dve_did.after("cmax", t))
                    act.activation(cs[:], cs[:], ACT.Exp).then_inc(*act_did.event("cexp", t))
                if n == 3:
                    act.wait_ge(*pe_did.after("catt", t, 3))
                    if t == 0:
                        act.wait_ge(*pe_did.after("att", "w", 1, 1, 4))
                    else:
                        act.wait_ge(*pe_did.after("catt", 0, 4))
                    act.activation(cp_t[:].rearrange("p (b c) -> p b c", b=2), aux[0:N_CMP, 2:4], ACT.Copy).then_inc(
                        *act_did.event("cp", t))

            def z2_out(n):
                name = (("za", 0), ("za", 1), ("zb", 0), ("zb", 1))[n]
                a = acc_of(END[name])
                act.wait_ge(*used.after(END[name]))
                if n == 0:
                    act.wait_ge(*pe_did.after("rope_flip", "qb", 1))
                if n >= 2:
                    act.wait_ge(*flip_source.after("y", n - 2))
                scaled(z2[n % 2], a, r2, ACT.Silu, act_did.event("z2", n))

            def y2_out(c):
                act.wait_ge(*dve_did.after("x3", c))
                squares([(x3[:, t, c * COLS:(c + 1) * COLS], sum3[:, t * 4 + c:t * 4 + c + 1]) for t in range(NT)],
                        ("sq3", c))

            def finish():
                act.wait_ge(*pool_did.after("r3"))
                act.wait_ge(*dve_did.after("y3", 3))
                for m in range(2):
                    y = y3[:, 0, m * D // 2:(m + 1) * D // 2]
                    act.activation(y, y, ACT.Copy, scale=r3[:, 0:1]).then_inc(*act_did.event("finish", m))

            for n in range(2):
                for t in range(NT):
                    flip("h1", n, t)
                split(n)
            steps = {"sq1": sq1, "few_rows": few_rows, "ba_split": ba_split, "softplus": softplus, "exp_gcum": exp_gcum, "sq2": sq2,
                     "ag_split": ag_split, "conv": conv, "conv_silu": conv_silu,
                     "token_out": token_out, "qk_out": qk_out, "decay": decay, "tri_flip": tri_flip,
                     "invert_flip": invert_flip, "delta": delta, "delta_norm": delta_norm, "z_out": z_out,
                     "m_v": m_v_, "mz_out": mz_out, "att": att, "flip": flip,
                     "gate_out": gate_out, "y_out": y_out, "head_gates": head_gates,
                     "rope": rope, "rope_flip": rope_flip, "blocks_split": blocks_split, "cmp_rows": cmp_rows_,
                     "cmp_fold": cmp_fold, "cmp_out": cmp_out, "catt": catt,
                     "z2_out": z2_out, "y2_out": y2_out, "finish": finish}
            for tick in range(TICKS + LAST):
                if tick + AHEAD < TICKS:
                    split(tick + AHEAD)
                for name, *args in PLAN[tick]:
                    if name in steps:
                        steps[name](*args)

        @block.vector
        def _(dve):
            n_chain = [0]

            def link(ins_):
                n_chain[0] += 1
                ins_.then_inc(dve_chain, 1)
                dve.wait_ge(dve_chain, n_chain[0])

            def split(no):
                slot = no % SPLIT_SLOTS
                dve.wait_ge(*hi_ready.after(no))
                n = PIECES[no][2] * GROUPS[PIECES[no][0]].cols
                dve.tensor_tensor(lo_w[slot][:, 0:n], raw_w[no % RAW_SLOTS][:, 0:n],
                                  hi_w[slot][:, 0:n].bitcast(F32), ALU.subtract).then_inc(*lo_ready.event(no))

            def flip(name, n, t):
                b = flip_bank(name, n, t)
                dve.wait_ge(*flip_hi.after(name, n, t))
                hi, lo = LHS[name]
                at = (slice(None), quad(n), slice(t * P, (t + 1) * P))
                dve.tensor_tensor(lo[at], aux[:, b].rearrange("p (k c) -> p k c", k=QUAD), hi[at].bitcast(F32),
                                  ALU.subtract).then_inc(*flip_lo.event(name, n, t))

            def ba_():
                dve.wait_ge(*pe_did.after("ba"))
                dve.wait_ge(*pool_did.after("r1"))
                for t in range(NT):
                    last = dve.tensor_scalar(ba[:, t * 16:(t + 1) * 16], aux[:, 0, t * 16:(t + 1) * 16], r1[:, t:t + 1],
                                             None, ALU.mult)
                link(last)
                dve.wait_ge(*const_ready.after(6))
                dve.tensor_tensor(tiles(sp0, HEADS), tiles(ba, 16)[:, :, HEADS:2 * HEADS], over_heads(dt_row, NT),
                                  ALU.add).then_inc(*dve_did.event("ba"))

            def gates():
                dve.wait_ge(*act_did.after("softplus"))
                link(dve.tensor_scalar(beta, beta, 1.0, None, ALU.add))
                link(dve.reciprocal(beta, beta))
                dve.tensor_scalar(nbeta, beta, -1.0, None, ALU.mult)
                link(dve.tensor_scalar(sp0, sp0, 0.0, None, ALU.max))
                link(dve.tensor_tensor(sp0, sp0, sp1, ALU.add))
                link(dve.tensor_scalar(sp0, sp0, -1.0, None, ALU.mult))
                dve.tensor_tensor(tiles(g, HEADS), tiles(sp0, HEADS), over_heads(nexp, NT), ALU.mult).then_inc(
                    *dve_did.event("g"))

            def gcum_():
                dve.wait_ge(*pe_did.after("gcum"))
                link(dve.tensor_copy(gcum, aux[:, 1, 0:NT * HEADS]))
                dve.tensor_scalar(ngcum, gcum, -1.0, None, ALU.mult)
                dve.tensor_tensor(tail, aux[:, 1, NT * HEADS:NT * HEADS + HEADS], gcum[:, 0:HEADS],
                                  ALU.subtract).then_inc(*dve_did.event("gcum"))

            def beta_gcum():
                dve.wait_ge(*act_did.after("eg"))
                dve.tensor_tensor(beg, beta, eg, ALU.mult).then_inc(*dve_did.event("beg"))

            def scale_x(n):
                cols = slice(n * COLS, (n + 1) * COLS)
                for t in range(NT):
                    dve.wait_ge(*x_ready[n // 2 * 2 + t].after(0))
                    dve.tensor_tensor(xw[:, t, cols], x_in[:, t, cols], acc[:, n // 2, n % 2], ALU.mult).then_inc(
                        *flip_source.event("h1", n, t))

            def norm1():
                dve.wait_ge(*act_did.after("sq1", 3))
                dve.tensor_reduce(tot, tiles(sum1, 4), AXX, ALU.add).then_inc(*dve_did.event("sum1"))

            def small_rows():
                dve.wait_ge(*pe_did.after("small_rows"))
                dve.tensor_copy(conv_w[:].rearrange("p j i -> p (j i)"), aux[:, 0, 0:CONV * 24])
                dve.tensor_copy(pos["k"][:], aux[:, 1, 0:CMP_L])
                dve.tensor_copy(pos["v"][:], aux[:, 1, CMP_L:2 * CMP_L]).then_inc(*dve_did.event("small_rows"))

            def ba_split():
                dve.wait_ge(*act_did.after("ba_hi"))
                dve.tensor_tensor(ba_parts[:, :, 1], ba_raw[:, :, 0:16], ba_parts[:, :, 0].bitcast(F32),
                                  ALU.subtract).then_inc(*dve_did.event("ba_lo"))
                dve.wait_ge(*block2_rows.after(8))

            def r1_row_():
                dve.wait_ge(*pool_did.after("r1"))
                for t in range(NT):
                    last = dve.tensor_scalar(r1_diag[:, t], ident[:], r1[:, t:t + 1], None, ALU.mult)
                last.then_inc(*dve_did.event("r1_diag"))
                dve.wait_ge(*pe_did.after("r1_row"))
                dve.tensor_copy(r1_row[:], aux[:, 2, 0:SEQ]).then_inc(*dve_did.event("r1_row"))

            def raw_out(part, h):
                dve.wait_ge(*used.after(END[("conv", part, h)]))
                if (part, h) != ("q", 0):
                    dve.wait_ge(*dve_did.after("conv", *before_conv(part, h)))
                    dve.wait_ge(*act_did.after("tap", *before_conv(part, h)))
                else:
                    dve.wait_ge(*dve_did.after("r1_row"))
                    dve.wait_ge(*act_did.after("sq1", 3))
                    dve.wait_ge(*flip_source.after("h1", 3, 1))
                dve.tensor_tensor(raw[:], channels_of(END[("conv", part, h)]), over_heads(r1_row[:]), ALU.mult).then_inc(
                    *dve_did.event("raw_out", part, h))

            def m_out(part, h):
                dve.wait_ge(*used.after(END[("moba", part, h)]))
                dve.tensor_tensor(m_t[part][:, quad(h)], channels_of(END[("moba", part, h)]), over_heads(r1_row[:]),
                                  ALU.mult).then_inc(*dve_did.event("m_out", part, h))

            def conv(part, h, n):
                dve.wait_ge(*act_did.after("tap", part, h))
                first = "qkv".index(part) * HEADS + h * QUAD
                for back in range(1, CONV):
                    for i in range(2 * n, 2 * n + 2):
                        last = dve.scalar_tensor_tensor(
                            cv[:, i, back:SEQ], raw[:, i, 0:SEQ - back],
                            conv_w[:, CONV - 1 - back, first + i:first + i + 1], cv[:, i, back:SEQ], ALU.mult, ALU.add)
                    if back < CONV - 1:
                        link(last)
                if n:
                    last.then_inc(*dve_did.event("conv", part, h))
                else:
                    link(last)

            def token_out(part, h):
                if part == "v":
                    dve.wait_ge(*pe_did.after("conv_back", part, h))
                    for t in range(NT):
                        last = dve.tensor_tensor(v_tok[:, t, quad(h)], aux[:, 2 + t].rearrange("p (i c) -> p i c", c=P),
                                                 over_cols(beta[:, t * HEADS + h * QUAD:t * HEADS + (h + 1) * QUAD]),
                                                 ALU.mult)
                    last.then_inc(*dve_did.event("token_out", part, h))
                    return
                dve.wait_ge(*act_did.after("sq", part, h))
                if (part, h) != ("q", 0):
                    dve.wait_ge(*pool_did.after("rnorm", *before_qk(part, h)))
                dve.tensor_reduce(tiles(ssq, QUAD), sq[:], AXX, ALU.add).then_inc(*dve_did.event("ssq", part, h))
                dve.wait_ge(*pool_did.after("rnorm", part, h))
                if part == "q" and h:
                    dve.wait_ge(*pe_did.after("qk_flip", "q", 0))
                for t in range(NT):
                    to = q_tok[:, t] if part == "q" else k_tok[:, t, quad(h)]
                    last = dve.tensor_tensor(to, aux[:, 2 + t].rearrange("p (i c) -> p i c", c=P),
                                             over_cols(rnorm[:, t * QUAD:(t + 1) * QUAD]), ALU.mult)
                last.then_inc(*dve_did.event("token_out", part, h))

            def gu(h, t):
                o = t * HEADS + h * QUAD
                if (h, t) == (0, 0):
                    dve.wait_ge(*pe_did.after("conv_back", "v", 1))
                    dve.wait_ge(*pe_did.after("qk_flip", "q", 1))
                    dve.wait_ge(*act_did.after("silu", "v", 1))
                dve.tensor_tensor(chain[t]["wide"][:], over_heads(upto[:]), over_cols(g[:, o:o + QUAD]),
                                  ALU.mult).then_inc(*dve_did.event("gu", h, t))

            def tri(h, t):
                c = chain[t]
                dve.wait_ge(*act_did.after("decay", h, t))
                dve.tensor_tensor(c["low_m"][:], c["inv"][:], over_heads(levels[:, 0]), ALU.mult)
                link(dve.tensor_tensor(c["low_t"][:], c["inv"][:], over_heads(upto[:]), ALU.mult))
                dve.tensor_tensor(attn_t[:, quad(h), t], aux[:, 2].rearrange("p (i c) -> p i c", c=P), c["low_t"][:],
                                  ALU.mult)
                for i in range(QUAD):
                    o = t * HEADS + h * QUAD + i
                    last = dve.scalar_tensor_tensor(c["wide"][:, i], aux[:, 1, i * P:(i + 1) * P], nbeta[:, o:o + 1],
                                                    c["low_m"][:, i], ALU.mult, ALU.mult)
                last.then_inc(*dve_did.event("tri", h, t))

            def masked(h, t, n):
                c = chain[t]
                return dve.tensor_tensor(c["low_m"][:], c["low_t"][:], over_heads(levels[:, n + 1]), ALU.mult)

            def unit_columns(h, t, n):
                b = 2 ** (n - 1)
                unit = blocks_of(ident, n, 1).unsqueeze(1).broadcast_to([P, QUAD, P // 2 // b, b])
                dve.tensor_copy(blocks_of(chain[t]["wide"], n, 1), unit)

            def invert_first(h, t):
                c = chain[t]
                inv_q = inv_t[:, quad(h), t]
                dve.wait_ge(*act_did.after("tri_flip", h, t))
                dve.tensor_tensor(c["inv"][:], c["wide"][:], over_heads(levels[:, 1]), ALU.mult)
                link(dve.tensor_tensor(inv_q, c["low_t"][:], over_heads(levels[:, 2]), ALU.mult))
                dve.tensor_tensor(c["inv"][:], c["inv"][:], over_heads(ident[:]), ALU.add)
                dve.tensor_tensor(inv_q, inv_q, over_heads(ident[:]), ALU.add)
                unit_columns(h, t, 2)
                masked(h, t, 2).then_inc(*dve_did.event("masked", h, t, 2))

            def invert_y(h, t, n):
                dve.wait_ge(*pe_did.after("invert_y", h, t, n))
                b = 2 ** (n - 1)
                unit = blocks_of(ident, n, 0).unsqueeze(1).broadcast_to([P, QUAD, P // 2 // b, b])
                dve.tensor_tensor(blocks_of(chain[t]["wide"], n, 0), half_bank(0, n), unit, ALU.add).then_inc(
                    *dve_did.event("invert_y", h, t, n))
                if n < LEVELS:
                    masked(h, t, n + 1).then_inc(*dve_did.event("masked", h, t, n + 1))

            def invert_t(h, t, n):
                dve.wait_ge(*pe_did.after("invert_t", h, t, n))
                dve.tensor_copy(blocks_of(inv_t[:, quad(h), t], n, 1), half_bank(2, n)).then_inc(
                    *dve_did.event("invert_t", h, t, n))
                if n < LEVELS:
                    unit_columns(h, t, n + 1)

            def invert_flip(h, t, n):
                if n <= BLOCK_LEVELS:
                    dve.wait_ge(*dve_did.after("invert_t", h, t, n))
                    dve.wait_ge(*pe_did.after("invert_y", h, t, n))
                    dve.transpose(chain[t]["inv"][:], inv_t[:, quad(h), t]).then_inc(
                        *dve_did.event("invert_flip", h, t, n))

            def delta(h, n):
                q4 = quad(h)
                o = HEADS + h * QUAD
                if n == 0:
                    dve.wait_ge(*act_did.after("eg"))
                    dve.tensor_tensor(k_tok[:, 0, q4], k_tok[:, 0, q4], over_cols(tail[:, q4]), ALU.mult).then_inc(
                        *dve_did.event("delta", h, 0))
                if n == 1:
                    dve.wait_ge(*pe_did.after("delta", h, 1))
                    dve.tensor_copy(k_tok[:, 0, q4], aux[:, 2].rearrange("p (i c) -> p i c", c=P)).then_inc(
                        *dve_did.event("delta", h, 1))
                if n == 2:
                    dve.wait_ge(*pe_did.after("delta", h, 2))
                    o1 = k_tok[:, 1, q4]
                    link(dve.tensor_tensor(delta_r[:], aux[:, 3].rearrange("p (i c) -> p i c", c=P),
                                           over_cols(beg[:, o:o + QUAD]), ALU.mult))
                    dve.tensor_tensor(o1, aux[:, 0].rearrange("p (i c) -> p i c", c=P),
                                      over_cols(eg[:, o:o + QUAD]), ALU.mult)
                    dve.tensor_tensor(delta_r[:], v_tok[:, 1, q4], delta_r[:], ALU.subtract).then_inc(
                        *dve_did.event("delta", h, 2))
                if n == 4:
                    dve.wait_ge(*pe_did.after("delta", h, 4))
                    o1 = k_tok[:, 1, q4]
                    dve.tensor_tensor(o1, aux[:, 2].rearrange("p (i c) -> p i c", c=P), o1, ALU.add).then_inc(*dve_did.event("delta", h, 4))

            def delta_norm(h):
                dve.wait_ge(*act_did.after("delta_sq", h))
                dve.tensor_reduce(tiles(ssq, QUAD), delta_sq[:], AXX, ALU.add).then_inc(*dve_did.event("delta_ssq", h))
                dve.wait_ge(*pool_did.after("delta_rnorm", h))
                for t in range(NT):
                    o = k_tok[:, t, quad(h)]
                    last = dve.tensor_tensor(o, o, over_cols(rnorm[:, t * QUAD:(t + 1) * QUAD]), ALU.mult)
                link(last)
                dve.wait_ge(*act_did.after("z", h))
                for t in range(NT):
                    o = k_tok[:, t, quad(h)]
                    last = dve.tensor_tensor(o, o, zs[:, t, quad(h)], ALU.mult)
                last.then_inc(*flip_source.event("oa", h))

            def z_out(h):
                dve.wait_ge(*act_did.after("z", h))
                for t in range(NT):
                    z = zs[:, t, quad(h)]
                    last = dve.tensor_tensor(z, z, over_heads(gnorm_w[:]), ALU.mult)
                link(last)

            def att(kind, h, t, n):
                k = (t + 1) * P
                s = att_s[:, 0:QUAD * k].rearrange("p (i c) -> p i c", c=k)
                if n == 1:
                    dve.wait_ge(*pe_did.after("att", kind, h, t, 0))
                    if att_before[(kind, h, t)]:
                        dve.wait_ge(*pe_did.after(*att_before[(kind, h, t)][:-1], 3))
                    ps = aux[:, 0:2].rearrange("p b c -> p (b c)")[:, 0:QUAD * k].rearrange("p (i c) -> p i c", c=k)
                    mask = masks[:, 1 if kind == "b" else 0, SEQ - k:SEQ]
                    link(dve.tensor_tensor(s, ps, over_heads(mask), ALU.add))
                    link(dve.tensor_reduce(mx[:, 0:QUAD], s, AXX, ALU.max))
                    if kind == "b":
                        sinks = sink_row[:, quad(h)]
                        link(dve.scalar_tensor_tensor(mx[:, 0:QUAD], mx[:, 0:QUAD], SCALE_B, sinks, ALU.mult, ALU.max))
                        dve.tensor_tensor(esink[:, 0:QUAD], sinks, mx[:, 0:QUAD], ALU.subtract)
                    dve.tensor_scalar(nmx[:, 0:QUAD], mx[:, 0:QUAD], -1.0 if kind == "b" else -SCALE, None,
                                      ALU.mult).then_inc(*dve_did.event("max", kind, h, t))
                if n == 4:
                    dve.wait_ge(*act_did.after("exp", kind, h, t))
                    d, r = den[:, 0:QUAD], rden[:, 0:QUAD]
                    if kind == "b":
                        link(dve.tensor_tensor(d, d, esink[:, 0:QUAD], ALU.add))
                    link(dve.reciprocal(r, d))
                    if kind in "sw":
                        dve.wait_ge(*act_did.after("head_gates"))
                        o = t * 24 + h * QUAD * 3
                        gate = head_gate[:, o:o + QUAD * 3].rearrange("p (i b) -> p i b", b=3)[:, :, 1 if kind == "s" else 2]
                        link(dve.tensor_tensor(r, r, gate, ALU.mult))
                    dve.wait_ge(*pe_did.after("att", kind, h, t, 4))
                    w = 64 if kind == "b" else P
                    o = aux[:, 2, 0:QUAD * w].rearrange("p (i c) -> p i c", c=w)
                    if kind == "m":
                        to = att_o[:].rearrange("p (i c) -> p i c", c=P)
                        if att_before[(kind, h, t)]:
                            dve.wait_ge(*flip_filled.after("ob", *att_before[(kind, h, t)][2:4]))
                        link(dve.tensor_tensor(to, o, over_cols(r), ALU.mult))
                        dve.wait_ge(*act_did.after("mz", h))
                        dve.tensor_tensor(to, to, mzs[:, t, quad(h)], ALU.mult).then_inc(*flip_source.event("ob", h, t))
                        return
                    to = oa_tok if kind in "sw" else ob_tok
                    to = to[:, t, h * QUAD * w:(h + 1) * QUAD * w].rearrange("p (i c) -> p i c", c=w)
                    if kind == "w":
                        for i in range(QUAD):
                            last = dve.scalar_tensor_tensor(to[:, i], o[:, i], r[:, i:i + 1], to[:, i], ALU.mult, ALU.add)
                    else:
                        last = dve.tensor_tensor(to, o, over_cols(r, w), ALU.mult)
                    last.then_inc(*dve_did.event("att", kind, h, t))

            def branch(ab, c):
                a = acc_of(END[("u" + ab, c)])
                dve.wait_ge(*act_did.after("gate_out", ab, c))
                dve.wait_ge(*used.after(END[("u" + ab, c)]))
                to = sg[ab][c % 2]
                last = dve.tensor_tensor(to[:], to[:], a, ALU.mult)
                if ab == "a":
                    last.then_inc(*dve_did.event("branch", ab, c))
                    return
                last.then_inc(*dve_did.event("branch_mult", c))
                dve.wait_ge(*dve_did.after("branch_mult", c))
                if c:
                    dve.wait_ge(*flip_filled.after("merged", c - 1, 1))
                dve.tensor_tensor(merged[:], sg["a"][c % 2][:], to[:], ALU.add).then_inc(*flip_source.event("merged", c))

            def y_out(c):
                a = acc_of(END[("wo", c)])
                dve.wait_ge(*x_again.after(2))
                dve.wait_ge(*used.after(END[("wo", c)]))
                cols = slice(c * COLS, (c + 1) * COLS)
                for t in reversed(range(NT)):
                    if t == 0:
                        dve.wait_ge(*act_did.after("y_out", c, t))
                    dve.tensor_tensor(y1[:, t, cols], a[:, t], post_row[:, cols], ALU.mult).then_inc(
                        *dve_did.event("y_out", c, t))

            def residual(n):
                if n == 0:
                    dve.wait_ge(*act_did.after("y_out", 3, 1))
                    dve.tensor_reduce(tot, tiles(sumy, 4), AXX, ALU.add).then_inc(*dve_did.event("sumy"))
                    dve.wait_ge(*pool_did.after("ry"))
                    dve.wait_ge(*dve_did.after("y_out", 3, 0))
                cols = slice(n * COLS, (n + 1) * COLS)
                for t in range(NT):
                    last = dve.scalar_tensor_tensor(x2[:, t, cols], y1[:, t, cols], ry[:, t:t + 1], x2[:, t, cols],
                                                    ALU.mult, ALU.add)
                last.then_inc(*dve_did.event("x2", n))
                dve.wait_ge(*dve_did.after("x2", n))
                for t in range(NT):
                    dve.tensor_tensor(y1[:, t, cols], x2[:, t, cols], row2[:, cols], ALU.mult).then_inc(
                        *flip_source.event("h2", n, t))

            def norm2():
                dve.wait_ge(*act_did.after("sq2", 3))
                dve.tensor_reduce(tot, tiles(sum2, 4), AXX, ALU.add).then_inc(*dve_did.event("sum2"))

            def ag_split():
                dve.wait_ge(*act_did.after("ag_hi"))
                dve.tensor_tensor(ag_parts[:, :, 1], ba_raw[:], ag_parts[:, :, 0].bitcast(F32), ALU.subtract).then_inc(*dve_did.event("ag_lo"))

            def head_gates():
                dve.wait_ge(*pool_did.after("r2"))
                for t in range(NT):
                    for table in (rope_a, rope_b):
                        last = dve.tensor_scalar(table[:, :, t], table[:, :, t], r2[:, t:t + 1], None, ALU.mult)
                link(last)

            def rope(*name):
                a = acc_of(END[name])
                dve.wait_ge(*used.after(END[name]))
                table, d, heads = {"qa": (rope_a, 128, 4), "qb": (rope_b, 64, 8), "kvb": (rope_b, 64, 2)}.get(
                    name[0], (rope_a, 128, 2))
                w, d2 = heads * d, d // 2
                for t in range(NT):
                    x = a[:, t, 0:w].rearrange("p (i c) -> p i c", c=d)
                    ra, rb = (rot[i][:, t, 0:w].rearrange("p (i c) -> p i c", c=d) for i in range(2))
                    dve.tensor_tensor(ra, x, over_heads(table[:, 0, t], heads), ALU.mult)
                    dve.tensor_tensor(rb[:, :, 0:d2], x[:, :, d2:d], over_heads(table[:, 1, t, 0:d2], heads), ALU.mult)
                    last = dve.tensor_tensor(rb[:, :, d2:d], x[:, :, 0:d2], over_heads(table[:, 1, t, d2:d], heads),
                                             ALU.mult)
                last.then_inc(*dve_did.event("rope_read", *name))
                dve.wait_ge(*dve_did.after("rope_read", *name))
                if rope_before[name]:
                    dve.wait_ge(*pe_did.after("rope_flip", *rope_before[name]))
                for t in range(NT):
                    if name[0] == "kvb":
                        ra, rb = (rot[i][:, t, 0:w].rearrange("p (i c) -> p i c", c=d) for i in range(2))
                        rc = rot[2][:, t, 0:2 * w].rearrange("p (i r c) -> p i r c", r=2, c=d)
                        for r in range(2):
                            last = dve.tensor_tensor(rc[:, :, r], ra, rb, ALU.add)
                    else:
                        last = dve.tensor_tensor(rot[2][:, t, 0:w], rot[0][:, t, 0:w], rot[1][:, t, 0:w], ALU.add)
                last.then_inc(*dve_did.event("rope", *name))

            def blocks(part):
                if part == "k":
                    dve.wait_ge(*spilled.after(0))
                dve.wait_ge(*act_did.after("rope_flip", "kcv"))
                s = kt2["kc" if part == "k" else "vc"][:].rearrange("p i (c l) -> p l i c", l=16)
                for n in range(2):
                    for i in range(2):
                        last = dve.tensor_tensor(blk[part][:, n * 16:(n + 1) * 16, i], s[:, :, i, n:n + N_CMP],
                                                 over_cols(pos[part][:, n * 16:(n + 1) * 16], N_CMP), ALU.add)
                last.then_inc(*dve_did.event("blocks", part))

            def blocks_split(part):
                dve.wait_ge(*act_did.after("blocks_hi", part))
                dve.tensor_tensor(blk_parts[part][:, :, 1], blk[part][:].rearrange("p l i c -> p l (i c)"),
                                  blk_parts[part][:, :, 0].bitcast(F32), ALU.subtract).then_inc(
                    *dve_did.event("blocks_lo", part))

            def catt(t, n):
                if n == 1:
                    dve.wait_ge(*pe_did.after("catt", t, 0))
                    s = aux[:, 0, 0:HEADS * N_CMP].rearrange("p (i c) -> p i c", c=N_CMP)
                    if t:
                        dve.wait_ge(*pe_did.after("catt", 0, 3))
                    link(dve.scalar_tensor_tensor(cs[:], s, SCALE, over_heads(cmask[:, 0, t], HEADS), ALU.mult, ALU.add))
                    link(dve.tensor_reduce(cmx, cs[:], AXX, ALU.max))
                    dve.tensor_tensor(cs[:], cs[:], over_cols(cmx, N_CMP), ALU.subtract).then_inc(
                        *dve_did.event("cmax", t))
                if n == 2:
                    dve.wait_ge(*act_did.after("cexp", t))
                    dve.tensor_tensor(cs[:], cs[:], over_heads(cmask[:, 1, t], HEADS), ALU.mult).then_inc(
                        *dve_did.event("cprob", t))
                    dve.wait_ge(*dve_did.after("cprob", t))
                    link(dve.tensor_reduce(cden, cs[:], AXX, ALU.add))
                    link(dve.tensor_scalar(cden, cden, TINY, None, ALU.max))
                    link(dve.reciprocal(crden, cden))
                    gate = head_gate[:, t * 24:(t + 1) * 24].rearrange("p (i b) -> p i b", b=3)[:, :, 0]
                    link(dve.tensor_tensor(crden, crden, gate, ALU.mult))
                if n == 4:
                    dve.wait_ge(*pe_did.after("catt", t, 4))
                    o = aux[:, 0:2].rearrange("p b (i c) -> p (b i) c", c=P)
                    for i in range(HEADS):
                        to = oa_tok[:, t, i * P:(i + 1) * P]
                        last = dve.scalar_tensor_tensor(to, o[:, i], crden[:, i:i + 1], to, ALU.mult, ALU.add)
                    last.then_inc(*dve_did.event("catt", t))

            def y_gate(n):
                dve.wait_ge(*act_did.after("z2", n))
                dve.wait_ge(*dve_did.after(*(("catt", 1) if n < 2 else ("att", "b", 2 * n - 3, 1))))
                tok = (oa_tok, ob_tok)[n // 2][:, :, n % 2 * COLS:(n % 2 + 1) * COLS]
                dve.tensor_tensor(tok, tok, z2[n % 2][:], ALU.mult).then_inc(*flip_source.event("y", n))

            def y2_out(c):
                a = acc_of(END[("w2", c)])
                dve.wait_ge(*x3_ready.after(0))
                dve.wait_ge(*last_ready.after(0))
                dve.wait_ge(*used.after(END[("w2", c)]))
                cols = slice(c * COLS, (c + 1) * COLS)
                dve.tensor_tensor(x3[:, :, cols], x3[:, :, cols], a, ALU.add).then_inc(*dve_did.event("x3", c))
                dve.wait_ge(*dve_did.after("x3", c))
                dve.tensor_tensor(y3[:, :, cols], x3[:, :, cols], over_heads(last_row[:, cols], NT),
                                  ALU.mult).then_inc(*dve_did.event("y3", c))

            def finish():
                dve.wait_ge(*act_did.after("sq3", 3))
                dve.tensor_reduce(tot, tiles(sum3, 4), AXX, ALU.add).then_inc(*dve_did.event("sum3"))
                dve.wait_ge(*pool_did.after("r3"))
                for m in range(2):
                    y = y3[:, 1, m * D // 2:(m + 1) * D // 2]
                    dve.tensor_scalar(y, y, r3[:, 1:2], None, ALU.mult).then_inc(*dve_did.event("finish", m))

            dve.wait_ge(*pe_did.after("row1"))
            scale_x(0)
            scale_x(1)
            for n in range(2):
                for t in range(NT):
                    flip("h1", n, t)
                split(n)
            steps = {"scale_x": scale_x, "norm1": norm1, "small_rows": small_rows, "ba_split": ba_split,
                     "norm2": norm2, "ag_split": ag_split, "beta_gcum": beta_gcum, "ba": ba_, "gates": gates,
                     "gcum": gcum_, "r1_row": r1_row_, "raw_out": raw_out, "m_out": m_out, "conv": conv,
                     "token_out": token_out, "gu": gu,
                     "tri": tri, "invert_first": invert_first, "invert_y": invert_y, "invert_t": invert_t,
                     "invert_flip": invert_flip, "delta": delta, "delta_norm": delta_norm, "z_out": z_out, "att": att, "flip": flip,
                     "branch": branch, "y_out": y_out, "residual": residual, "head_gates": head_gates, "rope": rope,
                     "blocks": blocks, "blocks_split": blocks_split, "catt": catt, "y_gate": y_gate, "y2_out": y2_out, "finish": finish}
            for tick in range(TICKS + LAST):
                if tick + AHEAD < TICKS:
                    split(tick + AHEAD)
                for name, *args in PLAN[tick]:
                    if name in steps:
                        steps[name](*args)

        @block.tensor
        def _(pe):
            held = {b: () for b in range(AUX)}

            def take(b, *readers):
                for s, *key in held[b]:
                    pe.wait_ge(*s.after(*key))
                held[b] = readers

            def turn(to, source):
                return pe.transpose(to, source, ident[0:source.shape[0], 0:source.shape[0]])

            acc_readers = {}
            for c in range(4):
                acc_readers[("ga", c)] = (act_did, "gate_out", "a", c)
                acc_readers[("gb", c)] = (act_did, "gate_out", "b", c)
                acc_readers[("ua", c)] = (dve_did, "branch", "a", c)
                acc_readers[("ub", c)] = (dve_did, "branch_mult", c)
                acc_readers[("wo", c)] = ((act_did, "y_out", c, 1), (dve_did, "y_out", c, 0))
                acc_readers[("w2", c)] = (dve_did, "x3", c)
            for h in range(2):
                for part in "qkv":
                    acc_readers[("conv", part, h)] = (dve_did, "raw_out", part, h)
                    acc_readers[("moba", part, h)] = (dve_did, "m_out", part, h) if part != "v" else (act_did, "m_v", h)
                acc_readers[("z", h)] = (act_did, "z", h)
                acc_readers[("mz", h)] = (act_did, "mz", h)
                acc_readers[("za", h)] = (act_did, "z2", h)
                acc_readers[("zb", h)] = (act_did, "z2", 2 + h)
                for name in ("qa", "qb"):
                    acc_readers[(name, h)] = (dve_did, "rope", name, h)
            for name in ("kcv", "ksv", "kwv", "kvb"):
                acc_readers[(name,)] = ((dve_did, "rope", name), (act_did, "values", name))
            for part in "kv":
                acc_readers[("cmp", part)] = (act_did, "cmp_rows", part)

            def wait_readers(name):
                r = acc_readers[name]
                for s, *key in (r if isinstance(r[0], tuple) else (r,)):
                    pe.wait_ge(*s.after(*key))

            filled = set()

            def products(no):
                g_, k0, n, first, last = PIECES[no]
                group = GROUPS[g_]
                if first and g_ >= 2:
                    wait_readers(GROUPS[g_ - 2].name)
                elif first:
                    pe.wait_ge(*flip_source.after("h1", 2 * g_ + 1, 1))
                to = acc[:, g_ % 2]
                if group.kind == "cmp":
                    hi, lo = (piece_view(w[no % SPLIT_SLOTS], no) for w in (hi_w, lo_w))
                    parts = blk_parts[group.name[1]]
                    pe.wait_ge(*lo_ready.after(no))
                    pe.wait_ge(*dve_did.after("blocks_lo", group.name[1]))
                    for k in range(k0, k0 + n):
                        at_end = last and k == k0 + n - 1
                        both = ((4 * N_CMP, parts[:, k].rearrange("p b c -> p (b c)"), hi),
                                (2 * N_CMP, parts[:, k, 0], lo))
                        for m, (rows, x, w) in enumerate(both[::-1] if at_end else both):
                            i = pe.matmul(to[0:rows, 0, 0:256], x, w[:, k - k0], start=first and k == k0 and m == 0,
                                          stop=at_end and m == 1)
                    i.then_inc(*used.event(no))
                    return
                slot = no % SPLIT_SLOTS
                hi = piece_view(hi_w[slot], no)
                lo = piece_view(lo_w[slot], no)
                x_hi, x_lo = LHS[group.lhs]
                for k in range(k0, k0 + n):
                    if (group.lhs, k // 4) not in filled:
                        filled.add((group.lhs, k // 4))
                        for t in range(NT):
                            pe.wait_ge(*flip_lo.after(group.lhs, k // 4, t))
                pe.wait_ge(*lo_ready.after(no))
                if group.kind == "channels":
                    for c in range(group.cols // P):
                        for k in range(n):
                            for m, (w, x) in enumerate(((hi, x_hi), (hi, x_lo), (lo, x_hi))):
                                i = pe.matmul(channels_of(no)[:, c], w[:, k, c * P:(c + 1) * P], x[:, k0 + k],
                                              start=first and c % 2 == 0 and k == 0 and m == 0,
                                              stop=last and c % 2 == 1 and k == n - 1 and m == 2)
                    i.then_inc(*used.event(no))
                    return
                for t in range(NT):
                    for k in range(n):
                        at = (slice(None), k0 + k, slice(t * P, (t + 1) * P))
                        for m, (x, w) in enumerate(((x_hi, hi), (x_hi, lo), (x_lo, hi))):
                            i = pe.matmul(to[:, t, 0:group.cols], x[at], w[:, k], start=first and k == 0 and m == 0,
                                          stop=last and k == n - 1 and m == 2)
                i.then_inc(*used.event(no))

            def flip(name, n, t):
                b = flip_bank(name, n, t)
                take(b, (flip_hi, name, n, t), (flip_lo, name, n, t))
                source = {"h1": (n, t), "h2": (n, t), "ob": (n, t)}.get(name, (n,))
                pe.wait_ge(*flip_source.after(name, *source))
                if name in ("h1", "h2"):
                    s = (xw if name == "h1" else y1)[:, t, n * COLS:(n + 1) * COLS]
                elif name == "oa":
                    s = k_tok[:, t, quad(n)].rearrange("p i c -> p (i c)")
                elif name == "ob":
                    s = att_o[:]
                elif name == "merged":
                    s = merged[:, t]
                else:
                    s = (oa_tok, ob_tok)[n // 2][:, t, n % 2 * COLS:(n % 2 + 1) * COLS]
                for i in range(QUAD):
                    last = turn(aux[:, b, i * P:(i + 1) * P], s[:, i * P:(i + 1) * P])
                last.then_inc(*flip_filled.event(name, n, t))

            def few_rows(key):
                n = {"ba": 16, "ag": 24}[key]
                w = {"ba": ba_parts, "ag": ag_parts}[key]
                take(0, (act_did, "few_rows", key))
                pe.wait_ge(*dve_did.after(key + "_lo"))
                for k in range(KT):
                    both = (2 * n, w[:, k].rearrange("p b c -> p (b c)"), h_hi), (n, w[:, k, 0], h_lo)
                    for m, (rows, w_k, x) in enumerate(both if k < KT - 1 else both[::-1]):
                        i = pe.matmul(aux[0:rows, 0, 0:SEQ], w_k, x[:, k], start=k == 0 and m == 0,
                                      stop=k == KT - 1 and m == 1)
                i.then_inc(*pe_did.event("few_rows", key))

            def few_columns(key, reader):
                n = {"ba": 16, "ag": 24}[key]
                take(0, (reader, key if key == "ba" else "head_gates"))
                pe.wait_ge(*act_did.after("few_rows", key))
                for t in range(NT):
                    for b in range(2):
                        i = pe.matmul(aux[:, 0, t * n:(t + 1) * n], few_t[0:2 * n, t * P:(t + 1) * P],
                                      ident[0:2 * n, b * n:(b + 1) * n], start=b == 0, stop=b == 1)
                i.then_inc(*pe_did.event(key))

            def ba_():
                few_columns("ba", dve_did)

            def ag():
                few_columns("ag", act_did)

            def gcum_():
                take(1, (dve_did, "gcum"))
                pe.wait_ge(*dve_did.after("g"))
                pe.wait_ge(*pool_did.after("ones"))
                pe.matmul(aux[:, 1, 0:NT * HEADS], upto[:], g, start=True, stop=True)
                pe.matmul(aux[:, 1, NT * HEADS:NT * HEADS + HEADS], ones[:], g[:, 0:HEADS], start=True,
                          stop=True).then_inc(*pe_did.event("gcum"))

            def conv_back(part, h):
                for b in (2, 3):
                    take(b, (dve_did, "token_out", part, h))
                pe.wait_ge(*act_did.after("silu", part, h))
                for t in range(NT):
                    for i in range(QUAD):
                        last = turn(aux[:, 2 + t, i * P:(i + 1) * P], sil[:, i, t * P:(t + 1) * P])
                last.then_inc(*pe_did.event("conv_back", part, h))

            def qk_flip(part, h):
                for b in (2, 3):
                    take(b, (act_did, "qk_out", part, h))
                pe.wait_ge(*dve_did.after("token_out", part, h))
                for i in range(QUAD):
                    for t in range(NT):
                        s = q_tok[:, t, i] if part == "q" else k_tok[:, t, h * QUAD + i]
                        o = i % 2 * SEQ + t * P
                        last = turn(aux[:, 2 + i // 2, o:o + P], s)
                last.then_inc(*pe_did.event("qk_flip", part, h))

            def gram(h, t):
                take(0, (act_did, "decay", h, t))
                take(1, (dve_did, "tri", h, t))
                take(2, (dve_did, "tri", h, t))
                pe.wait_ge(*dve_did.after("gu", h, t))
                pe.wait_ge(*act_did.after("qk_out", "k", h))
                pe.matmul(aux[:, 0], ones[:], chain[t]["wide"][:].rearrange("p i c -> p (i c)"), start=True, stop=True)
                for b, x in ((1, k_t), (2, q_t)):
                    for i in range(QUAD):
                        at = (slice(None), h * QUAD + i, slice(t * P, (t + 1) * P))
                        last = pe.matmul(aux[:, b, i * P:(i + 1) * P], k_t[at], x[at], start=True, stop=True)
                last.then_inc(*pe_did.event("gram", h, t))

            def tri_flip(h, t):
                take(3, (act_did, "tri_flip", h, t))
                pe.wait_ge(*dve_did.after("tri", h, t))
                for i in range(QUAD):
                    last = turn(aux[:, 3, i * P:(i + 1) * P], chain[t]["wide"][:, i])
                last.then_inc(*pe_did.event("tri_flip", h, t))

            def invert_y(h, t, n):
                take(0, (dve_did, "invert_y", h, t, n))
                pe.wait_ge(*dve_did.after("masked", h, t, n))
                if n > 2:
                    pe.wait_ge(*(dve_did if n - 1 <= BLOCK_LEVELS else act_did).after("invert_flip", h, t, n - 1))
                for i in range(QUAD):
                    last = pe.matmul(half_bank(0, n)[:, i], chain[t]["low_m"][:, i],
                                     blocks_of(chain[t]["inv"][:, i], n, 0), start=True, stop=True)
                last.then_inc(*pe_did.event("invert_y", h, t, n))

            def invert_t(h, t, n):
                take(2, (dve_did, "invert_t", h, t, n))
                pe.wait_ge(*dve_did.after("invert_y", h, t, n))
                if n > 2:
                    pe.wait_ge(*dve_did.after("invert_t", h, t, n - 1))
                for i in range(QUAD):
                    last = pe.matmul(half_bank(2, n)[:, i], chain[t]["wide"][:, i],
                                     blocks_of(inv_t[:, h * QUAD + i, t], n, 1), start=True, stop=True)
                last.then_inc(*pe_did.event("invert_t", h, t, n))

            def invert_flip(h, t, n):
                if n <= BLOCK_LEVELS:
                    return
                take(1, (act_did, "invert_flip", h, t, n))
                pe.wait_ge(*dve_did.after("invert_t", h, t, n))
                for i in range(QUAD):
                    last = pe.matmul(half_bank(1, n)[:, i], inv_t[:, h * QUAD + i, t], blocks_of(ident, n, 0),
                                     start=True, stop=True)
                last.then_inc(*pe_did.event("invert_flip", h, t, n))

            def delta(h, n):
                readers = {0: [(0, act_did, 0)], 1: [(1, act_did, 1), (2, dve_did, 1)],
                           2: [(3, dve_did, 2), (0, dve_did, 2)], 3: [(1, act_did, 3)], 4: [(2, dve_did, 4)]}
                for b, s, m in readers[n]:
                    take(b, (s, "delta", h, m))
                if n == 0:
                    for t in range(NT):
                        pe.wait_ge(*dve_did.after("invert_t", h, t, LEVELS))
                if n == 1:
                    pe.wait_ge(*dve_did.after("delta", h, 0))
                if n in (1, 2, 4):
                    pe.wait_ge(*act_did.after("delta", h, n - 1))
                if n == 3:
                    pe.wait_ge(*dve_did.after("delta", h, 2))
                for i in range(QUAD):
                    hd, o = h * QUAD + i, slice(i * P, (i + 1) * P)
                    if n == 0:
                        last = pe.matmul(aux[:, 0, o], inv_t[:, hd, 0], v_tok[:, 0, hd], start=True, stop=True)
                    if n == 1:
                        pe.matmul(aux[:, 1, o], k_tok[:, 0, hd], delta_u[:, i], start=True, stop=True)
                        last = pe.matmul(aux[:, 2, o], attn_t[:, hd, 0], delta_u[:, i], start=True, stop=True)
                    if n == 2:
                        pe.matmul(aux[:, 3, o], k_t[:, hd, P:SEQ], delta_s[:, i], start=True, stop=True)
                        last = pe.matmul(aux[:, 0, o], q_t[:, hd, P:SEQ], delta_s[:, i], start=True, stop=True)
                    if n == 3:
                        last = pe.matmul(aux[:, 1, o], inv_t[:, hd, 1], delta_r[:, i], start=True, stop=True)
                    if n == 4:
                        last = pe.matmul(aux[:, 2, o], attn_t[:, hd, 1], delta_u[:, i], start=True, stop=True)
                last.then_inc(*pe_did.event("delta", h, n))

            def att(kind, h, t, n):
                k = (t + 1) * P
                tok = slice(t * P, (t + 1) * P)
                if n == 0:
                    for b in range(2):
                        take(b, (dve_did, "max", kind, h, t))
                    s = aux[:, 0:2].rearrange("p b c -> p (b c)")
                    if kind == "m":
                        pe.wait_ge(*dve_did.after("m_out", "k", h))
                    elif kind == "b":
                        pe.wait_ge(*act_did.after("rope_flip", "kvb"))
                        pe.wait_ge(*act_did.after("rope_flip", "qb", h // 2))
                    else:
                        pe.wait_ge(*act_did.after("rope_flip", "qa", h))
                        pe.wait_ge(*act_did.after("rope_flip", "k" + kind + "v"))
                    if kind == "b":
                        for i in range(2):
                            last = pe.matmul(s[:, 2 * i * k:2 * (i + 1) * k].rearrange("p (i c) -> p i c", c=k),
                                             qb_t[h // 2][:, h % 2 * 2 + i, tok], kz[:, h // 2, :, 0:k], start=True, stop=True)
                    else:
                        for i in range(QUAD):
                            hd = h * QUAD + i
                            q = (m_t["q"] if kind == "m" else qa_t)[:, hd, tok]
                            keys = m_t["k"][:, hd, 0:k] if kind == "m" else kt2["k" + kind][:, h, 0:k]
                            last = pe.matmul(s[:, i * k:(i + 1) * k], q, keys, start=True, stop=True)
                elif n == 3:
                    for b in range(t + 1):
                        take(2 + b, (act_did, "att_p", kind, h, t))
                    pe.wait_ge(*act_did.after("exp", kind, h, t))
                    for b in range(t + 1):
                        for i in range(QUAD):
                            o = i * k + b * P
                            last = turn(aux[:, 2 + b, i * P:(i + 1) * P], att_s[:, o:o + P])
                elif n == 4:
                    take(2, (flip_source, "ob", h, t) if kind == "m" else (dve_did, "att", kind, h, t))
                    if kind == "m":
                        pe.wait_ge(*act_did.after("m_v", h))
                    else:
                        pe.wait_ge(*act_did.after("values", {"s": "ksv", "w": "kwv", "b": "kvb"}[kind]))
                    w = 64 if kind == "b" else P
                    for i in range(QUAD):
                        for b in range(t + 1):
                            if kind == "m":
                                v = m_v[:, b, h * QUAD + i]
                            elif kind == "b":
                                v = vb[:, b, h // 2]
                            else:
                                v = v2["v" + kind][:, b, h]
                            last = pe.matmul(aux[:, 2, i * w:(i + 1) * w], att_p[:, b, i * P:(i + 1) * P], v,
                                             start=b == 0, stop=b == t)
                else:
                    return
                last.then_inc(*pe_did.event("att", kind, h, t, n))

            def rope_flip(*name):
                for b in (2, 3):
                    take(b, (act_did, "rope_flip", *name))
                pe.wait_ge(*dve_did.after("rope", *name))
                if name[0] == "kcv":
                    pe.wait_ge(*act_did.after("values", "kcv"))
                for i in range(2 if name[0] in ("ksv", "kwv", "kvb") else QUAD):
                    for t in range(NT):
                        o = i % 2 * SEQ + t * P
                        last = turn(aux[:, 2 + i // 2, o:o + P], rot[2][:, t, i * P:(i + 1) * P])
                last.then_inc(*pe_did.event("rope_flip", *name))

            def cmp_fold(part):
                take(0, (act_did, "hs", part))
                pe.wait_ge(*act_did.after("cmp_rows", part))
                for m in range(2):
                    for b in range(2):
                        last = pe.matmul(aux[:, 0, m * 2 * N_CMP:(m + 1) * 2 * N_CMP], cmp_rows[:, m * P:(m + 1) * P],
                                         ident[0:4 * N_CMP, b * 2 * N_CMP:(b + 1) * 2 * N_CMP], start=b == 0,
                                         stop=b == 1)
                last.then_inc(*pe_did.event("cmp_fold", part))

            def cmp_out(part):
                take(0, (act_did, "cmp_out", part))
                pe.wait_ge(*act_did.after("hs", part))
                for i in range(1 if part == "k" else 2):
                    for m in range(2):
                        if part == "k":
                            last = pe.matmul(aux[:, 0, 0:2 * N_CMP], w2s["k"][:, m], hs["k"][:, m], start=m == 0,
                                             stop=m == 1)
                        else:
                            last = pe.matmul(aux[0:N_CMP, 0, i * P:(i + 1) * P],
                                             hs["v"][:, m, i * N_CMP:(i + 1) * N_CMP], w2s["v"][:, m], start=m == 0,
                                             stop=m == 1)
                last.then_inc(*pe_did.event("cmp_out", part))

            def catt(t, n):
                if n == 0:
                    take(0, (dve_did, "cmax", t))
                    pe.wait_ge(*act_did.after("cmp_out", "v"))
                    for i in range(HEADS):
                        last = pe.matmul(aux[:, 0, i * N_CMP:(i + 1) * N_CMP], qa_t[:, i, t * P:(t + 1) * P],
                                         ck_t[:, i // QUAD * N_CMP:(i // QUAD + 1) * N_CMP], start=True, stop=True)
                elif n == 3:
                    for b in (2, 3):
                        take(b, (act_did, "cp", t))
                    pe.wait_ge(*dve_did.after("cprob", t))
                    for i in range(HEADS):
                        last = turn(aux[0:N_CMP, 2 + i // QUAD, i % QUAD * P:(i % QUAD + 1) * P], cs[:, i])
                elif n == 4:
                    for b in (0, 1):
                        take(b, (dve_did, "catt", t))
                    pe.wait_ge(*act_did.after("cp", t))
                    for i in range(HEADS):
                        last = pe.matmul(aux[:, i // QUAD, i % QUAD * P:(i % QUAD + 1) * P],
                                         cp_t[:, i * P:(i + 1) * P], cv_tok[:, i // QUAD], start=True, stop=True)
                else:
                    return
                last.then_inc(*pe_did.event("catt", t, n))

            def r1_row_():
                take(2, (dve_did, "r1_row"))
                pe.wait_ge(*dve_did.after("r1_diag"))
                pe.wait_ge(*pool_did.after("ones"))
                pe.matmul(aux[:, 2, 0:SEQ], ones[:], r1_diag[:].rearrange("p t c -> p (t c)"), start=True,
                          stop=True).then_inc(*pe_did.event("r1_row"))

            def small_rows():
                for b in (0, 1):
                    take(b, (dve_did, "small_rows"))
                pe.wait_ge(*const_ready.after(6))
                turn(aux[:, 0, 0:96], rows_in[0:96, 0])
                turn(aux[:, 1, 0:64], rows_in[0:64, 1]).then_inc(*pe_did.event("small_rows"))

            pe.wait_ge(*row_ready.after(1))
            pe.wait_ge(*pool_did.after("ones"))
            for n in range(4):
                last = pe.matmul(acc[:, n // 2, n % 2], ones[0:1, :], row1[:, n * COLS:(n + 1) * COLS], start=True,
                                 stop=True)
            last.then_inc(*pe_did.event("row1"))
            for n in range(2):
                for t in range(NT):
                    flip("h1", n, t)
            steps = {"small_rows": small_rows, "few_rows": few_rows, "ba": ba_, "gcum": gcum_, "r1_row": r1_row_,
                     "conv_back": conv_back, "qk_flip": qk_flip, "invert_flip": invert_flip,
                     "gram": gram, "tri_flip": tri_flip, "invert_y": invert_y, "invert_t": invert_t, "delta": delta,
                     "att": att, "flip": flip, "ag": ag, "rope_flip": rope_flip,
                     "cmp_fold": cmp_fold, "cmp_out": cmp_out, "catt": catt}
            for tick in range(TICKS + LAST):
                if tick < TICKS:
                    products(tick)
                for name, *args in PLAN[tick]:
                    if name in steps:
                        steps[name](*args)

        return {"signals": {n: s.seen for n, s in signals.items()}}


INPUTS = ["x", "pre_norm_w", "w_in", "conv_w", "a_log", "dt_bias", "gdn_norm_w", "w_branch_a", "w_branch_b", "w_out",
          "post_norm_w", "w_in_2", "cmp_k_w1_2", "cmp_k_w2_2", "cmp_v_w1_2", "cmp_v_w2_2", "cmp_k_pos_2",
          "cmp_v_pos_2", "sinks_2", "w_out_2", "norm_g_2", "final_g_2"]


def kernel(**inputs):
    import concourse.bacc as _bacc
    from concourse.bass_utils import run_bass_kernel_spmd as _run

    arrays = {n: np.ascontiguousarray(inputs[n]) for n in INPUTS}
    arrays.update(constants())
    known = None
    for _ in range(2):
        nc = _bacc.Bacc("TRN2", target_bir_lowering=False, num_devices=1)
        ins = {n: nc.dram_tensor(f"in_{n}", a.shape, mybir.dt.from_np(a.dtype), kind="ExternalInput").ap()
               for n, a in arrays.items()}
        out = nc.dram_tensor("out_y", (1, SEQ, D), F32, kind="ExternalOutput").ap()
        known = build(nc, known, ins, out)
    r = _run(nc, [{f"in_{n}": a for n, a in arrays.items()}], core_ids=[0])
    return r.results[0]["out_y"]
```
